# Optimizing a Trainium2 kernel written in Bass

```python
import jax, jax.numpy as jnp
from jax import lax
import numpy as np
import jax
import jax.numpy as jnp

D_MODEL = 1024
BATCH = 1
SEQ = 256
DEPTH = 2

CHUNK = 64
Q_BLOCK = 128
HEAD_DIM = 64
D_MIX = D_MODEL
A_HEADS = 6
A_LEFT_CHUNKS = 8
A_REL_MAX = 128
A_NUM_REL = CHUNK + A_REL_MAX
B_HEADS = 5
IDX_HEADS = 8
IDX_DIM = 32
TOPK_MAX = 256
C_HEADS = 5
C_Q_RANK = 384
C_KV_RANK = 256
C_NOPE = 64
C_ROPE = 32
C_V = 64
D_FF = 2816
ROPE_THETA = 10000.0
EPS = 1e-6
NEG = -1e30

A_W = A_HEADS * HEAD_DIM
B_W = B_HEADS * HEAD_DIM
C_W = C_HEADS * C_V
IN_SIZES = (A_W, A_W, A_W, B_W, B_W, B_W, IDX_HEADS * IDX_DIM, IDX_DIM, IDX_HEADS,
            C_Q_RANK, C_KV_RANK, C_ROPE)
D_IN = 3 * A_W + 3 * B_W + IDX_HEADS * IDX_DIM + IDX_DIM + IDX_HEADS + C_Q_RANK + C_KV_RANK + C_ROPE


def rmsnorm(x, g):
    x32 = x.astype(jnp.float32)
    y = x32 * lax.rsqrt(jnp.mean(x32 * x32, axis=-1, keepdims=True) + EPS)
    return (y * g.astype(jnp.float32)).astype(x.dtype)

def rope(x, pos):
    d = x.shape[-1]
    inv = ROPE_THETA ** (-jnp.arange(0, d, 2, dtype=jnp.float32) / d)
    ang = pos.astype(jnp.float32)[:, None] * inv[None, :]
    cos = jnp.cos(ang)[:, None, :]
    sin = jnp.sin(ang)[:, None, :]
    x32 = x.astype(jnp.float32)
    x1, x2 = x32[..., : d // 2], x32[..., d // 2:]
    return jnp.concatenate([x1 * cos - x2 * sin, x1 * sin + x2 * cos], axis=-1).astype(x.dtype)

def swiglu(x, w_gate, w_up, w_down):
    return (jax.nn.silu(x @ w_gate) * (x @ w_up)) @ w_down

def sweep_query_blocks(fn, bsz, seq):
    out = lax.map(fn, jnp.arange(seq // Q_BLOCK) * Q_BLOCK)
    return jnp.moveaxis(out, 0, 1).reshape(bsz, seq, -1)

def chunk_relpos_attention(q, k, v, rel_bias):
    bsz, seq, h, d = q.shape
    nc = seq // CHUNK
    nb = A_LEFT_CHUNKS + 1
    pad = A_LEFT_CHUNKS * CHUNK
    qc = q.reshape(bsz, nc, CHUNK, h, d)
    kp = jnp.pad(k, ((0, 0), (pad, 0), (0, 0), (0, 0))).reshape(bsz, nc + A_LEFT_CHUNKS, CHUNK, h, d)
    vp = jnp.pad(v, ((0, 0), (pad, 0), (0, 0), (0, 0))).reshape(bsz, nc + A_LEFT_CHUNKS, CHUNK, h, d)
    kb = jnp.stack([kp[:, j:j + nc] for j in range(nb)], axis=2).reshape(bsz, nc, nb * CHUNK, h, d)
    vb = jnp.stack([vp[:, j:j + nc] for j in range(nb)], axis=2).reshape(bsz, nc, nb * CHUNK, h, d)
    s = jnp.einsum('bcqhd,bckhd->bhcqk', qc, kb).astype(jnp.float32) * (d ** -0.5)
    qi = jnp.arange(CHUNK)[:, None]
    ki = jnp.arange(nb * CHUNK)[None, :]
    rel = pad + qi - ki
    ridx = jnp.clip(rel, -(CHUNK - 1), A_REL_MAX) + (CHUNK - 1)
    bias = rel_bias.astype(jnp.float32)[:, ridx]
    valid = (jnp.arange(nc)[:, None] + ki // CHUNK - A_LEFT_CHUNKS) >= 0
    s = jnp.where(valid[None, None, :, None, :], s + bias[None, :, None], NEG)
    p = jax.nn.softmax(s, axis=-1).astype(v.dtype)
    o = jnp.einsum('bhcqk,bckhd->bcqhd', p, vb)
    return o.reshape(bsz, seq, h * d)

def dsa_attention(q, k, v, q_idx, k_idx, w_idx):
    bsz, seq, h, d = q.shape
    topk = min(TOPK_MAX, seq // 4)
    kchunk = jnp.arange(seq) // CHUNK
    gather = jax.vmap(lambda kk, ii: kk[ii])

    def block(q0):
        tc = (q0 + jnp.arange(Q_BLOCK)) // CHUNK
        qi = lax.dynamic_slice_in_dim(q_idx, q0, Q_BLOCK, axis=1)
        wi = lax.dynamic_slice_in_dim(w_idx, q0, Q_BLOCK, axis=1).astype(jnp.float32) * (IDX_HEADS ** -0.5)
        qb = lax.dynamic_slice_in_dim(q, q0, Q_BLOCK, axis=1)
        dots = jnp.einsum('bqhd,bsd->bqhs', qi, k_idx).astype(jnp.float32) * (IDX_DIM ** -0.5)
        score = jnp.einsum('bqh,bqhs->bqs', wi, jax.nn.relu(dots))
        adm = kchunk[None, :] <= tc[:, None]
        score = jnp.where(adm[None], score, NEG)
        _, idx = lax.top_k(score, topk)
        ksel = gather(k, idx)
        vsel = gather(v, idx)
        valid = (idx // CHUNK) <= tc[None, :, None]
        s = jnp.einsum('bqhd,bqkhd->bhqk', qb, ksel).astype(jnp.float32) * (d ** -0.5)
        s = jnp.where(valid[:, None], s, NEG)
        p = jax.nn.softmax(s, axis=-1).astype(v.dtype)
        return jnp.einsum('bhqk,bqkhd->bqhd', p, vsel)

    return sweep_query_blocks(block, bsz, seq)

def mla_attention(c_q, c_kv, k_rope, q_norm, kv_norm, w_uq, w_ukv, pos):
    bsz, seq, _ = c_q.shape
    q = (rmsnorm(c_q, q_norm) @ w_uq).reshape(bsz, seq, C_HEADS, C_NOPE + C_ROPE)
    qn, qr = q[..., :C_NOPE], rope(q[..., C_NOPE:], pos)
    kv = (rmsnorm(c_kv, kv_norm) @ w_ukv).reshape(bsz, seq, C_HEADS, C_NOPE + C_V)
    kn, v = kv[..., :C_NOPE], kv[..., C_NOPE:]
    kr = rope(k_rope[:, :, None, :], pos)[:, :, 0, :]
    kchunk = pos // CHUNK
    scale = (C_NOPE + C_ROPE) ** -0.5

    def block(q0):
        tc = (q0 + jnp.arange(Q_BLOCK)) // CHUNK
        qnb = lax.dynamic_slice_in_dim(qn, q0, Q_BLOCK, axis=1)
        qrb = lax.dynamic_slice_in_dim(qr, q0, Q_BLOCK, axis=1)
        s = (jnp.einsum('bqhd,bshd->bhqs', qnb, kn) + jnp.einsum('bqhr,bsr->bhqs', qrb, kr)).astype(jnp.float32) * scale
        s = jnp.where((kchunk[None, :] <= tc[:, None])[None, None], s, NEG)
        p = jax.nn.softmax(s, axis=-1).astype(v.dtype)
        return jnp.einsum('bhqs,bshd->bqhd', p, v)

    return sweep_query_blocks(block, bsz, seq)

def split_columns(h):
    parts, off = [], 0
    for size in IN_SIZES:
        parts.append(h[..., off:off + size])
        off += size
    return parts

def hybrid_layer(x, pos, ffn1_norm, ffn1_w_gate, ffn1_w_up, ffn1_w_down, mix_norm, w_in, a_rel_bias,
                 c_q_norm, c_kv_norm, c_w_uq, c_w_ukv, w_out, ffn2_norm, ffn2_w_gate, ffn2_w_up, ffn2_w_down):
    bsz, seq, _ = x.shape
    x = x + 0.5 * swiglu(rmsnorm(x, ffn1_norm), ffn1_w_gate, ffn1_w_up, ffn1_w_down)
    h = rmsnorm(x, mix_norm) @ w_in
    (a_q, a_k, a_v, b_q, b_k, b_v, i_q, i_k, i_w, c_q, c_kv, c_kr) = split_columns(h)
    hd4 = lambda t, nh: t.reshape(bsz, seq, nh, -1)
    o_a = chunk_relpos_attention(hd4(a_q, A_HEADS), hd4(a_k, A_HEADS), hd4(a_v, A_HEADS), a_rel_bias)
    o_b = dsa_attention(rope(hd4(b_q, B_HEADS), pos), rope(hd4(b_k, B_HEADS), pos), hd4(b_v, B_HEADS),
                        rope(hd4(i_q, IDX_HEADS), pos), rope(i_k[:, :, None, :], pos)[:, :, 0, :], i_w)
    o_c = mla_attention(c_q, c_kv, c_kr, c_q_norm, c_kv_norm, c_w_uq, c_w_ukv, pos)
    x = x + jnp.concatenate([o_a, o_b, o_c], axis=-1) @ w_out
    x = x + 0.5 * swiglu(rmsnorm(x, ffn2_norm), ffn2_w_gate, ffn2_w_up, ffn2_w_down)
    return x

def first_inputs(seed: int = 0) -> dict:
    key = jax.random.key(seed)
    ks = jax.random.split(key, 20)
    f32 = jnp.float32

    def nrm(k, shape, scale):
        return jax.random.normal(k, shape, f32) * scale

    def gain(k, n):
        return 1.0 + 0.02 * jax.random.normal(k, (DEPTH, n), f32)

    return {
        "x": jax.random.normal(ks[0], (BATCH, SEQ, D_MODEL), f32),
        "ffn1_norm": gain(ks[1], D_MODEL),
        "ffn1_w_gate": nrm(ks[2], (DEPTH, D_MODEL, D_FF), D_MODEL ** -0.5),
        "ffn1_w_up": nrm(ks[3], (DEPTH, D_MODEL, D_FF), D_MODEL ** -0.5),
        "ffn1_w_down": nrm(ks[4], (DEPTH, D_FF, D_MODEL), D_FF ** -0.5),
        "mix_norm": gain(ks[5], D_MODEL),
        "w_in": nrm(ks[6], (DEPTH, D_MODEL, D_IN), D_MODEL ** -0.5),
        "a_rel_bias": nrm(ks[7], (DEPTH, A_HEADS, A_NUM_REL), 0.1),
        "c_q_norm": gain(ks[8], C_Q_RANK),
        "c_kv_norm": gain(ks[9], C_KV_RANK),
        "c_w_uq": nrm(ks[10], (DEPTH, C_Q_RANK, C_HEADS * (C_NOPE + C_ROPE)), C_Q_RANK ** -0.5),
        "c_w_ukv": nrm(ks[11], (DEPTH, C_KV_RANK, C_HEADS * (C_NOPE + C_V)), C_KV_RANK ** -0.5),
        "w_out": nrm(ks[12], (DEPTH, D_MIX, D_MODEL), D_MIX ** -0.5),
        "ffn2_norm": gain(ks[13], D_MODEL),
        "ffn2_w_gate": nrm(ks[14], (DEPTH, D_MODEL, D_FF), D_MODEL ** -0.5),
        "ffn2_w_up": nrm(ks[15], (DEPTH, D_MODEL, D_FF), D_MODEL ** -0.5),
        "ffn2_w_down": nrm(ks[16], (DEPTH, D_FF, D_MODEL), D_FF ** -0.5),
        "final_norm": 1.0 + 0.02 * jax.random.normal(ks[17], (D_MODEL,), f32),
    }

def first_block(x, ffn1_norm, ffn1_w_gate, ffn1_w_up, ffn1_w_down, mix_norm, w_in, a_rel_bias,
              c_q_norm, c_kv_norm, c_w_uq, c_w_ukv, w_out, ffn2_norm, ffn2_w_gate, ffn2_w_up,
              ffn2_w_down, final_norm):
    pos = jnp.arange(x.shape[1], dtype=jnp.int32)
    for l in range(DEPTH):
        x = hybrid_layer(x, pos, ffn1_norm[l], ffn1_w_gate[l], ffn1_w_up[l], ffn1_w_down[l], mix_norm[l],
                         w_in[l], a_rel_bias[l], c_q_norm[l], c_kv_norm[l], c_w_uq[l], c_w_ukv[l], w_out[l],
                         ffn2_norm[l], ffn2_w_gate[l], ffn2_w_up[l], ffn2_w_down[l])
    return rmsnorm(x, final_norm)


DEPTH_2 = 1

CTX_LEN = 256
GRID_W = 64

ML_WIDTH = D_MODEL // 2
ML_HEADS = 4
ML_HEAD_DIM = ML_WIDTH // ML_HEADS
ML_CHUNK = 128
GLA_WIDTH = D_MODEL - ML_WIDTH
GLA_HEADS = 4
GLA_DV = GLA_WIDTH // GLA_HEADS
GLA_KEY_WIDTH = GLA_WIDTH // 2
GLA_DK = GLA_KEY_WIDTH // GLA_HEADS
GLA_RANK = 16
GLA_TAU = 16.0
GLA_CHUNK = 64
CONV_W = 3
MIX_WIDTH = ML_WIDTH + GLA_WIDTH
PROJ_WIDTHS = (ML_WIDTH, ML_WIDTH, ML_WIDTH, ML_WIDTH, 4 * ML_HEADS,
               GLA_KEY_WIDTH, GLA_KEY_WIDTH, GLA_WIDTH, GLA_WIDTH, 2 * GLA_RANK)
P_TOTAL = sum(PROJ_WIDTHS)

PEER_HEADS = 8
PEER_NKEYS = 128
PEER_EXPERTS = PEER_NKEYS * PEER_NKEYS
PEER_TOPK = 16
PEER_QDIM = 256
PEER_BLOCK = 128


def rms_norm(x, g):
    xf = x.astype(jnp.float32)
    y = xf * lax.rsqrt(jnp.mean(xf * xf, axis=-1, keepdims=True) + EPS)
    return y.astype(x.dtype) * g

def head_rms(h, g):
    y = h * lax.rsqrt(jnp.mean(h * h, axis=-1, keepdims=True) + EPS)
    return y.reshape(h.shape[:2] + (-1,)) * g

def short_conv(u, w, on_grid):
    bz, n, ch = u.shape
    if on_grid:
        rows = n // GRID_W
        u = u.reshape(bz * rows, GRID_W, ch)
    y = lax.conv_general_dilated(u, w[:, None, :].astype(u.dtype), (1,),
                                 [(CONV_W // 2, CONV_W // 2)],
                                 dimension_numbers=('NWC', 'WIO', 'NWC'),
                                 feature_group_count=ch)
    return y.reshape(bz, n, ch)

def to_chunks(t, size):
    bz, n, hh = t.shape[:3]
    t = t.reshape((bz, n // size, size, hh) + t.shape[3:])
    return jnp.moveaxis(t, 3, 1)

def from_chunks(t):
    bz, hh, nc, ll, d = t.shape
    return jnp.moveaxis(t, 1, 3).reshape(bz, nc * ll, hh, d)

def orient(t, direction):
    return jnp.flip(t, axis=1) if direction == 1 else t

def prep_mixers(z, conv_w, gate_b, lr_w2, alpha_b, on_grid):
    bz, n, _ = z.shape
    f32 = jnp.float32
    mq, mk, mv, mo, mg, gq, gk, gv, gr, glr = jnp.split(
        z, np.cumsum(PROJ_WIDTHS)[:-1].tolist(), axis=-1)
    mq, mk = jnp.split(jax.nn.silu(short_conv(jnp.concatenate([mq, mk], axis=-1), conv_w, on_grid)),
                       2, axis=-1)
    gates = (mg + gate_b).astype(f32).reshape(bz, n, 2, 2, ML_HEADS)
    alpha = jnp.einsum('bndr,drk->bndk', glr.reshape(bz, n, 2, GLA_RANK), lr_w2) + alpha_b
    return {
        'ml_q': mq.astype(f32).reshape(bz, n, ML_HEADS, ML_HEAD_DIM),
        'ml_k': (mk.astype(f32) * ML_HEAD_DIM ** -0.5).reshape(bz, n, ML_HEADS, ML_HEAD_DIM),
        'ml_v': mv.astype(f32).reshape(bz, n, ML_HEADS, ML_HEAD_DIM),
        'ml_o': mo,
        'ml_ig': gates[:, :, :, 0],
        'ml_lf': jax.nn.log_sigmoid(gates[:, :, :, 1]),
        'gla_q': (gq.astype(f32) * GLA_DK ** -0.5).reshape(bz, n, GLA_HEADS, GLA_DK),
        'gla_k': gk.astype(f32).reshape(bz, n, GLA_HEADS, GLA_DK),
        'gla_v': gv.astype(f32).reshape(bz, n, GLA_HEADS, GLA_DV),
        'gla_r': gr,
        'gla_la': (jax.nn.log_sigmoid(alpha.astype(f32)) / GLA_TAU).reshape(
            bz, n, 2, GLA_HEADS, GLA_DK),
    }

def mlstm_states(k, v, logf, ig, init):
    b = jnp.cumsum(logf, axis=-1)
    b_end = b[..., -1]
    w_log = b_end[..., None] - b + ig
    m_loc = jnp.max(w_log, axis=-1)
    w = jnp.exp(w_log - m_loc[..., None])
    c_loc = jnp.einsum('bhcld,bhcle->bhcde', w[..., None] * v, k)
    n_loc = jnp.einsum('bhcl,bhcle->bhce', w, k)

    def step(carry, inp):
        cm, nv, m = carry
        be, ml, cl, nl = inp
        m_new = jnp.maximum(be + m, ml)
        a = jnp.exp(be + m - m_new)
        bb = jnp.exp(ml - m_new)
        c_new = a[..., None, None] * cm + bb[..., None, None] * cl
        n_new = a[..., None] * nv + bb[..., None] * nl
        return (c_new, n_new, m_new), (cm, nv, m)

    xs = tuple(jnp.moveaxis(t, 2, 0) for t in (b_end, m_loc, c_loc, n_loc))
    final, starts = lax.scan(step, init, xs)
    starts = tuple(jnp.moveaxis(t, 0, 2) for t in starts)
    return starts, final

def mlstm_outputs(q, k, v, logf, ig, starts):
    c_s, n_s, m_s = starts
    ll = q.shape[-2]
    tri = jnp.tril(jnp.ones((ll, ll), dtype=bool))
    b = jnp.cumsum(logf, axis=-1)
    d_log = jnp.where(tri, b[..., :, None] - b[..., None, :] + ig[..., None, :], -jnp.inf)
    inter_log = b + m_s[..., None]
    m_t = jnp.maximum(inter_log, jnp.max(d_log, axis=-1))
    scores = jnp.einsum('bhctd,bhcsd->bhcts', q, k) * jnp.exp(d_log - m_t[..., None])
    inter = jnp.exp(inter_log - m_t)
    num = (jnp.einsum('bhcts,bhcsd->bhctd', scores, v)
           + inter[..., None] * jnp.einsum('bhcde,bhcte->bhctd', c_s, q))
    den = scores.sum(-1) + inter * jnp.einsum('bhce,bhcte->bhct', n_s, q)
    return num / jnp.maximum(jnp.abs(den), jnp.exp(-m_t))[..., None]

def mlstm_direction(lat, ctx, with_ctx_out):
    q, k, v, lf, ig = lat
    qc, kc, vc, lfc, igc = ctx
    bz, hh, _, _, d = q.shape
    init = (jnp.zeros((bz, hh, d, d), jnp.float32), jnp.zeros((bz, hh, d), jnp.float32),
            jnp.zeros((bz, hh), jnp.float32))
    ctx_starts, ctx_final = mlstm_states(kc, vc, lfc, igc, init)
    lat_starts, _ = mlstm_states(k, v, lf, ig, ctx_final)
    h = mlstm_outputs(q, k, v, lf, ig, lat_starts)
    hc = mlstm_outputs(qc, kc, vc, lfc, igc, ctx_starts) if with_ctx_out else None
    return h, hc

def gla_states(k, v, loga, init):
    b = jnp.cumsum(loga, axis=-2)
    b_end = b[..., -1, :]
    s_loc = jnp.einsum('bhcld,bhcle->bhcde', k * jnp.exp(b_end[..., None, :] - b), v)

    def step(s, inp):
        be, sl = inp
        return jnp.exp(be)[..., None] * s + sl, s

    final, starts = lax.scan(step, init, (jnp.moveaxis(b_end, 2, 0), jnp.moveaxis(s_loc, 2, 0)))
    return jnp.moveaxis(starts, 0, 2), final

def gla_outputs(q, k, v, loga, s_start):
    ll = q.shape[-2]
    tri = jnp.tril(jnp.ones((ll, ll), dtype=bool))
    b = jnp.cumsum(loga, axis=-2)
    ref = b[..., ll // 2, :][..., None, :]
    att = jnp.einsum('bhctd,bhcsd->bhcts', q * jnp.exp(b - ref), k * jnp.exp(ref - b))
    att = jnp.where(tri, att, 0.0)
    return (jnp.einsum('bhcts,bhcse->bhcte', att, v)
            + jnp.einsum('bhctd,bhcde->bhcte', q * jnp.exp(b), s_start))

def gla_direction(lat, ctx, with_ctx_out):
    q, k, v, la = lat
    qc, kc, vc, lac = ctx
    bz, hh = q.shape[:2]
    init = jnp.zeros((bz, hh, GLA_DK, GLA_DV), jnp.float32)
    ctx_starts, ctx_final = gla_states(kc, vc, lac, init)
    lat_starts, _ = gla_states(k, v, la, ctx_final)
    h = gla_outputs(q, k, v, la, lat_starts)
    hc = gla_outputs(qc, kc, vc, lac, ctx_starts) if with_ctx_out else None
    return h, hc

def ml_inputs(p, d):
    return [to_chunks(orient(t, d), ML_CHUNK)
            for t in (p['ml_q'], p['ml_k'], p['ml_v'], p['ml_lf'][:, :, d], p['ml_ig'][:, :, d])]

def gla_inputs(p, d):
    return [to_chunks(orient(t, d), GLA_CHUNK)
            for t in (p['gla_q'], p['gla_k'], p['gla_v'], p['gla_la'][:, :, d])]

def mix_out(ml_h, ml_o, gla_h, gla_r, ml_g, gla_g, w_out, dtype):
    ml = jax.nn.sigmoid(ml_o) * head_rms(ml_h, ml_g)
    gl = jax.nn.silu(gla_r) * head_rms(gla_h, gla_g)
    return (jnp.concatenate([ml, gl], axis=-1) @ w_out).astype(dtype)

def token_mixer(h_lat, h_ctx, w_in, conv_w, gate_b, lr_w2, alpha_b, ml_g, gla_g, w_out,
                with_ctx_out):
    lat = prep_mixers(h_lat @ w_in, conv_w, gate_b, lr_w2, alpha_b, True)
    ctx = prep_mixers(h_ctx @ w_in, conv_w, gate_b, lr_w2, alpha_b, False)
    ml_lat, ml_ctx, gla_lat, gla_ctx = [], [], [], []
    for d in range(2):
        h, hc = mlstm_direction(ml_inputs(lat, d), ml_inputs(ctx, d), with_ctx_out)
        ml_lat.append(orient(from_chunks(h), d))
        g, gc = gla_direction(gla_inputs(lat, d), gla_inputs(ctx, d), with_ctx_out)
        gla_lat.append(orient(from_chunks(g), d))
        if with_ctx_out:
            ml_ctx.append(orient(from_chunks(hc), d))
            gla_ctx.append(orient(from_chunks(gc), d))
    y = mix_out(ml_lat[0] + ml_lat[1], lat['ml_o'], gla_lat[0] + gla_lat[1], lat['gla_r'],
                ml_g, gla_g, w_out, h_lat.dtype)
    yc = None
    if with_ctx_out:
        yc = mix_out(ml_ctx[0] + ml_ctx[1], ctx['ml_o'], gla_ctx[0] + gla_ctx[1], ctx['gla_r'],
                     ml_g, gla_g, w_out, h_ctx.dtype)
    return y, yc

def peer_ffn(h, wq, keys, u_tab, v_tab):
    bz, n, d = h.shape
    blocks = h.reshape(bz * n // PEER_BLOCK, PEER_BLOCK, d)

    def retrieve(xb):
        q = (xb @ wq).reshape(PEER_BLOCK, PEER_HEADS, 2, PEER_QDIM // 2)
        s = jnp.einsum('tphq,phkq->tphk', q, keys)
        top_s, top_i = lax.top_k(s, PEER_TOPK)
        cand = top_s[:, :, 0, :, None] + top_s[:, :, 1, None, :]
        best_s, best_c = lax.top_k(cand.reshape(PEER_BLOCK, PEER_HEADS, PEER_TOPK * PEER_TOPK),
                                   PEER_TOPK)
        i1 = jnp.take_along_axis(top_i[:, :, 0], best_c // PEER_TOPK, axis=-1)
        i2 = jnp.take_along_axis(top_i[:, :, 1], best_c % PEER_TOPK, axis=-1)
        idx = i1 * PEER_NKEYS + i2
        g = jax.nn.softmax(best_s.astype(jnp.float32), axis=-1).astype(xb.dtype)
        act = jax.nn.gelu(jnp.einsum('tpkd,td->tpk', u_tab[idx], xb), approximate=False)
        return jnp.einsum('tpk,tpkd->td', g * act, v_tab[idx])

    return lax.map(retrieve, blocks).reshape(bz, n, d)

def second_inputs(seed: int = 0) -> dict:
    key = jax.random.key(seed)
    ks = jax.random.split(key, 24)

    def nrm(k, shape, scale):
        return jax.random.normal(k, shape, jnp.float32) * scale

    f_bias = jnp.linspace(3.0, 6.0, ML_HEADS, dtype=jnp.float32)
    i_part = nrm(ks[8], (DEPTH_2, 2, 1, ML_HEADS), 0.1)
    f_part = f_bias + nrm(ks[9], (DEPTH_2, 2, 1, ML_HEADS), 0.1)
    ml_gate_b = jnp.concatenate([i_part, f_part], axis=2).reshape(DEPTH_2, 4 * ML_HEADS)
    return {
        'x': nrm(ks[0], (BATCH, SEQ, D_MODEL), 1.0),
        'c': nrm(ks[1], (BATCH, D_MODEL), 1.0),
        'ctx': nrm(ks[2], (BATCH, CTX_LEN, D_MODEL), 1.0),
        'c_ctx': nrm(ks[3], (D_MODEL,), 1.0),
        'w_mod': nrm(ks[4], (DEPTH_2, D_MODEL, 6 * D_MODEL), 0.5 * D_MODEL ** -0.5),
        'b_mod': nrm(ks[5], (DEPTH_2, 6 * D_MODEL), 0.02),
        'norm1_g': 1.0 + nrm(ks[6], (DEPTH_2, D_MODEL), 0.02),
        'w_in': nrm(ks[7], (DEPTH_2, D_MODEL, P_TOTAL), D_MODEL ** -0.5),
        'ml_conv_w': nrm(ks[10], (DEPTH_2, CONV_W, 2 * ML_WIDTH), CONV_W ** -0.5),
        'ml_gate_b': ml_gate_b,
        'ml_norm_g': 1.0 + nrm(ks[11], (DEPTH_2, ML_WIDTH), 0.02),
        'gla_lr_w2': nrm(ks[12], (DEPTH_2, 2, GLA_RANK, GLA_KEY_WIDTH), GLA_RANK ** -0.5),
        'gla_alpha_b': nrm(ks[13], (DEPTH_2, 2, GLA_KEY_WIDTH), 0.1),
        'gla_norm_g': 1.0 + nrm(ks[14], (DEPTH_2, GLA_WIDTH), 0.02),
        'w_out': nrm(ks[15], (DEPTH_2, MIX_WIDTH, D_MODEL), MIX_WIDTH ** -0.5),
        'norm2_g': 1.0 + nrm(ks[16], (DEPTH_2, D_MODEL), 0.02),
        'peer_wq': nrm(ks[17], (DEPTH_2, D_MODEL, PEER_HEADS * PEER_QDIM), D_MODEL ** -0.5),
        'peer_keys': nrm(ks[18], (DEPTH_2, PEER_HEADS, 2, PEER_NKEYS, PEER_QDIM // 2),
                         (PEER_QDIM // 2) ** -0.5),
        'peer_u': nrm(ks[19], (DEPTH_2, PEER_EXPERTS, D_MODEL), D_MODEL ** -0.5),
        'peer_v': nrm(ks[20], (DEPTH_2, PEER_EXPERTS, D_MODEL), PEER_HEADS ** -0.5),
        'norm_f_g': 1.0 + nrm(ks[21], (D_MODEL,), 0.02),
    }

def second_block(x, c, ctx, c_ctx, w_mod, b_mod, norm1_g, w_in, ml_conv_w, ml_gate_b, ml_norm_g,
              gla_lr_w2, gla_alpha_b, gla_norm_g, w_out, norm2_g, peer_wq, peer_keys, peer_u,
              peer_v, norm_f_g):
    cond = jax.nn.silu(c)
    cond_ctx = jax.nn.silu(c_ctx)
    for layer in range(DEPTH_2):
        update_ctx = layer + 1 < DEPTH_2
        mod = (cond @ w_mod[layer] + b_mod[layer])[:, None, :]
        mod_c = cond_ctx @ w_mod[layer] + b_mod[layer]
        sh1, sc1, g1, sh2, sc2, g2 = jnp.split(mod, 6, axis=-1)
        csh1, csc1, cg1, csh2, csc2, cg2 = jnp.split(mod_c, 6, axis=-1)

        h = rms_norm(x, norm1_g[layer]) * (1.0 + sc1) + sh1
        hc = rms_norm(ctx, norm1_g[layer]) * (1.0 + csc1) + csh1
        y, yc = token_mixer(h, hc, w_in[layer], ml_conv_w[layer], ml_gate_b[layer],
                            gla_lr_w2[layer], gla_alpha_b[layer], ml_norm_g[layer],
                            gla_norm_g[layer], w_out[layer], update_ctx)
        x = x + g1 * y
        h2 = rms_norm(x, norm2_g[layer]) * (1.0 + sc2) + sh2
        x = x + g2 * peer_ffn(h2, peer_wq[layer], peer_keys[layer], peer_u[layer], peer_v[layer])

        if update_ctx:
            ctx = ctx + cg1 * yc
            hc2 = rms_norm(ctx, norm2_g[layer]) * (1.0 + csc2) + csh2
            ctx = ctx + cg2 * peer_ffn(hc2, peer_wq[layer], peer_keys[layer], peer_u[layer],
                                       peer_v[layer])
    return rms_norm(x, norm_f_g)


def setup_inputs(seed=0):
    out = dict(first_inputs(seed))
    for name, value in second_inputs(seed + 1).items():
        if name != "x":
            out[name + "_2"] = value
    return out


def reference(
    x, ffn1_norm, ffn1_w_gate, ffn1_w_up, ffn1_w_down, mix_norm, w_in, a_rel_bias, c_q_norm,
    c_kv_norm, c_w_uq, c_w_ukv, w_out, ffn2_norm, ffn2_w_gate, ffn2_w_up, ffn2_w_down,
    final_norm, c_2, ctx_2, c_ctx_2, w_mod_2, b_mod_2, norm1_g_2, w_in_2, ml_conv_w_2,
    ml_gate_b_2, ml_norm_g_2, gla_lr_w2_2, gla_alpha_b_2, gla_norm_g_2, w_out_2, norm2_g_2,
    peer_wq_2, peer_keys_2, peer_u_2, peer_v_2, norm_f_g_2,
):
    x = first_block(
        x, ffn1_norm, ffn1_w_gate, ffn1_w_up, ffn1_w_down, mix_norm, w_in, a_rel_bias, c_q_norm,
        c_kv_norm, c_w_uq, c_w_ukv, w_out, ffn2_norm, ffn2_w_gate, ffn2_w_up, ffn2_w_down,
        final_norm,
    )
    return second_block(
        x, c_2, ctx_2, c_ctx_2, w_mod_2, b_mod_2, norm1_g_2, w_in_2, ml_conv_w_2, ml_gate_b_2,
        ml_norm_g_2, gla_lr_w2_2, gla_alpha_b_2, gla_norm_g_2, w_out_2, norm2_g_2, peer_wq_2,
        peer_keys_2, peer_u_2, peer_v_2, norm_f_g_2,
    )


_drawn_inputs = setup_inputs


def setup_inputs(seed=0):
    import zlib

    import numpy as np

    out = dict(_drawn_inputs(seed))
    spreads = {}
    factors = {'a_rel_bias': 3.405,
     'c_q_norm': 8.0,
     'c_kv_norm': 6.835,
     'ffn2_norm': 3.423,
     'b_mod_2': 2.813,
     'norm1_g_2': 7.836,
     'ml_norm_g_2': 64.0,
     'gla_alpha_b_2': 7.131,
     'gla_norm_g_2': 21.65,
     'norm2_g_2': 52.08,
     'norm_f_g_2': 8.463,
     'ml_conv_w_2': 6.406}
    for name, (base, spread) in spreads.items():
        noise = np.random.default_rng([zlib.crc32(name.encode()), seed]).standard_normal(out[name].shape)
        drawn = base * np.exp(spread * noise) if base else spread * noise
        out[name] = jnp.asarray(drawn.astype(out[name].dtype))
    for name, factor in factors.items():
        out[name] = (out[name] * factor).astype(out[name].dtype)
    return out
```

```python
import numpy as np
import concourse.bass as bass
from concourse import mybir
from contextlib import ExitStack

F32 = mybir.dt.float32
U32 = mybir.dt.uint32
ALU = mybir.AluOpType
ACT = mybir.ActivationFunctionType
AX = mybir.AxisListType
NEG = -1e30
LOW = -3e38
EPS = 1e-6


class Queue:

    def __init__(self, sem, chained):
        self.sem, self.chained, self.n, self.items = sem, chained, 0, []

    def __call__(self, fn, *after, free=False):
        if self.chained and not free and self.n:
            after = after + ((self.sem, self.n),)
        self.n += 1
        self.items.append((after, fn, self.sem, 1))
        return (self.sem, self.n)

    def wait(self, *after):
        self.items.append((after, None, None, 0))

    def dma(self, fn, sem, *after):
        self.items.append((after, fn, sem, 16))

    def now(self):
        return (self.sem, self.n)

    def emit(self, engine):
        seen = {}
        for after, fn, sem, by in self.items:
            for s, v in after:
                if v > seen.get(id(s), 0):
                    engine.wait_ge(s, v)
                    seen[id(s)] = v
            if fn is not None:
                fn(engine).then_inc(sem, by)


def build(nc, A, out, dbg, stop=None):
    ctx = ExitStack()
    with ctx:
        def sb(name, *shape, dt=F32):
            return ctx.enter_context(nc.sbuf_tensor(name, list(shape), dt))

        def sem(name):
            return ctx.enter_context(nc.semaphore(name))

        PE = Queue(sem("s_pe"), False)
        V = Queue(sem("s_v"), True)
        S = Queue(sem("s_s"), True)
        G = Queue(sem("s_g"), True)
        SP = Queue(sem("s_sp"), False)
        outsem = sem("s_out")

        PB = [ctx.enter_context(nc.psum_tensor(f"PB{i}", [128, 512], F32)) for i in range(8)]

        def mm(o, l, r, st=True, sp=True):
            return lambda e: e.matmul(o, l, r, start=st, stop=sp)

        def P(ops, *after):
            def run(e):
                for f in ops:
                    x = f(e)
                return x
            return PE(run, *after)

        def barrier():
            now = [q.now() for q in (PE, V, S, G)]
            for q in (PE, V, S, G):
                q.wait(*[t for t in now if t[0] is not q.sem or q is not PE])
            return now

        X = sb("X", 128, 2, 1024)
        HT = sb("HT", 128, 8, 512)
        NS, SLOT = 6, 2560
        RING = sb("RING", 128, NS, SLOT)
        BIGN = 25500
        BIG = sb("BIG", 128, BIGN)
        CST = sb("CST", 128, 1024)
        IDENT, J, J8 = CST[:, 0:128], CST[:, 128:256], CST[:, 256:384]
        ROPE = CST[:, 384:768].rearrange("p (b n) -> p b n", b=2)
        COLS = sb("COLS", 128, 384)
        SM = sb("SM", 128, 256)
        ONES = sb("ONES", 128, 128)
        HALF = sb("HALF", 1, 128)
        NROW = sb("NROW", 1, 64)
        ROWS = sb("ROWS", 128, 128)
        ROWS2 = sb("ROWS2", 128, 128)

        class Carve:

            def __init__(self, at=0):
                self.at = at

            def __call__(self, *shape, parts=128):
                n = int(np.prod(shape))
                assert self.at + n <= BIGN, (self.at, n)
                v = BIG[0:parts, self.at:self.at + n]
                self.at += n
                if len(shape) == 2:
                    v = v.rearrange("p (a b) -> p a b", a=shape[0])
                elif len(shape) == 3:
                    v = v.rearrange("p (a b c) -> p a b c", a=shape[0], b=shape[1])
                elif len(shape) == 4:
                    v = v.rearrange("p (a b c d) -> p a b c d", a=shape[0], b=shape[1], c=shape[2])
                return v

        slot_sem = [sem(f"s_w{i}") for i in range(NS)]
        slot_n = [0] * NS
        slot_free = [()] * NS
        at = [0]

        def load(src, *shape, parts=128, after=()):
            i = at[0] % NS
            at[0] += 1
            n = int(np.prod(shape))
            assert n <= SLOT and slot_free[i] is not None
            v = RING[0:parts, i, 0:n]
            if len(shape) == 2:
                v = v.rearrange("p (a b) -> p a b", a=shape[0])
            SP.dma(lambda e: e.dma_start(v, src), slot_sem[i], *slot_free[i], *after)
            slot_n[i] += 16
            slot_free[i] = None
            return v, (slot_sem[i], slot_n[i]), i

        def free(i, *tokens):
            slot_free[i] = tokens

        once = {}

        def load_once(name, dst, src, *after):
            if name not in once:
                once[name] = [sem("s_" + name), 0]
            s = once[name]
            s[1] += 16
            SP.dma(lambda e: e.dma_start(dst, src), s[0], *after)
            return (s[0], s[1])

        def dump(name, view, *after):
            if name in dbg:
                SP.dma(lambda e: e.dma_start(dbg[name], view), outsem, *after)
                dumped[0] += 16
                for q in (PE, V, S, G):
                    q.wait((outsem, dumped[0]))

        dumped = [0]

        load_once("cst", CST[:, 0:768], A["c_cst"])
        rows = [("ffn1_norm", 16), ("mix_norm", 16), ("ffn2_norm", 16), ("norm1_g_2", 8), ("norm2_g_2", 8),
                ("ml_norm_g_2", 4), ("gla_norm_g_2", 4), ("c_q_norm", 6), ("c_kv_norm", 4),
                ("ml_conv_w_2", 24), ("gla_alpha_b_2", 4)]
        COL = {}
        r = 0
        for name, n in rows:
            src = A[name]
            nd = len(src.shape)
            if nd == 1:
                v = src.rearrange("(a p) -> a p", p=128)
            elif nd == 2:
                v = src.rearrange("l (a p) -> (l a) p", p=128)
            else:
                v = src.rearrange("l k (a p) -> (l k a) p", p=128)
            load_once("cst", ROWS[r:r + n, :], v)
            COL[name] = r
            r += n
        nrow = r
        load_once("cst", ROWS2[0:48, :], A["b_mod_2"].rearrange("l (a p) -> (l a) p", p=128))
        load_once("cst", ROWS2[48:56, :], A["c_2"].rearrange("l (a p) -> (l a) p", p=128))
        cst = load_once("cst", ROWS2[56:64, :], A["c_ctx_2"].rearrange("(a p) -> a p", p=128))
        xin = load_once("x", X[:, :, :], A["x"].rearrange("o (b p) n -> p (o b) n", p=128))
        V(lambda e: e.memset(ONES[:, :], 1.0), free=True)
        V(lambda e: e.memset(HALF[:, :], 0.0), free=True)
        V(lambda e: e.memset(HALF[:, 0:64], 1.0))
        kv = V(lambda e: e.memset(NROW[:, :], NEG), free=True)
        P([lambda e: e.transpose(PB[0][:, 0:nrow], ROWS[0:nrow, :], IDENT[0:nrow, 0:nrow])], cst)
        t = P([lambda e: e.transpose(PB[1][:, 0:64], ROWS2[0:64, :], IDENT[0:64, 0:64])])
        V(lambda e: e.tensor_copy(COLS[:, 0:nrow], PB[0][:, 0:nrow]), t, cst, kv)
        V(lambda e: e.tensor_copy(COLS[:, 128:192], PB[1][:, 0:64]), xin)
        S.wait(cst, xin)

        def col(name, i):
            c = COL[name] + i
            return COLS[:, c:c + 1]

        def rstd(views, n, dst, junk, *after):
            for i, v in enumerate(views):
                t = S((lambda v, i: lambda e: e.activation(junk[:, 0:n], v, ACT.Square,
                                                          accum_out=dst[:, i:i + 1]))(v, i), *after)
            k = len(views)
            V(lambda e: e.tensor_scalar(dst[:, 0:k], dst[:, 0:k], 1.0 / n, EPS, ALU.mult, ALU.add), t)
            t = V(lambda e: e.reciprocal(dst[:, 0:k], dst[:, 0:k]))
            t = S(lambda e: e.activation(dst[:, 0:k], dst[:, 0:k], ACT.Sqrt), t)
            return t

        def norm_transposed(hn, src, dstT, gname, l, shift=None, toff=0, gcol=None, scol=None):
            t = rstd([src[:, b, :] for b in range(2)], 1024, SM[:, 0:2], hn.rearrange("p b n -> p (b n)"),
                     V.now())
            for b in range(2):
                t = V((lambda b: lambda e: e.tensor_scalar(hn[:, b, :], src[:, b, :], SM[:, b:b + 1], None,
                                                          ALU.mult))(b), t)
            ev = [V.now(), S.now()]
            for j in range(4):
                ops = []
                for k in range(2):
                    for b in range(2):
                        ops.append((lambda j, k, b: lambda e: e.transpose(
                            PB[4 + j][:, k * 256 + b * 128:k * 256 + b * 128 + 128],
                            hn[:, b, (2 * j + k) * 128:(2 * j + k + 1) * 128], IDENT))(j, k, b))
                tp = P(ops, t, *ev)
                for k in range(2):
                    kc = 2 * j + k
                    g = col(gname, l * 8 + kc) if gcol is None else gcol[:, kc:kc + 1]
                    if scol is None:
                        V((lambda j, k, kc, g: lambda e: e.tensor_scalar(
                            dstT[:, kc, toff:toff + 256], PB[4 + j][:, k * 256:k * 256 + 256], g, None,
                            ALU.mult))(j, k, kc, g), tp)
                    else:
                        V((lambda j, k, kc, g: lambda e: e.tensor_scalar(
                            dstT[:, kc, toff:toff + 256], PB[4 + j][:, k * 256:k * 256 + 256], g,
                            scol[:, kc:kc + 1], ALU.mult, ALU.add))(j, k, kc, g), tp)
            return V.now()

        def ffn(l, which):
            c = Carve()
            hn = c(2, 1024)
            sg = c(4, 256)
            act = c(4, 256)
            wg, wu, wd = (A[f"ffn{which}_w_{x}"][l] for x in ("gate", "up", "down"))
            wg = wg.rearrange("(k p) n -> p k n", p=128)
            wu = wu.rearrange("(k p) n -> p k n", p=128)
            wd = wd.rearrange("(f p) n -> p f n", p=128)
            barrier()
            ready = norm_transposed(hn, X, HT, f"ffn{which}_norm", l)
            ta = {}
            tdown = {}
            tiles = {}

            def down(f):
                w, arr, i = tiles[f // 2, 2]
                ops = [mm(PB[2 * b + h][:, :], act[:, f % 4, b * 128:(b + 1) * 128],
                          w[:, f % 2, h * 512:(h + 1) * 512], f == 0, f == 21)
                       for b in range(2) for h in range(2)]
                tdown[f] = P(ops, ta[f], arr)
                if f % 2:
                    free(i, tdown[f])

            for f in range(22):
                if f % 2 == 0:
                    j = f // 2
                    tiles[j, 0] = load(wg[:, :, j * 256:(j + 1) * 256], 8, 256)
                    tiles[j, 1] = load(wu[:, :, j * 256:(j + 1) * 256], 8, 256)
                    tiles[j, 2] = load(wd[:, 2 * j:2 * j + 2, :], 2, 1024)
                bank = PB[4 + f % 4]
                tk = None
                for s in range(2):
                    w, arr, i = tiles[f // 2, s]
                    ops = [mm(bank[:, s * 256:(s + 1) * 256], w[:, k, (f % 2) * 128:(f % 2 + 1) * 128],
                              HT[:, k, 0:256], k == 0, k == 7) for k in range(8)]
                    tk = P(ops, ready, arr, *([ta[f - 4]] if f >= 4 else []))
                    if f % 2:
                        free(i, tk)
                f4 = f % 4
                ts = S((lambda f4, bank: lambda e: e.activation(sg[:, f4, :], bank[:, 0:256], ACT.Silu))(f4, bank),
                       tk, *([ta[f - 4]] if f >= 4 else []), free=True)
                ta[f] = V((lambda f4, bank: lambda e: e.tensor_tensor(act[:, f4, :], bank[:, 256:512],
                                                                      sg[:, f4, :], ALU.mult))(f4, bank),
                          ts, *([tdown[f - 4]] if f >= 4 else []))
                if f >= 2:
                    down(f - 2)
            down(20)
            down(21)
            for b in range(2):
                for h in range(2):
                    xv = X[:, b, h * 512:(h + 1) * 512]
                    V((lambda b, h, xv: lambda e: e.scalar_tensor_tensor(xv, PB[2 * b + h][:, :], 0.5, xv,
                                                                         ALU.mult, ALU.add))(b, h, xv),
                      tdown[21])

        def rope(x, nh, d, b, off, t1, t2):
            h = d // 2
            C = ROPE[:, b, off:off + d].unsqueeze(1).broadcast_to([128, nh, d])
            S1 = ROPE[:, b, off + d:off + d + h].unsqueeze(1).broadcast_to([128, nh, h])
            S2 = ROPE[:, b, off + d + h:off + 2 * d].unsqueeze(1).broadcast_to([128, nh, h])
            t1 = t1[:, 0:nh * d].rearrange("p (n d) -> p n d", d=d)
            t2 = t2[:, 0:nh * d].rearrange("p (n d) -> p n d", d=d)
            V(lambda e: e.tensor_tensor(t1, x, C, ALU.mult))
            V(lambda e: e.tensor_tensor(t2[:, :, 0:h], x[:, :, h:d], S1, ALU.mult), free=True)
            V(lambda e: e.tensor_tensor(t2[:, :, h:d], x[:, :, 0:h], S2, ALU.mult), free=True)
            return V(lambda e: e.tensor_tensor(x, t1, t2, ALU.add))

        def transposes(jobs, banks, after):
            toks = []
            bank_free = {}
            for g in range(0, len(jobs), 4):
                bk = banks[(g // 4) % len(banks)]
                part = jobs[g:g + 4]
                ops = []
                for i, (dst, src) in enumerate(part):
                    m, n = dst.shape[0], src.shape[0]
                    ops.append((lambda i, src, m, n, bk: lambda e: e.transpose(
                        PB[bk][0:m, i * 128:i * 128 + n], src, IDENT[0:n, 0:n]))(i, src, m, n, bk))
                tp = P(ops, *after, *bank_free.get(bk, ()))
                got = []
                for i, (dst, src) in enumerate(part):
                    m, n = dst.shape[0], src.shape[0]
                    q = (S, V)[(g // 4) % 2]
                    if q is S:
                        fn = (lambda i, dst, m, n, bk: lambda e: e.activation(
                            dst, PB[bk][0:m, i * 128:i * 128 + n], ACT.Copy))(i, dst, m, n, bk)
                    else:
                        fn = (lambda i, dst, m, n, bk: lambda e: e.tensor_copy(
                            dst, PB[bk][0:m, i * 128:i * 128 + n]))(i, dst, m, n, bk)
                    got.append(q(fn, tp, *after, free=True))
                bank_free[bk] = tuple(got)
                toks += got
            return (S.now(), V.now())

        def attend(units, sc, pb, pt, rs, ready):
            n = len(units)
            t1, tmx, tex, ttr, tev, to, tdst = {}, {}, {}, {}, {}, {}, {}
            for i in range(n + 3):
                if i < n:
                    q, k, extra, vs, dst, scale = units[i]
                    nk = k.shape[-1]
                    ps = PB[i % 4]
                    ops = [mm(ps[:, 0:nk], q, k, True, not extra)]
                    for x, (a, b_, l_, r_) in enumerate(extra):
                        ops.append(mm(ps[:, a:b_], l_, r_, False, x == len(extra) - 1))
                    t1[i] = P(ops, *ready, *([tex[i - 4]] if i >= 4 else []))
                    m = rs[:, (i % 4) * 4:(i % 4) * 4 + 4]
                    V((lambda ps, m, nk: lambda e: e.tensor_reduce(m[:, 0:1], ps[:, 0:nk], AX.X, ALU.max,
                                                                  negate=True))(ps, m, nk), t1[i],
                      *([tex[i - 4]] if i >= 4 else []))
                    tmx[i] = V((lambda m, scale: lambda e: e.tensor_scalar(m[:, 1:2], m[:, 0:1], scale, None,
                                                                          ALU.mult))(m, scale))
                    tex[i] = S((lambda ps, m, nk, i, scale: lambda e: e.activation(
                        pb[:, i % 4, 0:nk], ps[:, 0:nk], ACT.Exp, bias=m[:, 1:2], scale=scale,
                        accum_out=m[:, 2:3]))(ps, m, nk, i, scale), tmx[i],
                        *([ttr[i - 4], tdst[i - 4]] if i >= 4 else []))
                u = i - 2
                if 0 <= u < n:
                    nb = units[u][1].shape[-1] // 128
                    bk = PB[4 + u % 2]
                    ops = [(lambda kb, bk, u: lambda e: e.transpose(bk[:, kb * 128:(kb + 1) * 128],
                                                                  pb[:, u % 4, kb * 128:(kb + 1) * 128],
                                                                  IDENT))(kb, bk, u) for kb in range(nb)]
                    ttr[u] = P(ops, tex[u], *([tev[u - 2]] if u >= 2 else []))
                    q_ = (S, V)[u % 2]
                    if q_ is S:
                        fn = (lambda bk, u, nb: lambda e: e.activation(pt[:, u % 2, 0:nb * 128], bk[:, 0:nb * 128],
                                                                      ACT.Copy))(bk, u, nb)
                    else:
                        fn = (lambda bk, u, nb: lambda e: e.tensor_copy(pt[:, u % 2, 0:nb * 128],
                                                                       bk[:, 0:nb * 128]))(bk, u, nb)
                    tev[u] = q_(fn, ttr[u], *([to[u - 2]] if u >= 2 else []))
                u = i - 3
                if 0 <= u < n:
                    vs, dst = units[u][3], units[u][4]
                    po = PB[6 + u % 2][:, 0:64]
                    ops = [mm(po, pt[:, u % 2, kb * 128:(kb + 1) * 128], v, kb == 0, kb == len(vs) - 1)
                           for kb, v in enumerate(vs)]
                    to[u] = P(ops, tev[u], *([tdst[u - 2]] if u >= 2 else []))
                    m = rs[:, (u % 4) * 4:(u % 4) * 4 + 4]
                    V((lambda m: lambda e: e.reciprocal(m[:, 3:4], m[:, 2:3]))(m), tex[u])
                    tdst[u] = V((lambda m, dst, po: lambda e: e.tensor_scalar(dst, po, m[:, 3:4], None,
                                                                            ALU.mult))(m, dst, po), to[u])
            return V.now()

        def hybrid(l):
            c = Carve()
            H = c(2, 3080)
            hn = c(2, 1024)
            ready = (barrier(), norm_transposed(hn, X, HT, "mix_norm", l))[1]
            wv = A["w_in"][l].rearrange("(k p) n -> p k n", p=128)
            W = 308
            prev = {}
            for j in range(10):
                w, arr, i = load(wv[:, :, j * W:(j + 1) * W], 8, W)
                for b in range(2):
                    n = 2 * j + b
                    bank = PB[n % 4]
                    tk = P([mm(bank[:, 0:W], HT[:, k, b * 128:(b + 1) * 128], w[:, k, :], k == 0, k == 7)
                            for k in range(8)], ready, arr, *([prev[n - 4]] if n >= 4 else []))
                    dst = H[:, b, j * W:(j + 1) * W]
                    if n % 2:
                        prev[n] = V((lambda dst, bank: lambda e: e.tensor_copy(dst, bank[:, 0:W]))(dst, bank), tk)
                    else:
                        prev[n] = S((lambda dst, bank: lambda e: e.activation(dst, bank[:, 0:W], ACT.Copy))(dst, bank),
                                    tk)
                free(i, tk)
            barrier()
            dump(f"H{l}", H, V.now(), S.now())
            O = hn
            WB = c(6, 256)
            lb = load_once("bias", WB, A["c_relw"][l], V.now(), PE.now())
            t1, t2 = c(640), c(640)
            for b in range(2):
                rope(H[:, b, 1152:1792].rearrange("p (n d) -> p n d", d=64), 10, 64, b, 0, t1, t2)
                rope(H[:, b, 2112:2400].rearrange("p (n d) -> p n d", d=32), 9, 32, b, 128, t1, t2)
                rope(H[:, b, 3048:3080].rearrange("p (n d) -> p n d", d=32), 1, 32, b, 128, t1, t2)
            LT = c(5, 256)
            ln = c(2, 640)
            rstd([H[:, b, 2408:2792] for b in range(2)], 384, SM[:, 0:2], t1, V.now())
            rstd([H[:, b, 2792:3048] for b in range(2)], 256, SM[:, 2:4], t1, V.now())
            for b in range(2):
                V((lambda b: lambda e: e.tensor_scalar(ln[:, b, 0:384], H[:, b, 2408:2792], SM[:, b:b + 1], None,
                                                      ALU.mult))(b), S.now())
                V((lambda b: lambda e: e.tensor_scalar(ln[:, b, 384:640], H[:, b, 2792:3048], SM[:, 2 + b:3 + b],
                                                      None, ALU.mult))(b))
            tl = V.now()
            for k in range(5):
                g = col("c_q_norm", l * 3 + k) if k < 3 else col("c_kv_norm", l * 2 + k - 3)
                tp = P([(lambda k, b: lambda e: e.transpose(PB[k][:, b * 128:(b + 1) * 128],
                                                           ln[:, b, k * 128:(k + 1) * 128], IDENT))(k, b)
                        for b in range(2)], tl)
                V((lambda k, g: lambda e: e.tensor_scalar(LT[:, k, :], PB[k][:, 0:256], g, None, ALU.mult))(k, g), tp)
            QC = c(2, 480)
            KV = c(2, 640)
            wq, aq, iq = load(A["c_w_uq"][l].rearrange("(k p) n -> p k n", p=128), 3, 480)
            wk, ak, ik = load(A["c_w_ukv"][l].rearrange("(k p) n -> p k n", p=128), 2, 640)
            barrier()
            tq = []
            for b in range(2):
                tk = P([mm(PB[b][:, 0:480], LT[:, k, b * 128:(b + 1) * 128], wq[:, k, :], k == 0, k == 2)
                        for k in range(3)], aq)
                V((lambda b: lambda e: e.tensor_copy(QC[:, b, :], PB[b][:, 0:480]))(b), tk)
                for h in range(2):
                    tk2 = P([mm(PB[2 + 2 * b + h][:, 0:320], LT[:, 3 + k, b * 128:(b + 1) * 128],
                                wk[:, k, h * 320:(h + 1) * 320], k == 0, k == 1) for k in range(2)], ak)
                    S((lambda b, h: lambda e: e.activation(KV[:, b, h * 320:(h + 1) * 320],
                                                          PB[2 + 2 * b + h][:, 0:320], ACT.Copy))(b, h), tk2)
            free(iq, tk)
            free(ik, tk2)
            QV = QC.rearrange("p b (h d) -> p b h d", d=96)
            KVV = KV.rearrange("p b (h d) -> p b h d", d=128)
            KC = c(2, 480)
            KCV = KC.rearrange("p b (h d) -> p b h d", d=96)
            for b in range(2):
                rope(QV[:, b, :, 64:96], 5, 32, b, 128, t1, t2)
                G((lambda b: lambda e: e.tensor_copy(KCV[:, b, :, 0:64], KVV[:, b, :, 0:64]))(b), S.now())
                G((lambda b: lambda e: e.tensor_copy(
                    KCV[:, b, :, 64:96], H[:, b, 3048:3080].unsqueeze(1).broadcast_to([128, 5, 32])))(b), tl)
            IK = t1[:, 0:256].rearrange("p (b r d) -> p b r d", b=2, r=4)
            for b in range(2):
                t = V((lambda b: lambda e: e.tensor_copy(
                    IK[:, b, :, :], H[:, b, 2368:2400].unsqueeze(1).broadcast_to([128, 4, 32])))(b))
            barrier()
            AQ, AK, BQ, BK = c(3, 256), c(3, 256), c(3, 256), c(3, 256)
            CQ, CK = c(5, 256), c(5, 256)
            IQT, IKT = c(2, 256), c(256)
            jobs = []
            for b in range(2):
                s = slice(b * 128, (b + 1) * 128)
                for k in range(2):
                    jobs.append((IQT[:, k, s], H[:, b, 2112 + k * 128:2112 + (k + 1) * 128]))
                jobs.append((IKT[:, s], IK[:, b, :, :].rearrange("p r d -> p (r d)")))
            for dst, base, w in ((AQ, 0, 384), (AK, 384, 384), (BQ, 1152, 320), (BK, 1472, 320)):
                for k in range(3):
                    for b in range(2):
                        m = min(128, w - k * 128)
                        jobs.append((dst[0:m, k, b * 128:(b + 1) * 128],
                                     H[:, b, base + k * 128:base + k * 128 + m]))
            for h in range(5):
                for b in range(2):
                    jobs.append((CQ[0:96, h, b * 128:(b + 1) * 128], QC[:, b, h * 96:(h + 1) * 96]))
                    jobs.append((CK[0:96, h, b * 128:(b + 1) * 128], KC[:, b, h * 96:(h + 1) * 96]))
            transposes(jobs, list(range(8)), (V.now(),))
            barrier()
            SCR = c(2, 256)
            WRK = c(2, 256)
            TMP = c(256)
            SEL = c(2, 256)
            WI = SM[:, 16:32].rearrange("p (b h) -> p b h", b=2)
            t = V(lambda e: e.tensor_scalar(WI, H[:, :, 2400:2408], float(8 ** -0.5 * 32 ** -0.5), None, ALU.mult))
            for b in range(2):
                nk = 128 * (b + 1)
                toks = []
                for h in range(8):
                    r0 = 32 * (h % 4)
                    toks.append(P([mm(PB[h][:, 0:nk], IQT[r0:r0 + 32, h // 4, b * 128:(b + 1) * 128],
                                      IKT[r0:r0 + 32, 0:nk])], V.now()))
                for h in range(8):
                    dst = SCR[:, b, 0:nk]
                    if h == 0:
                        V((lambda dst, nk, b: lambda e: e.tensor_scalar(
                            dst, PB[0][:, 0:nk], 0.0, WI[:, b, 0:1], ALU.max, ALU.mult))(dst, nk, b), toks[0])
                    else:
                        V((lambda h, nk, b: lambda e: e.tensor_scalar(
                            TMP[:, 0:nk], PB[h][:, 0:nk], 0.0, WI[:, b, h:h + 1], ALU.max, ALU.mult))(h, nk, b),
                          toks[h])
                        V((lambda dst, nk: lambda e: e.tensor_tensor(dst, dst, TMP[:, 0:nk], ALU.add))(dst, nk))
                V((lambda b, nk: lambda e: e.memset(SCR[0:64, b, nk - 64:nk], NEG))(b, nk))
                m8 = SM[:, 32:40]
                for r_ in range(8):
                    src = (SCR if r_ == 0 else WRK)[:, b, 0:nk]
                    V((lambda src: lambda e: e.max(m8, src))(src))
                    V((lambda src, b, nk: lambda e: e.match_replace(WRK[:, b, 0:nk], m8, src, LOW))(src, b, nk))
                V((lambda b, nk: lambda e: e.tensor_scalar(SEL[:, b, 0:nk], WRK[:, b, 0:nk], -2e38, NEG,
                                                          ALU.is_gt, ALU.mult))(b, nk))
            barrier()
            pb = ln.rearrange("p b n -> p (b n)")[:, 0:1024].rearrange("p (a n) -> p a n", a=4)
            pt = KC.rearrange("p b n -> p (b n)")[:, 0:512].rearrange("p (a n) -> p a n", a=2)
            rs = SM[:, 48:64]
            units = []
            for h in range(6):
                for b in range(2):
                    nk = 128 * (b + 1)
                    r0 = 64 * (h % 2)
                    vs = [H[:, kb, 768 + h * 64:768 + (h + 1) * 64] for kb in range(b + 1)]
                    units.append((AQ[r0:r0 + 64, h // 2, b * 128:(b + 1) * 128], AK[r0:r0 + 64, h // 2, 0:nk],
                                  [(0, nk, J8, WB[:, h, 128 * (1 - b):256]), (nk - 64, nk, HALF[:, :], NROW[:, :])],
                                  vs, O[:, b, h * 64:(h + 1) * 64], 0.125))
            for h in range(5):
                for b in range(2):
                    nk = 128 * (b + 1)
                    r0 = 64 * (h % 2)
                    vs = [H[:, kb, 1792 + h * 64:1792 + (h + 1) * 64] for kb in range(b + 1)]
                    units.append((BQ[r0:r0 + 64, h // 2, b * 128:(b + 1) * 128], BK[r0:r0 + 64, h // 2, 0:nk],
                                  [(0, nk, IDENT, SEL[:, b, 0:nk])],
                                  vs, O[:, b, 384 + h * 64:384 + (h + 1) * 64], 0.125))
            for h in range(5):
                for b in range(2):
                    nk = 128 * (b + 1)
                    vs = [KVV[:, kb, h, 64:128] for kb in range(b + 1)]
                    units.append((CQ[0:96, h, b * 128:(b + 1) * 128], CK[0:96, h, 0:nk],
                                  [(nk - 64, nk, HALF[:, :], NROW[:, :])],
                                  vs, O[:, b, 704 + h * 64:704 + (h + 1) * 64], float(96 ** -0.5)))
            attend(units, None, pb, pt, rs, [lb])
            barrier()
            dump(f"O{l}", O, V.now())
            project_out(O, A["w_out"][l], None)
            dump(f"X{l}", X[:, :, :], V.now())

        def project_out(O, w, gate, gains=None):
            for j in range(4):
                tp = P([(lambda j, k, b: lambda e: e.transpose(
                    PB[j][:, k * 256 + b * 128:k * 256 + b * 128 + 128],
                    O[:, b, (2 * j + k) * 128:(2 * j + k + 1) * 128], IDENT))(j, k, b)
                    for k in range(2) for b in range(2)])
                for k in range(2):
                    kc = 2 * j + k
                    if gains is None:
                        V((lambda j, k, kc: lambda e: e.tensor_copy(
                            HT[:, kc, 0:256], PB[j][:, k * 256:k * 256 + 256]))(j, k, kc), tp)
                    else:
                        V((lambda j, k, kc: lambda e: e.tensor_scalar(
                            HT[:, kc, 0:256], PB[j][:, k * 256:k * 256 + 256], gains(kc), None,
                            ALU.mult))(j, k, kc), tp)
            ready = V.now()
            wv = w.rearrange("(k p) n -> p k n", p=128)
            n = 0
            prev = {}
            for j in range(4):
                wt, arr, i = load(wv[:, :, j * 256:(j + 1) * 256], 8, 256)
                for b in range(2):
                    bank = PB[4 + n % 4]
                    tk = P([mm(bank[:, 0:256], HT[:, k, b * 128:(b + 1) * 128], wt[:, k, :], k == 0, k == 7)
                            for k in range(8)], ready, arr, *([prev[n - 4]] if n >= 4 else []))
                    xv = X[:, b, j * 256:(j + 1) * 256]
                    if gate is None:
                        prev[n] = V((lambda bank, xv: lambda e: e.tensor_tensor(xv, xv, bank[:, 0:256],
                                                                              ALU.add))(bank, xv), tk)
                    else:
                        gv = gate[:, j * 256:(j + 1) * 256]
                        V((lambda bank, gv: lambda e: e.tensor_tensor(bank[:, 0:256], bank[:, 0:256], gv,
                                                                     ALU.mult))(bank, gv), tk)
                        prev[n] = V((lambda bank, xv: lambda e: e.tensor_tensor(xv, xv, bank[:, 0:256],
                                                                              ALU.add))(bank, xv), tk)
                    n += 1
                free(i, tk)

        class Region:

            def __init__(self, base, at, end):
                self.base, self.at, self.end = base, at, end

            def __call__(self, *shape, parts=128):
                n = int(np.prod(shape))
                assert self.at + n <= self.end, (self.at, n, self.end)
                v = self.base[0:parts, self.at:self.at + n]
                self.at += n
                names = "abcd"[:len(shape)]
                if len(shape) > 1:
                    v = v.rearrange("p (" + " ".join(names) + ") -> p " + " ".join(names),
                                    **{k: s for k, s in zip(names[:-1], shape)})
                return v

        def second():
            barrier()
            reg = Region(BIG, 0, BIGN)
            G1, G2 = reg(1024), reg(1024)
            at_a = reg.at
            hn, CX = reg(2, 1024), reg(2, 1024)
            FG = HT[:, 0:2, :].rearrange("p a b -> p (a b)")
            C2 = sb("C2", 128, 2064)
            now = V.now(), S.now(), PE.now(), G.now()
            c2 = load_once("c2", C2[:, :], A["c_cst2"])
            c2 = load_once("c2", FG, A["final_norm"].partition_broadcast(128), *now)
            c2 = load_once("c2", G1, A["b_mod_2"][0, 2048:3072].partition_broadcast(128), *now)
            c2 = load_once("c2", G2, A["b_mod_2"][0, 5120:6144].partition_broadcast(128), *now)
            c2 = load_once("c2", CX, A["ctx_2"].rearrange("o (b p) n -> p (o b) n", p=128), *now)
            MASK = C2[:, 0:256].rearrange("p (d t) -> p d t", d=2)
            GM = C2[:, 256:512].rearrange("p (d t) -> p d t", d=2)
            D0, D1, D64 = C2[0:8, 512:1024], C2[0:8, 1024:1536], C2[:, 1536:2048]
            IO16 = C2[:, 2048:2064]
            V.wait(c2)
            S.wait(c2)
            PE.wait(c2)
            tr = rstd([X[:, b, :] for b in range(2)], 1024, SM[:, 0:2], hn.rearrange("p b n -> p (b n)"), *now)
            for b in range(2):
                V((lambda b: lambda e: e.scalar_tensor_tensor(X[:, b, :], X[:, b, :], SM[:, b:b + 1], FG,
                                                             ALU.mult, ALU.mult))(b), tr)
            dump("XN", X[:, :, :], V.now())
            CT = SM[:, 64:80].rearrange("p (k w) -> p k w", w=2)
            CF = SM[:, 80:96]
            ts = S(lambda e: e.activation(CF, COLS[:, 176:192], ACT.Silu), V.now())
            tct = V(lambda e: e.tensor_copy(CT, CF.rearrange("p (w k) -> p k w", w=2)), ts)
            MR = hn[0:2, 0, :].rearrange("p (a n) -> p a n", a=4)
            wm = A["w_mod_2"][0].rearrange("(k p) n -> p k n", p=128)
            mcol = 0
            tmr, tuse = {}, {}
            for j in range(24):
                w, arr, i = load(wm[:, :, j * 256:(j + 1) * 256], 8, 256)
                bank = PB[j % 2]
                tk = P([mm(bank[0:2, 0:256], CT[:, k, :], w[:, k, :], k == 0, k == 7) for k in range(8)],
                       tct, arr, *([tmr[j - 2]] if j >= 2 else []))
                free(i, tk)
                tmr[j] = V((lambda j, bank: lambda e: e.tensor_copy(MR[:, j % 4, :], bank[0:2, 0:256]))(j, bank),
                           tk, *([tuse[j - 4]] if j >= 4 else []))
                if j // 4 in (2, 5):
                    dst = (G1 if j // 4 == 2 else G2)[:, (j % 4) * 256:(j % 4 + 1) * 256]
                    gb = PB[2 + j % 2]
                    tuse[j] = P([mm(gb[:, 0:256], ONES[0:1, :], MR[0:1, j % 4, :])], tmr[j])
                    V((lambda dst, gb: lambda e: e.tensor_tensor(dst, dst, gb[:, 0:256], ALU.add))(dst, gb), tuse[j])
                    tmr[j] = V.now()
                else:
                    ops = []
                    for h in range(2):
                        ops.append((lambda mcol, h, j: lambda e: e.transpose(
                            PB[7][:, 2 * mcol + 2 * h:2 * mcol + 2 * h + 2],
                            MR[:, j % 4, h * 128:(h + 1) * 128], IDENT[0:2, 0:2]))(mcol, h, j))
                    mcol += 2
                    tuse[j] = P(ops, tmr[j])
            MC = SM[:, 96:160].rearrange("p (s k w) -> p s k w", s=4, w=2)
            pv = PB[7][:, 0:64].rearrange("p (s k w) -> p s k w", s=4, w=2)
            for s, c0 in enumerate((0, 8, 24, 32)):
                bc = COLS[:, 128 + c0:136 + c0].unsqueeze(2).broadcast_to([128, 8, 2])
                V((lambda s, bc: lambda e: e.tensor_tensor(MC[:, s, :, :], pv[:, s, :, :], bc, ALU.add))(s, bc),
                  tuse[19])
            GA = SM[:, 160:208].rearrange("p (s k) -> p s k", s=6)
            for s, (row, w, name) in enumerate(((1, 0, "norm1_g_2"), (1, 1, "norm1_g_2"), (3, 0, "norm2_g_2"))):
                gn = COLS[:, COL[name]:COL[name] + 8]
                V((lambda s, row, w, gn: lambda e: e.scalar_tensor_tensor(
                    GA[:, 2 * s, :], MC[:, row, :, w], 1.0, gn, ALU.add, ALU.mult))(s, row, w, gn))
                V((lambda s, row, w: lambda e: e.tensor_copy(GA[:, 2 * s + 1, :], MC[:, row - 1, :, w]))(s, row, w))
            barrier()
            norm_transposed(hn, X, HT, None, 0, toff=0, gcol=GA[:, 0, :], scol=GA[:, 1, :])
            ready = norm_transposed(hn, CX, HT, None, 0, toff=256, gcol=GA[:, 2, :], scol=GA[:, 3, :])
            QR, KR = Region(BIG, at_a, at_a + 3072)(4, 256), Region(BIG, at_a + 1024, at_a + 3072)(4, 512)
            QT, KT, KTOK = reg(4, 256), reg(4, 512), reg(4, 512)
            VA = reg(4, 4, 129)
            MO, GV, GR, GQ, GK = reg(2, 512), reg(4, 512), reg(2, 512), reg(2, 256), reg(2, 512)
            GLR = reg(512, parts=32)
            GT = SM[:, 0:64].rearrange("p (b g) -> p b g", b=4)
            barrier()
            V(lambda e: e.memset(VA[:, :, :, 128:129], 1.0))
            wv = A["w_in_2"][0].rearrange("(k p) n -> p k n", p=128)
            n = [0]
            prev = {}

            def project(prods, width, evac, arr, parts=128):
                m = n[0]
                bank = PB[m % 8]
                tk = P([mm(bank[0:parts, 0:width], l_, r_, k == 0, k == 7) for k, (l_, r_) in enumerate(prods)],
                       ready, arr, *([prev[m - 8]] if m >= 8 else []))
                q = (V, S)[m % 2]
                prev[m] = q(evac(q, bank[0:parts, 0:width]), tk)
                n[0] += 1
                return tk

            def copy_to(dst, scale=1.0):
                def evac(q, src):
                    if q is V:
                        return lambda e: e.tensor_scalar(dst, src, scale, None, ALU.mult)
                    return lambda e: e.activation(dst, src, ACT.Copy, scale=scale)
                return evac

            def features(w, arr, c0, m, nt, dst, scale=1.0):
                return project([(w[:, k, c0:c0 + m], HT[:, k, 0:nt]) for k in range(8)], nt, copy_to(dst, scale),
                               arr, parts=m)

            def tokens(w, arr, c0, m, b, dst):
                s = slice(b * 128, (b + 1) * 128)
                return project([(HT[:, k, s], w[:, k, c0:c0 + m]) for k in range(8)], m,
                               copy_to(dst) if len(dst.shape) == 2 else
                               (lambda q, src: copy_to(dst)(q, src.rearrange("p (h d) -> p h d", d=128))), arr)

            def cols(a, b_):
                return load(wv[:, :, a:b_], 8, b_ - a)

            for j in range(2):
                w, arr, i = cols(j * 256, j * 256 + 256)
                for k in range(2):
                    tk = features(w, arr, k * 128, 128, 256, QR[:, 2 * j + k, :])
                free(i, tk)
            for j in range(2):
                w, arr, i = cols(512 + j * 256, 768 + j * 256)
                for k in range(2):
                    tk = features(w, arr, k * 128, 128, 512, KR[:, 2 * j + k, :])
                free(i, tk)
            for j in range(2):
                w, arr, i = cols(1024 + j * 256, 1280 + j * 256)
                for b in range(4):
                    tk = tokens(w, arr, 0, 256, b, VA[:, b, 2 * j:2 * j + 2, 0:128])
                free(i, tk)
            for j in range(2):
                w, arr, i = cols(1536 + j * 256, 1792 + j * 256)
                for b in range(2):
                    tk = tokens(w, arr, 0, 256, b, MO[:, b, j * 256:(j + 1) * 256])
                free(i, tk)
            w, arr, i = cols(2048, 2320)
            for b in range(4):
                tokens(w, arr, 0, 16, b, GT[:, b, :])
            for k in range(2):
                tk = features(w, arr, 16 + k * 128, 128, 256, GQ[:, k, :], 0.125)
            free(i, tk)
            w, arr, i = cols(2320, 2576)
            for k in range(2):
                tk = features(w, arr, k * 128, 128, 512, GK[:, k, :])
            free(i, tk)
            for j in range(2):
                w, arr, i = cols(2576 + j * 256, 2832 + j * 256)
                for b in range(4):
                    tk = tokens(w, arr, 0, 256, b, GV[:, b, j * 256:(j + 1) * 256])
                free(i, tk)
            w, arr, i = cols(3088, 3344)
            for b in range(2):
                tk = tokens(w, arr, 0, 256, b, GR[:, b, 0:256])
            free(i, tk)
            w, arr, i = cols(3344, 3632)
            for b in range(2):
                tokens(w, arr, 0, 256, b, GR[:, b, 256:512])
            tk = features(w, arr, 256, 32, 512, GLR)
            free(i, tk)
            t = barrier()
            cw = COL["ml_conv_w_2"]
            for src, dst, h0, nt in ((QR, QT, 0, 256), (KR, KT, 4, 512)):
                for h in range(4):
                    w0, w1, w2 = (COLS[:, cw + 8 * j + h0 + h:cw + 8 * j + h0 + h + 1] for j in range(3))
                    u, y = src[:, h, :], dst[:, h, :]
                    V((lambda u, y, w1: lambda e: e.tensor_scalar(y, u, w1, None, ALU.mult))(u, y, w1))
                    parts = [(u[:, 0:256].rearrange("p (r t) -> p r t", t=64),
                              y[:, 0:256].rearrange("p (r t) -> p r t", t=64), 64)]
                    if nt == 512:
                        parts.append((u[:, 256:512].rearrange("p (r t) -> p r t", t=256),
                                      y[:, 256:512].rearrange("p (r t) -> p r t", t=256), 256))
                    for uu, yy, m in parts:
                        for wc, a_, b_ in ((w0, slice(1, m), slice(0, m - 1)), (w2, slice(0, m - 1), slice(1, m))):
                            V((lambda uu, yy, wc, a_, b_: lambda e: e.scalar_tensor_tensor(
                                yy[:, :, a_], uu[:, :, b_], wc, yy[:, :, a_], ALU.mult, ALU.add))(uu, yy, wc, a_, b_))
            ts = S(lambda e: e.activation(QT, QT, ACT.Silu), V.now())
            ts = S(lambda e: e.activation(KT, KT, ACT.Silu))
            V(lambda e: e.tensor_scalar(KT, KT, float(128 ** -0.5), None, ALU.mult), ts)
            ts = S(lambda e: e.activation(MO, MO, ACT.Sigmoid))
            ts = S(lambda e: e.activation(GR, GR, ACT.Silu))
            barrier()
            transposes([(KTOK[:, b, h * 128:(h + 1) * 128], KT[:, h, b * 128:(b + 1) * 128])
                        for b in range(4) for h in range(4)], list(range(8)), (V.now(),))
            tmp = Region(BIG, reg.at, BIGN)
            GB = tmp(16)
            tb_ = load_once("gb", GB, A["ml_gate_b_2"][0].partition_broadcast(128), *t)
            GP = tmp(4, 4, 8)
            V(lambda e: e.tensor_tensor(GT, GT, GB.unsqueeze(1).broadcast_to([128, 4, 16]), ALU.add), tb_)
            V(lambda e: e.memset(GP, 0.0))
            for d in range(2):
                for q in range(2):
                    V((lambda d, q: lambda e: e.tensor_copy(GP[:, 2 * q + d, :, d * 4:d * 4 + 4],
                                                           GT[:, :, d * 8 + q * 4:d * 8 + q * 4 + 4]))(d, q))
            barrier()
            ORD = [[2, 3, 0, 1], [3, 2, 1, 0]]
            ops = []
            for q in range(2):
                for c in range(4):
                    o_ = PB[q][0:8, c * 128:(c + 1) * 128]
                    ops.append(mm(o_, GP[:, 2 * q, ORD[0][c], :], IDENT, True, False))
                    ops.append(mm(o_, GP[:, 2 * q + 1, ORD[1][c], :], J, False, True))
            tk = P(ops)
            rr = Region(BIG, at_a, at_a + 4096)
            RQ = rr(5, 4, 128, parts=8)
            Bc, CM, LF = rr(4, 128, parts=8), rr(4, 128, parts=8), rr(4, 128, parts=8)
            fl = "p c t -> p (c t)"
            igp = PB[0][0:8, :]
            fp = PB[1][0:8, :]
            lf, bb, cm = LF.rearrange(fl), Bc.rearrange(fl), CM.rearrange(fl)
            S(lambda e: e.activation(lf, fp, ACT.Abs), tk, V.now())
            ts = S(lambda e: e.activation(lf, lf, ACT.Exp, scale=-1.0))
            V(lambda e: e.tensor_scalar(lf, lf, 1.0, None, ALU.add), ts)
            ts = S(lambda e: e.activation(lf, lf, ACT.Ln), V.now())
            V(lambda e: e.scalar_tensor_tensor(lf, fp, 0.0, lf, ALU.min, ALU.subtract), ts)
            V(lambda e: e.tensor_tensor_scan(bb, D0, lf, 0.0, ALU.mult, ALU.add))
            a_row = RQ[:, 0, :, :].rearrange(fl)
            V(lambda e: e.tensor_tensor(a_row, igp, bb, ALU.subtract))
            V(lambda e: e.tensor_tensor_scan(cm, D1, a_row, LOW, ALU.add, ALU.max))
            MM = SM[0:8, 208:216]
            V(lambda e: e.memset(MM[:, 0:1], 0.0))
            for c in range(4):
                V((lambda c: lambda e: e.tensor_scalar(MM[:, c + 1:c + 2], CM[:, c, 127:128], MM[:, c:c + 1],
                                                      Bc[:, c, 127:128], ALU.max, ALU.add))(c))
                V((lambda c: lambda e: e.tensor_scalar(CM[:, c, :], CM[:, c, :], MM[:, c:c + 1], None,
                                                      ALU.max))(c))
            V(lambda e: e.tensor_scalar(RQ[:, 1, :, :], CM, -1.0, None, ALU.mult))
            V(lambda e: e.tensor_tensor(LF, Bc, CM, ALU.add))
            S(lambda e: e.activation(RQ[:, 3, :, :], LF, ACT.Exp, scale=-1.0), V.now())
            for c in range(4):
                S((lambda c: lambda e: e.activation(RQ[:, 2, c, :], CM[:, c, :], ACT.Exp, scale=-1.0,
                                                   bias=MM[:, c:c + 1]))(c))
                S((lambda c: lambda e: e.activation(RQ[:, 4, c, :], RQ[:, 0, c, :], ACT.Exp,
                                                   bias=RQ[:, 1, c, 127:128]))(c))
            DG8 = tmp(4, 8, parts=8)
            for c in range(4):
                V((lambda c: lambda e: e.tensor_scalar(DG8[:, c, :], IDENT[0:8, 0:8], RQ[:, 2, c, 127:128], None,
                                                      ALU.mult))(c), S.now())
            DEC = tmp(32)
            ops = [(lambda c, q: lambda e: e.transpose(PB[2][:, (c * 5 + q) * 8:(c * 5 + q) * 8 + 8],
                                                      RQ[:, q, c, :], IDENT[0:8, 0:8]))(c, q)
                   for c in range(4) for q in range(5)]
            ops.append(mm(PB[3][:, 0:32], ONES[0:8, :], DG8.rearrange("p c r -> p (c r)")))
            tk = P(ops, V.now(), S.now())
            CP, NAT = tmp(4, 5, 8), tmp(4, 5, 8)
            V(lambda e: e.tensor_copy(CP.rearrange("p c q r -> p (c q r)"), PB[2][:, 0:160]), tk)
            V(lambda e: e.tensor_copy(DEC, PB[3][:, 0:32]))
            tk = P([mm(PB[4][:, 0:160], J, CP.rearrange("p c q r -> p (c q r)"))], V.now())
            nv = PB[4][:, 0:160].rearrange("p (c q r) -> p c q r", c=4, q=5)
            for c in range(4):
                V((lambda c: lambda e: e.tensor_copy(NAT[:, ORD[0][c], :, 0:4], CP[:, c, :, 0:4]))(c), tk)
                V((lambda c: lambda e: e.tensor_copy(NAT[:, ORD[1][c], :, 4:8], nv[:, c, :, 4:8]))(c))
            barrier()
            EE, ST, DGm = tmp(4, 128), tmp(4, 128), tmp(4, 128)
            CS = [tmp(4, 129), tmp(4, 129)]
            WVA = tmp(4, 129)
            PS1 = tmp(2, 129)
            RR = tmp(2, 129)
            HM = tmp(2, 4, 128)
            DN = SM[:, 216:224]

            def state(d, c):
                b = ORD[d][c]
                wc = NAT[:, b, 4, 4 * d:4 * d + 4].unsqueeze(2).broadcast_to([128, 4, 129])
                tw = V(lambda e: e.tensor_tensor(WVA, VA[:, b, :, :], wc, ALU.mult), PE.now())
                for p in range(2):
                    tk = P([mm(PB[p][:, h * 129:(h + 1) * 129], KTOK[:, b, (2 * p + h) * 128:(2 * p + h + 1) * 128],
                               WVA[:, 2 * p + h, :]) for h in range(2)], tw)
                    for h in range(2):
                        hh = 2 * p + h
                        src = PB[p][:, h * 129:(h + 1) * 129]
                        dst = CS[d][:, hh, :]
                        if c == 0:
                            V((lambda dst, src: lambda e: e.tensor_copy(dst, src))(dst, src), tk)
                        else:
                            x = c * 8 + d * 4 + hh
                            V((lambda dst, src, x: lambda e: e.scalar_tensor_tensor(
                                dst, dst, DEC[:, x:x + 1], src, ALU.mult, ALU.add))(dst, src, x), tk)

            def outputs(d, c):
                b = ORD[d][c]
                s = slice(b * 128, (b + 1) * 128)
                gc = NAT[:, b, 1, 4 * d:4 * d + 4].unsqueeze(2).broadcast_to([128, 4, 128])
                tg = V(lambda e: e.tensor_tensor(DGm, IDENT.unsqueeze(1).broadcast_to([128, 4, 128]), gc,
                                                 ALU.mult), PE.now())
                te = P([mm(PB[2][:, :], ONES[:, :], DGm.rearrange("p h t -> p (h t)"), True, False)] +
                       [mm(PB[2][:, h * 128:(h + 1) * 128], IDENT, MASK[:, d, :], False, h == 3)
                        for h in range(4)], tg, S.now())
                for h in range(4):
                    S((lambda h: lambda e: e.activation(EE[:, h, :], PB[2][:, h * 128:(h + 1) * 128], ACT.Exp,
                                                       bias=NAT[:, b, 0, 4 * d + h:4 * d + h + 1]))(h), te, tg)
                tq = P([mm(PB[3][:, h * 128:(h + 1) * 128], KT[:, h, s], QT[:, h, s]) for h in range(4)], tg)
                tst = V(lambda e: e.tensor_tensor(ST.rearrange("p h t -> p (h t)"), PB[3][:, :],
                                                  EE.rearrange("p h t -> p (h t)"), ALU.mult), tq, S.now())
                for p in range(2):
                    tk1 = P([mm(PB[4 + p][:, h * 129:(h + 1) * 129], ST[:, 2 * p + h, :], VA[:, b, 2 * p + h, :])
                             for h in range(2)], tst)
                    tk2 = P([mm(PB[6 + p][:, h * 129:(h + 1) * 129], QT[:, 2 * p + h, s], CS[d][:, 2 * p + h, :])
                             for h in range(2)], tst)
                    ts = S((lambda p: lambda e: e.activation(PS1.rearrange("p h t -> p (h t)"),
                                                            PB[4 + p][:, 0:258], ACT.Copy))(p), tk1, V.now())
                    for h in range(2):
                        hh = 2 * p + h
                        r = 4 * d + hh
                        V((lambda p, h, r: lambda e: e.scalar_tensor_tensor(
                            RR[:, h, :], PB[6 + p][:, h * 129:(h + 1) * 129], NAT[:, b, 2, r:r + 1], PS1[:, h, :],
                            ALU.mult, ALU.add))(p, h, r), tk2, ts)
                    r = 4 * d + 2 * p
                    V(lambda e: e.scalar_tensor_tensor(DN[:, 0:2], RR[:, :, 128], -1.0, RR[:, :, 128],
                                                       ALU.mult, ALU.max))
                    V((lambda r: lambda e: e.tensor_tensor(DN[:, 0:2], DN[:, 0:2], NAT[:, b, 3, r:r + 2],
                                                          ALU.max))(r))
                    V(lambda e: e.reciprocal(DN[:, 2:4], DN[:, 0:2]))
                    for h in range(2):
                        dst = HM[:, b, 2 * p + h, :]
                        if d == 0:
                            V((lambda dst, h: lambda e: e.tensor_scalar(dst, RR[:, h, 0:128], DN[:, 2 + h:3 + h], None,
                                                                       ALU.mult))(dst, h))
                        else:
                            V((lambda dst, h: lambda e: e.scalar_tensor_tensor(
                                dst, RR[:, h, 0:128], DN[:, 2 + h:3 + h], dst, ALU.mult, ALU.add))(dst, h))

            for d in range(2):
                state(d, 0)
                state(d, 1)
                outputs(d, 2)
                state(d, 2)
                outputs(d, 3)
            dump("HM", HM.rearrange("p b h t -> p b (h t)"), V.now())
            t = barrier()
            keep = Region(BIG, at_a, at_a + 4096 + 7184)
            LA, BB = keep(2, 2, 512), keep(2, 2, 512)
            W2 = keep(512, parts=32)
            QB = keep(2, 2, 256)
            QQ, KK, KS, KST = keep(2, 256), keep(2, 256), keep(2, 512), keep(4, 256)
            SS = [keep(2, 256), keep(2, 256)]
            AT = keep(4, 128)
            EBE = keep(2, 2, 8)
            HG = HT[:, 0:2, :]
            TE = HT[:, 2:4, :]
            TF = HT[:, 4:6, 0:256]
            tz = V(lambda e: e.memset(W2, 0.0))
            for d in range(2):
                tw = load_once("lrw", W2[d * 16:(d + 1) * 16, d * 256:(d + 1) * 256], A["gla_lr_w2_2"][0, d], tz, *t)
            V(lambda e: e.memset(SS[0], 0.0))
            V(lambda e: e.memset(SS[1], 0.0))
            V(lambda e: e.memset(QB, 0.0))
            ops = [mm(PB[2 * d + f][:, :], W2[:, d * 256 + f * 128:d * 256 + (f + 1) * 128], GLR)
                   for d in range(2) for f in range(2)]
            tk = P(ops, tw, V.now())
            for d in range(2):
                for f in range(2):
                    V((lambda d, f: lambda e: e.tensor_scalar(LA[:, d, f, :], PB[2 * d + f][:, :],
                                                             col("gla_alpha_b_2", 2 * d + f), None, ALU.add))(d, f), tk)
            S(lambda e: e.activation(BB, LA, ACT.Abs), V.now())
            ts = S(lambda e: e.activation(BB, BB, ACT.Exp, scale=-1.0))
            V(lambda e: e.tensor_scalar(BB, BB, 1.0, None, ALU.add), ts)
            ts = S(lambda e: e.activation(BB, BB, ACT.Ln), V.now())
            V(lambda e: e.tensor_scalar(LA, LA, 0.0, None, ALU.min))
            V(lambda e: e.tensor_tensor(LA, LA, BB, ALU.subtract), ts)
            V(lambda e: e.tensor_scalar(LA, LA, 1.0 / 16, None, ALU.mult))
            for d in range(2):
                for f in range(2):
                    V((lambda d, f: lambda e: e.tensor_tensor_scan(BB[:, d, f, :], D64, LA[:, d, f, :], 0.0,
                                                                  ALU.mult, ALU.add))(d, f))
            for f in range(2):
                bv = BB[:, 1, f, :].rearrange("p (c t) -> p c t", t=64)
                lv = LA[:, 1, f, :].rearrange("p (c t) -> p c t", t=64)
                V((lambda bv, lv: lambda e: e.tensor_tensor(lv, lv, bv, ALU.subtract))(bv, lv))
                V((lambda bv, lv: lambda e: e.tensor_tensor(
                    lv, lv, bv[:, :, 63:64].broadcast_to([128, 8, 64]), ALU.add))(bv, lv))
                V((lambda f: lambda e: e.tensor_copy(BB[:, 1, f, :], LA[:, 1, f, :]))(f))
            ZR = AT[0:1, :, :].rearrange("p h t -> p (h t)")
            V(lambda e: e.memset(ZR, 0.0))
            P([mm(PB[6 + b][:, :], ONES[0:1, :], ZR, True, False) for b in range(2)], V.now())
            pair = [0]
            for d in range(2):
                end, mid = (63, 32) if d == 0 else (0, 31)
                for f in range(2):
                    bv = BB[:, d, f, :].rearrange("p (c t) -> p c t", t=64)
                    be = bv[:, :, end:end + 1]
                    te = TE[:, f, :].rearrange("p (c t) -> p c t", t=64)
                    tf = TF[:, f, :].rearrange("p (c t) -> p c t", t=64)
                    V((lambda te, be, bv: lambda e: e.tensor_tensor(te, be.broadcast_to([128, 8, 64]), bv,
                                                                   ALU.subtract))(te, be, bv), PE.now())
                    V((lambda tf, bv, mid: lambda e: e.tensor_tensor(
                        tf, bv[:, 0:4, :], bv[:, 0:4, mid:mid + 1].broadcast_to([128, 4, 64]),
                        ALU.subtract))(tf, bv, mid))
                    S((lambda d, f, be: lambda e: e.activation(EBE[:, d, f, :].unsqueeze(2), be, ACT.Exp))(d, f, be),
                      V.now())
                S(lambda e: e.activation(TE, TE, ACT.Exp), V.now())
                S(lambda e: e.activation(QQ, TF, ACT.Exp), PE.now())
                S(lambda e: e.activation(KK, TF, ACT.Exp, scale=-1.0))
                S((lambda d: lambda e: e.activation(TF, BB[:, d, :, 0:256], ACT.Exp))(d))
                V(lambda e: e.tensor_tensor(KS, TE, GK, ALU.mult), S.now(), PE.now())
                V(lambda e: e.tensor_tensor(QQ, QQ, GQ, ALU.mult))
                V(lambda e: e.tensor_tensor(KK, KK, GK[:, :, 0:256], ALU.mult))
                for f in range(2):
                    tv = TF[:, f, :].rearrange("p (c h t) -> p c h t", c=2, h=2)
                    gv = GQ[:, f, :].rearrange("p (c h t) -> p c h t", c=2, h=2)
                    for x in range(2):
                        qv = QB[:, x, f, :].rearrange("p (c h t) -> p c h t", c=2, h=2)
                        V((lambda qv, tv, gv, x: lambda e: e.tensor_tensor(qv[:, :, x, :], tv[:, :, x, :],
                                                                         gv[:, :, x, :], ALU.mult))(qv, tv, gv, x))
                barrier()
                transposes([(KST[:, b, f * 128:(f + 1) * 128], KS[:, f, b * 128:(b + 1) * 128])
                            for b in range(4) for f in range(2)], [0, 1], (V.now(),))
                barrier()
                for b in range(2):
                    s = slice(b * 128, (b + 1) * 128)
                    gm = GM[:, d, :].unsqueeze(1).broadcast_to([128, 2, 128])
                    for x in range(2):
                        r = slice(64 * x, 64 * x + 64)
                        bank = PB[(2, 5)[x]]
                        tk = P([mm(bank[:, f * 128:(f + 1) * 128], KK[r, f, s], QQ[r, f, s]) for f in range(2)],
                               V.now())
                        av = AT.rearrange("p (f x) t -> p f x t", x=2)[:, :, x, :]
                        pv2 = bank[:, 0:256].rearrange("p (h t) -> p h t", h=2)
                        V((lambda av, pv2, gm: lambda e: e.tensor_tensor(av, pv2, gm, ALU.min))(av, pv2, gm), tk)
                        V((lambda av, gm: lambda e: e.scalar_tensor_tensor(av, gm, -1.0, av, ALU.mult,
                                                                         ALU.max))(av, gm))
                    P([mm(PB[6 + b][:, h * 128:(h + 1) * 128], AT[:, h, :], GV[:, b, h * 128:(h + 1) * 128],
                          False, False) for h in range(4)], V.now())
                    V.wait(PE.now())
                chunks = [4, 5, 6, 7, 0, 1, 2, 3] if d == 0 else [7, 6, 5, 4, 3, 2, 1, 0]
                if d == 1:
                    V(lambda e: e.memset(SS[0], 0.0), PE.now())
                for n_, ch in enumerate(chunks):
                    b, x = ch // 2, ch % 2
                    cur, nxt = SS[n_ % 2], SS[(n_ + 1) % 2]
                    if n_ >= 4:
                        last = d == 1 and n_ == 7
                        P([mm(PB[6 + b][:, f * 256:(f + 1) * 256], QB[:, x, f, b * 128:(b + 1) * 128], cur[:, f, :],
                              False, (d == 1 and x == 0 and f == 1)) for f in range(2)], V.now())
                    if n_ < 7:
                        bank = PB[3 + n_ % 2]
                        tk = P([mm(bank[:, f * 256:(f + 1) * 256], KST[64 * x:64 * x + 64, b, f * 128:(f + 1) * 128],
                                   GV[64 * x:64 * x + 64, b, f * 256:(f + 1) * 256]) for f in range(2)], V.now())
                        for f in range(2):
                            for h in range(2):
                                r = slice(64 * h, 64 * h + 64)
                                q = slice(128 * h, 128 * h + 128)
                                V((lambda cur, nxt, f, r, q, bank, h, ch, d: lambda e: e.scalar_tensor_tensor(
                                    nxt[r, f, q], cur[r, f, q], EBE[r, d, f, ch:ch + 1],
                                    bank[r, f * 256 + 128 * h:f * 256 + 128 * h + 128], ALU.mult, ALU.add))(
                                        cur, nxt, f, r, q, bank, h, ch, d), tk)
                barrier()
            for b in range(2):
                S((lambda b: lambda e: e.activation(HG[:, b, :], PB[6 + b][:, :], ACT.Copy))(b))
            dump("HG", HG, S.now())
            barrier()
            OO = keep.base[:, at_a:at_a + 2048].rearrange("p (b n) -> p b n", b=2)
            R8 = SM[:, 224:240]
            TT = BIG[:, at_a + 2048:at_a + 3072].rearrange("p (b n) -> p b n", b=2)
            HMf = HM.rearrange("p b h t -> p b (h t)")
            for s_, (src, gate, o0) in enumerate(((HMf, MO, 0), (HG, GR, 512))):
                V((lambda src: lambda e: e.tensor_tensor(TT, src, src, ALU.mult))(src))
                V((lambda s_: lambda e: e.tensor_reduce(R8[:, s_ * 8:s_ * 8 + 8],
                                                       TT.rearrange("p b (h t) -> p (b h) t", h=4), AX.X,
                                                       ALU.add))(s_))
                V((lambda src, gate, o0: lambda e: e.tensor_tensor(OO[:, :, o0:o0 + 512], src, gate,
                                                                  ALU.mult))(src, gate, o0))
            V(lambda e: e.tensor_scalar(R8, R8, 1.0 / 128, EPS, ALU.mult, ALU.add))
            V(lambda e: e.reciprocal(R8, R8))
            ts = S(lambda e: e.activation(R8, R8, ACT.Sqrt), V.now())
            for s_ in range(2):
                for b in range(2):
                    ov = OO[:, b, s_ * 512:(s_ + 1) * 512].rearrange("p (h t) -> p h t", h=4)
                    rv = R8[:, s_ * 8 + b * 4:s_ * 8 + b * 4 + 4].unsqueeze(2).broadcast_to([128, 4, 128])
                    V((lambda ov, rv: lambda e: e.tensor_tensor(ov, ov, rv, ALU.mult))(ov, rv), ts)
            barrier()
            project_out(OO, A["w_out_2"][0], G1,
                        lambda kc: col("ml_norm_g_2", kc) if kc < 4 else col("gla_norm_g_2", kc - 4))
            dump("Y", X[:, :, :], V.now())
            barrier()
            if stop == "mix":
                return
            peer(GA, G2, IO16, at_a)

        def peer(GA, G2, IO16, at_a):
            reg = Region(BIG, at_a, BIGN)
            hn = reg(2, 1024)
            H2 = reg(2, 1024)
            QP = reg(16, 256)
            KEYT = reg(16, 128)
            big = Region(BIG, reg.at, BIGN)
            KEYS = big(16, 128)
            tkeys = load_once("keys", KEYS, A["peer_keys_2"][0].rearrange("h s k q -> k (h s) q"),
                              V.now(), S.now(), PE.now(), G.now())
            norm_transposed(hn, X, HT, None, 0, gcol=GA[:, 4, :], scol=GA[:, 5, :])
            barrier()
            transposes([(H2[:, b, k * 128:(k + 1) * 128], HT[:, k, b * 128:(b + 1) * 128])
                        for b in range(2) for k in range(8)], [0, 1, 2, 3], (V.now(),))
            V.wait(tkeys)
            S.wait(tkeys)
            PE.wait(tkeys)
            transposes([(KEYT[:, k, :], KEYS[:, k, :]) for k in range(16)], [4, 5, 6, 7], (V.now(),))
            barrier()
            wv = A["peer_wq_2"][0].rearrange("(k p) n -> p k n", p=128)
            prev = {}
            for j in range(8):
                w, arr, i = load(wv[:, :, j * 256:(j + 1) * 256], 8, 256)
                for c in range(2):
                    tk = P([mm(PB[j % 4][:, c * 256:(c + 1) * 256], w[:, k, c * 128:(c + 1) * 128], HT[:, k, 0:256],
                               k == 0, k == 7) for k in range(8)], arr, *([prev[j - 4]] if j >= 4 else []))
                free(i, tk)
                prev[j] = S((lambda j: lambda e: e.activation(
                    QP[:, 2 * j:2 * j + 2, :], PB[j % 4][:, :].rearrange("p (a b) -> p a b", a=2), ACT.Copy))(j), tk)
            barrier()
            big = Region(BIG, reg.at, BIGN)
            SC, WK, WK2 = big(16, 128), big(256), big(256)
            CD, OH = big(8, 16, 16), big(8, 16, 16)
            TS = big(16, 16)
            TI, TIF = big(16, 16), big(16, 16)
            TI = TI.bitcast(U32)
            BS, I1F, I2F, ID1, ID2 = big(8, 16), big(8, 16), big(8, 16), big(8, 16), big(8, 16)
            BI, I1 = big(8, 16).bitcast(U32), big(8, 16).bitcast(U32)
            IDX = big(2, 128).bitcast(U32)
            GW = big(2, 8, 16)
            AV = big(2, 128)
            for b in range(2):
                for g in range(4):
                    tk = P([mm(PB[4 + g][:, x * 128:(x + 1) * 128], QP[:, 4 * g + x, b * 128:(b + 1) * 128],
                               KEYT[:, 4 * g + x, :]) for x in range(4)], V.now(), S.now())
                    S((lambda g: lambda e: e.activation(SC[:, 4 * g:4 * g + 4, :],
                                                       PB[4 + g][:, :].rearrange("p (a b) -> p a b", a=4),
                                                       ACT.Copy))(g), tk, V.now())

                def top16(vals, idx, src, work):
                    V(lambda e: e.max(vals[:, 0:8], src))
                    V(lambda e: e.max_index(idx[:, 0:8], vals[:, 0:8], src))
                    V(lambda e: e.match_replace(work, vals[:, 0:8], src, LOW))
                    V(lambda e: e.max(vals[:, 8:16], work))
                    V(lambda e: e.max_index(idx[:, 8:16], vals[:, 8:16], work))

                V.wait(S.now())
                for x in range(16):
                    top16(TS[:, x, :], TI[:, x, :], SC[:, x, :], WK[:, 0:128])
                tsv = TS.rearrange("p (h s) k -> p h s k", s=2)
                V(lambda e: e.tensor_copy(TIF, TI))
                V(lambda e: e.tensor_tensor(CD, tsv[:, :, 0, :].unsqueeze(3).broadcast_to([128, 8, 16, 16]),
                                            tsv[:, :, 1, :].unsqueeze(2).broadcast_to([128, 8, 16, 16]), ALU.add))
                for h in range(8):
                    top16(BS[:, h, :], BI[:, h, :], CD[:, h, :, :].rearrange("p a b -> p (a b)"), WK)
                tif = TIF.rearrange("p (h s) k -> p h s k", s=2)
                for s_, (idf, dst) in enumerate(((I1F, ID1), (I2F, ID2))):
                    op, val = ((ALU.logical_shift_right, 4), (ALU.bitwise_and, 15))[s_]
                    V((lambda op, val: lambda e: e.tensor_scalar(I1, BI, val, None, op))(op, val))
                    V((lambda idf: lambda e: e.tensor_copy(idf, I1))(idf))
                    V((lambda idf: lambda e: e.tensor_tensor(
                        OH.rearrange("p h k j -> p (h k) j"),
                        idf.rearrange("p h k -> p (h k)").unsqueeze(2).broadcast_to([128, 128, 16]),
                        IO16.unsqueeze(1).broadcast_to([128, 128, 16]), ALU.is_equal))(idf))
                    V((lambda s_: lambda e: e.tensor_tensor(
                        OH, OH, tif[:, :, s_, :].unsqueeze(2).broadcast_to([128, 8, 16, 16]), ALU.mult))(s_))
                    V((lambda dst: lambda e: e.tensor_reduce(dst.rearrange("p h k -> p (h k)"),
                                                            OH.rearrange("p h k j -> p (h k) j"), AX.X,
                                                            ALU.add))(dst))
                V(lambda e: e.scalar_tensor_tensor(ID1, ID1, 128.0, ID2, ALU.mult, ALU.add))
                V((lambda b: lambda e: e.tensor_copy(IDX[:, b, :], ID1.rearrange("p h k -> p (h k)")))(b))
                V((lambda b: lambda e: e.tensor_tensor(GW[:, b, :, :], BS,
                                                      BS[:, :, 0:1].broadcast_to([128, 8, 16]),
                                                      ALU.subtract))(b))
                ts = S((lambda b: lambda e: e.activation(GW[:, b, :, :], GW[:, b, :, :], ACT.Exp))(b), V.now())
                V((lambda b: lambda e: e.tensor_reduce(SM[:, 0:8], GW[:, b, :, :], AX.X, ALU.add))(b), ts)
                V(lambda e: e.reciprocal(SM[:, 8:16], SM[:, 0:8]))
                V((lambda b: lambda e: e.tensor_tensor(GW[:, b, :, :], GW[:, b, :, :],
                                                      SM[:, 8:16].unsqueeze(2).broadcast_to([128, 8, 16]),
                                                      ALU.mult))(b))
            barrier()
            NG = 15
            ROW = RING[:, :, :].rearrange("p a b -> p (a b)").rearrange("p (s n) -> p s n", n=1024)
            gs = [sem(f"s_row{i}") for i in range(NG)]
            gn = [0] * NG
            used = [None] * NG
            ACC = QP.rearrange("p a b -> p (a b)")[:, 0:2048].rearrange("p (b n) -> p b n", b=2)
            JUNK = hn[:, 0, :]
            V(lambda e: e.memset(ACC, 0.0))
            tx = V.now()
            g = 0
            ups, us = A["peer_u_2"][0], A["peer_v_2"][0]

            def gather(table, b, j):
                nonlocal g
                i = g % NG
                g += 1
                G.dma((lambda i, b, j: lambda e: e.indirect_dma_start(
                    out=ROW[:, i, :], out_offset=None, in_=table,
                    in_offset=bass.IndirectOffsetOnAxis(ap=IDX[:, b, j:j + 1], axis=0)))(i, b, j),
                    gs[i], *([used[i]] if used[i] else [tx]))
                gn[i] += 16
                return i, (gs[i], gn[i])

            for b in range(2):
                for j in range(128):
                    i, arr = gather(ups, b, j)
                    used[i] = V((lambda i, b, j: lambda e: e.tensor_tensor_reduce(
                        out=JUNK, in0=ROW[:, i, :], in1=H2[:, b, :], scale=1.0, scalar=0.0, op0=ALU.mult,
                        op1=ALU.add, accum_out=AV[:, b, j:j + 1]))(i, b, j), arr)
                ts = S((lambda b: lambda e: e.activation(AV[:, b, :], AV[:, b, :], ACT.Gelu))(b), V.now())
                V((lambda b: lambda e: e.tensor_tensor(AV[:, b, :], AV[:, b, :],
                                                      GW[:, b, :, :].rearrange("p h k -> p (h k)"),
                                                      ALU.mult))(b), ts)
                for j in range(128):
                    i, arr = gather(us, b, j)
                    used[i] = V((lambda i, b, j: lambda e: e.scalar_tensor_tensor(
                        ACC[:, b, :], ROW[:, i, :], AV[:, b, j:j + 1], ACC[:, b, :], ALU.mult, ALU.add))(i, b, j), arr)
            FG = HT[:, 0:2, :].rearrange("p a b -> p (a b)")
            tf = load_once("nf", FG, A["norm_f_g_2"].partition_broadcast(128), tx)
            V(lambda e: e.tensor_tensor(ACC, ACC, G2.unsqueeze(1).broadcast_to([128, 2, 1024]), ALU.mult))
            V(lambda e: e.tensor_tensor(X[:, :, :], X[:, :, :], ACC, ALU.add))
            tr = rstd([X[:, b, :] for b in range(2)], 1024, SM[:, 0:2], hn.rearrange("p b n -> p (b n)"), V.now())
            for b in range(2):
                V((lambda b: lambda e: e.scalar_tensor_tensor(X[:, b, :], X[:, b, :], SM[:, b:b + 1], FG,
                                                             ALU.mult, ALU.mult))(b), tr, tf)

        def finish():
            t = barrier()
            SP.dma(lambda e: e.dma_start(out.rearrange("o (b p) n -> p (o b) n", p=128), X[:, :, :]), outsem, *t)
            SP.wait((outsem, dumped[0] + 16))

        def program():
            for l in range(2):
                ffn(l, 1)
                dump(f"F{l}", X[:, :, :], V.now())
                if stop == f"ffn{l}":
                    return
                hybrid(l)
                if stop == f"hyb{l}":
                    return
                ffn(l, 2)
            if stop == "first":
                return
            second()

        program()
        finish()

        block = ctx.enter_context(nc.Block())

        @block.sync
        def _(e):
            SP.emit(e)

        @block.tensor
        def _(e):
            PE.emit(e)

        @block.vector
        def _(e):
            V.emit(e)

        @block.scalar
        def _(e):
            S.emit(e)

        @block.gpsimd
        def _(e):
            G.emit(e)


_INS = ["x", "ffn1_norm", "ffn1_w_gate", "ffn1_w_up", "ffn1_w_down", "mix_norm", "w_in", "c_q_norm",
        "c_kv_norm", "c_w_uq", "c_w_ukv", "w_out", "ffn2_norm", "ffn2_w_gate", "ffn2_w_up", "ffn2_w_down",
        "final_norm", "c_2", "ctx_2", "c_ctx_2", "w_mod_2", "b_mod_2", "norm1_g_2", "w_in_2", "ml_conv_w_2",
        "ml_gate_b_2", "ml_norm_g_2", "gla_lr_w2_2", "gla_alpha_b_2", "gla_norm_g_2", "w_out_2", "norm2_g_2",
        "peer_wq_2", "peer_keys_2", "peer_u_2", "peer_v_2", "norm_f_g_2"]


def constants():
    c = np.zeros((128, 768), np.float32)
    c[:, 0:128] = np.eye(128)
    c[:, 128:256] = np.eye(128)[::-1]
    c[:, 256:384] = 8 * np.eye(128)[::-1]
    pos = np.arange(256, dtype=np.float32)
    t = np.zeros((256, 192), np.float32)
    for d, off in ((64, 0), (32, 128)):
        inv = (np.float32(10000.0) ** (-np.arange(0, d, 2, dtype=np.float32) / np.float32(d))).astype(np.float32)
        ang = (pos[:, None] * inv[None, :]).astype(np.float32).astype(np.float64)
        co, si = np.cos(ang), np.sin(ang)
        t[:, off:off + 2 * d] = np.concatenate([co, co, -si, si], axis=1)
    c[:, 384:768] = t.reshape(2, 128, 192).transpose(1, 0, 2).reshape(128, 384)
    return c


def constants2():
    c = np.zeros((128, 2064), np.float32)
    s, t = np.arange(128)[:, None], np.arange(128)[None, :]
    c[:, 0:128] = np.where(s <= t, 0, NEG)
    c[:, 128:256] = np.where(s >= t, 0, NEG)
    same = s // 64 == t // 64
    c[:, 256:384] = np.where(same & (s <= t), 3e38, 0)
    c[:, 384:512] = np.where(same & (s >= t), 3e38, 0)
    n = np.arange(512)
    c[:, 512:1024] = np.where(n % 128 == 0, 0, 1)
    c[:, 1024:1536] = np.where(n % 128 == 0, -3e37, 0)
    c[:, 1536:2048] = np.where(n % 64 == 0, 0, 1)
    c[:, 2048:2064] = np.arange(16)
    return c


def tensors(nc, inputs):
    arrays, A = {}, {}
    for name in _INS:
        arrays["in_" + name] = np.ascontiguousarray(inputs[name])
    order = np.clip(255 - np.arange(383), -63, 128) + 63
    arrays["in_c_rel"] = np.ascontiguousarray(np.asarray(inputs["a_rel_bias"])[:, :, order])
    arrays["in_c_cst"] = constants()
    arrays["in_c_cst2"] = constants2()
    for name, a in arrays.items():
        A[name[3:]] = nc.dram_tensor(name, a.shape, mybir.dt.from_np(a.dtype), kind="ExternalInput").ap()
    rel = A["c_rel"]
    A["c_relw"] = [bass.AP(tensor=rel.tensor, offset=l * 6 * 383, ap=[[1, 128], [383, 6], [1, 256]])
                   for l in range(2)]
    return arrays, A


def kernel(**inputs):
    import concourse.bacc as _bacc
    from concourse.bass_utils import run_bass_kernel_spmd as _run

    nc = _bacc.Bacc("TRN2", target_bir_lowering=False, num_devices=1)
    arrays, A = tensors(nc, inputs)
    o = nc.dram_tensor("out_0", (1, 256, 1024), F32, kind="ExternalOutput").ap()
    build(nc, A, o, {})
    r = _run(nc, [arrays], core_ids=[0])
    return r.results[0]["out_0"]
```

```python
import numpy as np
import concourse.bass as bass
from concourse import mybir
from contextlib import ExitStack

F32 = mybir.dt.float32
U32 = mybir.dt.uint32
F32R = mybir.dt.float32r
ALU = mybir.AluOpType
ACT = mybir.ActivationFunctionType
AX = mybir.AxisListType
NEG = -1e30
LOW = -3e38
EPS = 1e-6


class Queue:

    def __init__(self, sem, chained):
        self.sem, self.chained, self.n, self.items = sem, chained, 0, []

    def __call__(self, fn, *after, free=False):
        if self.chained and not free and self.n:
            after = after + ((self.sem, self.n),)
        self.n += 1
        self.items.append((after, fn, self.sem, 1))
        return (self.sem, self.n)

    def wait(self, *after):
        self.items.append((after, None, None, 0))

    def dma(self, fn, sem, *after):
        self.items.append((after, fn, sem, 16))

    def now(self):
        return (self.sem, self.n)

    def emit(self, engine):
        seen = {}
        for after, fn, sem, by in self.items:
            for s, v in after:
                if v > seen.get(id(s), 0):
                    engine.wait_ge(s, v)
                    seen[id(s)] = v
            if fn is not None:
                fn(engine).then_inc(sem, by)


def build(nc, A, out, dbg, stop=None):
    ctx = ExitStack()
    with ctx:
        def sb(name, *shape, dt=F32):
            return ctx.enter_context(nc.sbuf_tensor(name, list(shape), dt))

        def sem(name):
            return ctx.enter_context(nc.semaphore(name))

        PE = Queue(sem("s_pe"), False)
        V = Queue(sem("s_v"), True)
        S = Queue(sem("s_s"), True)
        G = Queue(sem("s_g"), True)
        SP = Queue(sem("s_sp"), False)
        outsem = sem("s_out")

        PB = [ctx.enter_context(nc.psum_tensor(f"PB{i}", [128, 512], F32)) for i in range(8)]

        def mm(o, l, r, st=True, sp=True):
            return lambda e: e.matmul(o, l, r, start=st, stop=sp)

        def P(ops, *after):
            def run(e):
                for f in ops:
                    x = f(e)
                return x
            return PE(run, *after)

        def barrier():
            now = [q.now() for q in (PE, V, S, G)]
            for q in (PE, V, S, G):
                q.wait(*[t for t in now if t[0] is not q.sem or q is not PE])
            return now

        NS, SLOT, BIGN = 5, 2240, 18460
        with (nc.sbuf_tensor("RAW", [128, NS * SLOT], F32) as RAW, nc.sbuf_tensor("HTF", [128, 8192], F32) as HTF,
              nc.sbuf_tensor("BIG", [128, BIGN], F32) as BIG, nc.sbuf_tensor("HIF", [128, NS * SLOT], F32) as HIF):
            pass
        LOWS = sb("LOWS", 128, NS * SLOT, dt=F32R)
        HTR = sb("HTR", 128, 8192, dt=F32R)
        BIGR = sb("BIGR", 128, BIGN, dt=F32R)
        HIGH = sb("HIGH", 128, NS * SLOT, dt=F32R)
        HTH = HTR[:, 0:4096].rearrange("p (k t) -> p k t", k=8)
        HTL = HTR[:, 4096:8192].rearrange("p (k t) -> p k t", k=8)
        X = sb("X", 128, 2, 1024)
        CST = sb("CST", 128, 768)
        IDENT, J, J8 = CST[:, 0:128], CST[:, 128:256], CST[:, 256:384]
        ROPE = CST[:, 384:768].rearrange("p (b n) -> p b n", b=2)
        COLS = sb("COLS", 128, 256)
        MODC = sb("MODC", 128, 64)
        CT = sb("CT", 128, 16)
        SM = sb("SM", 128, 256)
        ONES = sb("ONES", 128, 128)
        HALF = sb("HALF", 1, 128)
        NROW = sb("NROW", 1, 64)

        class Region:

            def __init__(self, base, at, end):
                self.base, self.at, self.end = base, at, end

            def __call__(self, *shape, parts=128):
                n = int(np.prod(shape))
                assert self.at + n <= self.end, (self.at, n, self.end)
                self.at += n
                return shaped(self.base[0:parts, self.at - n:self.at], shape)

        def shaped(v, shape):
            names = "abcd"[:len(shape)]
            if len(shape) > 1:
                v = v.rearrange("p (" + " ".join(names) + ") -> p " + " ".join(names),
                                **{k: s for k, s in zip(names[:-1], shape)})
            return v

        NX = NS + 2
        XAT = BIGN - 2 * SLOT * 2
        MEM = [(RAW, HIGH, LOWS, i * SLOT, i * SLOT) for i in range(NS)] + \
            [(BIG, BIGR, BIGR, XAT + i * SLOT, XAT + (2 + i) * SLOT) for i in range(2)]
        slot_sem = [sem(f"s_w{i}") for i in range(NX)]
        slot_n, last = [0] * NX, [None] * NX
        tiles, extra = [], {}
        at = {"load": 0, "high": 0, "low": 0, "use": 0}

        class Tile:
            def __init__(self, n, src, shape, split, wide):
                some = range(NX if wide else NS)
                i = min(some, key=lambda i: -1 if last[i] is None else last[i].n)
                self.n, self.i, self.src, self.split, self.released = n, i, src, split, None
                self.before, last[i] = last[i], self
                self.sem, self.wide = slot_sem[i], wide
                self.size = int(np.prod(shape))
                assert self.size <= SLOT
                raw, high, low, a, c = MEM[i]
                self.raw, self.h, self.l = (shaped(m[:, x:x + self.size], shape)
                                            for m, x in ((raw, a), (high, c), (low, a)))

            def free(self, *tokens):
                self.released = tokens
                loads()

        def plan(src, *shape, split=True, wide=False):
            tiles.append(Tile(len(tiles), src, shape, split, wide))

        def loads():
            while at["load"] < len(tiles):
                t = tiles[at["load"]]
                after = ()
                if t.before is not None:
                    if t.before.released is None:
                        return
                    after = t.before.released
                if t.i >= NS:
                    if t.wide not in extra:
                        return
                    after = after + extra[t.wide]
                SP.dma((lambda t: lambda e: e.dma_start(t.raw, t.src))(t), t.sem, *after)
                slot_n[t.i] += 16
                t.arrived = (t.sem, slot_n[t.i])
                at["load"] += 1

        def need(ahead=1):
            n = at["use"]
            at["use"] += 1
            while at["high"] < min(n + 2 + ahead, len(tiles)) and at["high"] < at["load"]:
                t = tiles[at["high"]]
                if t.split:
                    t.high = S((lambda t: lambda e: e.activation(t.h, t.raw, ACT.Copy))(t), t.arrived, free=True)
                at["high"] += 1
            while at["low"] < min(n + 1 + ahead, len(tiles)) and at["low"] < at["high"]:
                t = tiles[at["low"]]
                t.ready = t.arrived
                if t.split:
                    t.ready = V((lambda t: lambda e: e.tensor_tensor(t.l, t.raw, t.h.bitcast(F32), ALU.subtract))(t),
                                t.high, free=True)
                at["low"] += 1
            assert at["low"] > n, n
            return tiles[n]

        def mm3(o, ls, rs, st=True, sp=True):
            ops = []
            for k, ((lh, ll), (rh, rl)) in enumerate(zip(ls, rs)):
                f, z = st and k == 0, sp and k == len(ls) - 1
                ops += [mm(o, lh, rh, f, False), mm(o, lh, rl, False, False), mm(o, ll, rh, False, z)]
            return ops

        once = {}

        def load_once(name, dst, src, *after):
            if name not in once:
                once[name] = [sem("s_" + name), 0]
            s = once[name]
            s[1] += 16
            SP.dma(lambda e: e.dma_start(dst, src), s[0], *after)
            return (s[0], s[1])

        def dump(name, view, *after):
            if name in dbg:
                SP.dma(lambda e: e.dma_start(dbg[name], view), outsem, *after)
                dumped[0] += 16
                for q in (PE, V, S, G):
                    q.wait((outsem, dumped[0]))

        dumped = [0]

        ROWS, ROWS2 = BIG[:, 0:128], BIG[:, 128:256]
        load_once("cst", CST[:, 0:768], A["c_cst"])
        rows = [("ffn1_norm", 16), ("mix_norm", 16), ("ffn2_norm", 16), ("norm1_g_2", 8), ("norm2_g_2", 8),
                ("ml_norm_g_2", 4), ("gla_norm_g_2", 4), ("c_q_norm", 6), ("c_kv_norm", 4),
                ("ml_conv_w_2", 24), ("gla_alpha_b_2", 4)]
        COL = {}
        r = 0
        for name, n in rows:
            src = A[name]
            nd = len(src.shape)
            if nd == 1:
                v = src.rearrange("(a p) -> a p", p=128)
            elif nd == 2:
                v = src.rearrange("l (a p) -> (l a) p", p=128)
            else:
                v = src.rearrange("l k (a p) -> (l k a) p", p=128)
            load_once("cst", ROWS[r:r + n, :], v)
            COL[name] = r
            r += n
        nrow = r
        load_once("cst", ROWS2[0:48, :], A["b_mod_2"].rearrange("l (a p) -> (l a) p", p=128))
        load_once("cst", ROWS2[48:56, :], A["c_2"].rearrange("l (a p) -> (l a) p", p=128))
        cst = load_once("cst", ROWS2[56:64, :], A["c_ctx_2"].rearrange("(a p) -> a p", p=128))
        xin = load_once("x", X[:, :, :], A["x"].rearrange("o (b p) n -> p (o b) n", p=128))
        V(lambda e: e.memset(ONES[:, :], 1.0), free=True)
        V(lambda e: e.memset(HALF[:, :], 0.0), free=True)
        V(lambda e: e.memset(HALF[:, 0:64], 1.0))
        kv = V(lambda e: e.memset(NROW[:, :], NEG), free=True)
        P([lambda e: e.transpose(PB[0][:, 0:nrow], ROWS[0:nrow, :], IDENT[0:nrow, 0:nrow])], cst)
        t = P([lambda e: e.transpose(PB[1][:, 0:64], ROWS2[0:64, :], IDENT[0:64, 0:64])])
        V(lambda e: e.tensor_copy(COLS[:, 0:nrow], PB[0][:, 0:nrow]), t, cst, kv)
        t = V(lambda e: e.tensor_copy(COLS[:, 128:192], PB[1][:, 0:64]), xin)
        S.wait(cst, xin)
        ts = S(lambda e: e.activation(COLS[:, 192:208], COLS[:, 176:192], ACT.Silu), t)
        V(lambda e: e.tensor_copy(CT[:, :], COLS[:, 192:208]), ts)
        COND = CT[:, :].rearrange("p (w k) -> p w k", w=2)

        def col(name, i):
            c = COL[name] + i
            return COLS[:, c:c + 1]

        def rstd(views, n, dst, junk, *after):
            for i, v in enumerate(views):
                t = S((lambda v, i: lambda e: e.activation(junk[:, 0:n], v, ACT.Square,
                                                          accum_out=dst[:, i:i + 1]))(v, i), *after)
            k = len(views)
            V(lambda e: e.tensor_scalar(dst[:, 0:k], dst[:, 0:k], 1.0 / n, EPS, ALU.mult, ALU.add), t)
            t = V(lambda e: e.reciprocal(dst[:, 0:k], dst[:, 0:k]))
            t = S(lambda e: e.activation(dst[:, 0:k], dst[:, 0:k], ACT.Sqrt), t)
            return t

        def transposed(src, gain, toff=0, shift=None, banks=(4, 5, 6, 7), after=()):
            tok = None
            for j in range(4):
                bk = PB[banks[j]]
                tp = P([(lambda j, k, b, bk: lambda e: e.transpose(
                    bk[:, k * 256 + b * 128:k * 256 + b * 128 + 128],
                    src[:, b, (2 * j + k) * 128:(2 * j + k + 1) * 128], IDENT))(j, k, b, bk)
                    for k in range(2) for b in range(2)], *after)
                for k in range(2):
                    kc = 2 * j + k
                    hd, ld = HTH[:, kc, toff:toff + 256], HTL[:, kc, toff:toff + 256]
                    ps = bk[:, k * 256:k * 256 + 256]
                    g = 1.0 if gain is None else gain(kc)
                    if shift is None:
                        th = S((lambda hd, ps, g: lambda e: e.activation(hd, ps, ACT.Copy, scale=g))(hd, ps, g),
                               tp, *after, free=True)
                    else:
                        y = HTF[:, 4096 + kc * 512 + toff:4096 + kc * 512 + toff + 256]
                        V((lambda y, ps, kc, g: lambda e: e.tensor_scalar(y, ps, g, shift(kc), ALU.mult,
                                                                         ALU.add))(y, ps, kc, g), tp, free=True)
                        V((lambda y, hd: lambda e: e.tensor_copy(hd, y))(y, hd))
                        tok = V((lambda y, hd, ld: lambda e: e.tensor_tensor(ld, y, hd.bitcast(F32),
                                                                            ALU.subtract))(y, hd, ld))
                if shift is None:
                    for k in range(2):
                        kc = 2 * j + k
                        hd, ld = HTH[:, kc, toff:toff + 256], HTL[:, kc, toff:toff + 256]
                        ps = bk[:, k * 256:k * 256 + 256]
                        g = 1.0 if gain is None else gain(kc)
                        tok = V((lambda hd, ld, ps, g: lambda e: e.scalar_tensor_tensor(
                            ld, ps, g, hd.bitcast(F32), ALU.mult, ALU.subtract))(hd, ld, ps, g), th, free=True)
            return tok

        def normed(hn, src, *after):
            t = rstd([src[:, b, :] for b in range(2)], 1024, SM[:, 0:2],
                     HTF[:, 0:1024] if hn is src else hn.rearrange("p b n -> p (b n)"), *after)
            for b in range(2):
                t = V((lambda b: lambda e: e.tensor_scalar(hn[:, b, :], src[:, b, :], SM[:, b:b + 1], None,
                                                          ALU.mult))(b), t)
            return t

        def halves(src, dst_h, dst_l, *after):
            V(lambda e: e.tensor_copy(dst_h, src), *after)
            return V(lambda e: e.tensor_tensor(dst_l, src, dst_h.bitcast(F32), ALU.subtract))

        MODS = {(0, 1): 0, (0, 2): 6, (1, 1): 12, (1, 2): 18}

        def plan_ffn(l, which):
            wg, wu, wd = (A[f"ffn{which}_w_{x}"][l] for x in ("gate", "up", "down"))
            wg = wg.rearrange("(k p) n -> p k n", p=128)
            wu = wu.rearrange("(k p) n -> p k n", p=128)
            wd = wd.rearrange("(f p) n -> p f n", p=128)
            wm = A["w_mod_2"][0].rearrange("(k p) n -> p k n", p=128)
            for j in range(11):
                phase = (l, which) if j > 1 else False
                plan(wg[:, :, j * 256:(j + 1) * 256], 8, 256, wide=phase)
                plan(wu[:, :, j * 256:(j + 1) * 256], 8, 256, wide=phase)
                if 3 <= j < 9:
                    m = MODS[l, which] + j - 3
                    plan(wm[:, :, m * 256:(m + 1) * 256], 8, 256, split=False, wide=phase)
                plan(wd[:, 2 * j:2 * j + 2, :], 2, 1024, wide=phase)

        def modulation(t, m, w, acc):
            a = acc[:, w, :]
            V(lambda e: e.tensor_scalar(a, t.raw[:, 0, :], COND[:, w, 0:1], None, ALU.mult), t.ready, PE.now())
            for k in range(1, 8):
                V((lambda k: lambda e: e.scalar_tensor_tensor(a, t.raw[:, k, :], COND[:, w, k:k + 1], a,
                                                             ALU.mult, ALU.add))(k))
            if w == (m < 8):
                t.free(V.now())
            return [mm(PB[7][:, 2 * w + h:2 * w + h + 1], a[:, h * 128:(h + 1) * 128], ONES[:, 0:1])
                    for h in range(2)], V.now(), m, w

        def modulation_out(ops, tv, m, w):
            tk = P(ops, tv)
            V(lambda e: e.tensor_tensor(MODC[:, 48 * w + 2 * m:48 * w + 2 * m + 2], PB[7][:, 2 * w:2 * w + 2],
                                        COLS[:, 128 + 2 * m:130 + 2 * m], ALU.add), tk)

        def ffn(l, which):
            reg = Region(BIG, 0, BIGN)
            hn, sg, pr, acc = reg(2, 1024), reg(3, 256), reg(3, 256), reg(2, 256)
            ah = Region(BIGR, reg.at, BIGN)(3, 256)
            al = Region(BIGR, reg.at + 768, BIGN)(3, 256)
            name = f"ffn{which}_norm"
            assert reg.at + 1536 <= XAT
            now = barrier()
            extra[l, which] = tuple(now)
            loads()
            t = normed(hn, X, V.now())
            ready = transposed(hn, lambda kc: col(name, l * 8 + kc), after=(t,))
            ta, tdown, td = {}, {}, {}
            AH = 2
            pend = None

            def down(f):
                w = td[f // 2]
                c = f % 3
                ops = []
                for b in range(2):
                    s = slice(b * 128, (b + 1) * 128)
                    for h in range(2):
                        q = slice(h * 512, (h + 1) * 512)
                        ops += mm3(PB[2 * b + h][:, :], [(ah[:, c, s], al[:, c, s])],
                                   [(w.h[:, f % 2, q], w.l[:, f % 2, q])], f == 0, f == 21)
                tdown[f] = P(ops, ta[f], w.ready)
                if f % 2:
                    w.free(tdown[f])

            tg = {}
            for f in range(22):
                c = f % 3
                if f % 2 == 0:
                    ws = [need(AH), need(AH)]
                bank = PB[4 + c]
                for s_ in range(2):
                    w = ws[s_]
                    q = slice((f % 2) * 128, (f % 2 + 1) * 128)
                    tk = P(mm3(bank[:, s_ * 256:(s_ + 1) * 256], [(w.h[:, k, q], w.l[:, k, q]) for k in range(8)],
                               [(HTH[:, k, 0:256], HTL[:, k, 0:256]) for k in range(8)]),
                           ready, w.ready, *([tg[f - 3]] if f >= 3 else []))
                    if f % 2:
                        w.free(tk)
                ts = S((lambda c, bank: lambda e: e.activation(sg[:, c, :], bank[:, 0:256], ACT.Silu))(c, bank),
                       tk, *([ta[f - 3]] if f >= 3 else []), free=True)
                tg[f] = V((lambda c, bank: lambda e: e.tensor_tensor(pr[:, c, :], bank[:, 256:512], sg[:, c, :],
                                                                    ALU.mult))(c, bank), ts)
                ta[f] = halves(pr[:, c, :], ah[:, c, :], al[:, c, :], *([tdown[f - 3]] if f >= 3 else []))
                if f >= 1:
                    down(f - 1)
                if pend is not None:
                    modulation_out(*pend)
                    pend = None
                if f % 2 == 0:
                    j = f // 2
                    if 3 <= j < 9:
                        tm, m = need(AH), MODS[l, which] + j - 3
                        pend = modulation(tm, m, 0, acc)
                    td[j] = need(AH)
                elif 3 <= f // 2 < 9 and m < 8:
                    pend = modulation(tm, m, 1, acc)
            down(21)
            for b in range(2):
                for h in range(2):
                    xv = X[:, b, h * 512:(h + 1) * 512]
                    V((lambda b, h, xv: lambda e: e.scalar_tensor_tensor(xv, PB[2 * b + h][:, :], 0.5, xv,
                                                                         ALU.mult, ALU.add))(b, h, xv),
                      tdown[21])

        def rope(x, nh, d, b, off, t1, t2):
            h = d // 2
            C = ROPE[:, b, off:off + d].unsqueeze(1).broadcast_to([128, nh, d])
            S1 = ROPE[:, b, off + d:off + d + h].unsqueeze(1).broadcast_to([128, nh, h])
            S2 = ROPE[:, b, off + d + h:off + 2 * d].unsqueeze(1).broadcast_to([128, nh, h])
            t1 = t1[:, 0:nh * d].rearrange("p (n d) -> p n d", d=d)
            t2 = t2[:, 0:nh * d].rearrange("p (n d) -> p n d", d=d)
            V(lambda e: e.tensor_tensor(t1, x, C, ALU.mult))
            V(lambda e: e.tensor_tensor(t2[:, :, 0:h], x[:, :, h:d], S1, ALU.mult), free=True)
            V(lambda e: e.tensor_tensor(t2[:, :, h:d], x[:, :, 0:h], S2, ALU.mult), free=True)
            return V(lambda e: e.tensor_tensor(x, t1, t2, ALU.add))

        def transposes(jobs, banks, after):
            toks = []
            bank_free = {}
            for g in range(0, len(jobs), 4):
                bk = banks[(g // 4) % len(banks)]
                part = jobs[g:g + 4]
                ops = []
                for i, (dst, src) in enumerate(part):
                    m, n = dst.shape[0], src.shape[0]
                    ops.append((lambda i, src, m, n, bk: lambda e: e.transpose(
                        PB[bk][0:m, i * 128:i * 128 + n], src, IDENT[0:n, 0:n]))(i, src, m, n, bk))
                tp = P(ops, *after, *bank_free.get(bk, ()))
                got = []
                for i, (dst, src) in enumerate(part):
                    m, n = dst.shape[0], src.shape[0]
                    q = (S, V)[(g // 4) % 2]
                    if q is S:
                        fn = (lambda i, dst, m, n, bk: lambda e: e.activation(
                            dst, PB[bk][0:m, i * 128:i * 128 + n], ACT.Copy))(i, dst, m, n, bk)
                    else:
                        fn = (lambda i, dst, m, n, bk: lambda e: e.tensor_copy(
                            dst, PB[bk][0:m, i * 128:i * 128 + n]))(i, dst, m, n, bk)
                    got.append(q(fn, tp, *after, free=True))
                bank_free[bk] = tuple(got)
                toks += got
            return (S.now(), V.now())

        def attend(units, sc, pb, pt, rs, ready):
            n = len(units)
            t1, tmx, tex, ttr, tev, to, tdst = {}, {}, {}, {}, {}, {}, {}
            for i in range(n + 3):
                if i < n:
                    q, k, extra, vs, dst, scale = units[i]
                    nk = k.shape[-1]
                    ps = PB[i % 4]
                    ops = [mm(ps[:, 0:nk], q, k, True, not extra)]
                    for x, (a, b_, l_, r_) in enumerate(extra):
                        ops.append(mm(ps[:, a:b_], l_, r_, False, x == len(extra) - 1))
                    t1[i] = P(ops, *ready, *([tex[i - 4]] if i >= 4 else []))
                    m = rs[:, (i % 4) * 4:(i % 4) * 4 + 4]
                    V((lambda ps, m, nk: lambda e: e.tensor_reduce(m[:, 0:1], ps[:, 0:nk], AX.X, ALU.max,
                                                                  negate=True))(ps, m, nk), t1[i],
                      *([tex[i - 4]] if i >= 4 else []))
                    tmx[i] = V((lambda m, scale: lambda e: e.tensor_scalar(m[:, 1:2], m[:, 0:1], scale, None,
                                                                          ALU.mult))(m, scale))
                    tex[i] = S((lambda ps, m, nk, i, scale: lambda e: e.activation(
                        pb[:, i % 4, 0:nk], ps[:, 0:nk], ACT.Exp, bias=m[:, 1:2], scale=scale,
                        accum_out=m[:, 2:3]))(ps, m, nk, i, scale), tmx[i],
                        *([ttr[i - 4], tdst[i - 4]] if i >= 4 else []))
                u = i - 2
                if 0 <= u < n:
                    nb = units[u][1].shape[-1] // 128
                    bk = PB[4 + u % 2]
                    ops = [(lambda kb, bk, u: lambda e: e.transpose(bk[:, kb * 128:(kb + 1) * 128],
                                                                  pb[:, u % 4, kb * 128:(kb + 1) * 128],
                                                                  IDENT))(kb, bk, u) for kb in range(nb)]
                    ttr[u] = P(ops, tex[u], *([tev[u - 2]] if u >= 2 else []))
                    q_ = (S, V)[u % 2]
                    if q_ is S:
                        fn = (lambda bk, u, nb: lambda e: e.activation(pt[:, u % 2, 0:nb * 128], bk[:, 0:nb * 128],
                                                                      ACT.Copy))(bk, u, nb)
                    else:
                        fn = (lambda bk, u, nb: lambda e: e.tensor_copy(pt[:, u % 2, 0:nb * 128],
                                                                       bk[:, 0:nb * 128]))(bk, u, nb)
                    tev[u] = q_(fn, ttr[u], *([to[u - 2]] if u >= 2 else []))
                u = i - 3
                if 0 <= u < n:
                    vs, dst = units[u][3], units[u][4]
                    po = PB[6 + u % 2][:, 0:64]
                    ops = [mm(po, pt[:, u % 2, kb * 128:(kb + 1) * 128], v, kb == 0, kb == len(vs) - 1)
                           for kb, v in enumerate(vs)]
                    to[u] = P(ops, tev[u], *([tdst[u - 2]] if u >= 2 else []))
                    m = rs[:, (u % 4) * 4:(u % 4) * 4 + 4]
                    V((lambda m: lambda e: e.reciprocal(m[:, 3:4], m[:, 2:3]))(m), tex[u])
                    tdst[u] = V((lambda m, dst, po: lambda e: e.tensor_scalar(dst, po, m[:, 3:4], None,
                                                                            ALU.mult))(m, dst, po), to[u])
            return V.now()

        def plan_hybrid(l):
            wv = A["w_in"][l].rearrange("(k p) n -> p k n", p=128)
            for j in range(11):
                plan(wv[:, :, j * 280:(j + 1) * 280], 8, 280)
            plan(A["c_w_uq"][l].rearrange("(k p) n -> p k n", p=128), 3, 480)
            plan(A["c_w_ukv"][l].rearrange("(k p) n -> p k n", p=128), 2, 640)
            plan_out(A["w_out"][l])

        def hybrid(l):
            c = Region(BIG, 0, BIGN)
            ht = Region(HTF, 0, 8192)
            H = c(2, 3080)
            hn = c(2, 1024)
            barrier()
            t = normed(hn, X, V.now())
            ready = transposed(hn, lambda kc: col("mix_norm", l * 8 + kc), after=(t,))
            W = 280
            prev = {}
            for j in range(11):
                w = need()
                for b in range(2):
                    n = 2 * j + b
                    bank = PB[n % 4]
                    s = slice(b * 128, (b + 1) * 128)
                    tk = P(mm3(bank[:, 0:W], [(HTH[:, k, s], HTL[:, k, s]) for k in range(8)],
                               [(w.h[:, k, :], w.l[:, k, :]) for k in range(8)]),
                           ready, w.ready, *([prev[n - 4]] if n >= 4 else []))
                    dst = H[:, b, j * W:(j + 1) * W]
                    if n % 2:
                        prev[n] = V((lambda dst, bank: lambda e: e.tensor_copy(dst, bank[:, 0:W]))(dst, bank), tk,
                                    free=True)
                    else:
                        prev[n] = S((lambda dst, bank: lambda e: e.activation(dst, bank[:, 0:W], ACT.Copy))(dst, bank),
                                    tk, free=True)
                w.free(tk)
            barrier()
            dump(f"H{l}", H, V.now(), S.now())
            O = hn
            WB = c(6, 256)
            lb = load_once("bias", WB, A["c_relw"][l], V.now(), PE.now())
            t1, t2 = ht(640), ht(640)
            for b in range(2):
                rope(H[:, b, 1152:1792].rearrange("p (n d) -> p n d", d=64), 10, 64, b, 0, t1, t2)
                rope(H[:, b, 2112:2400].rearrange("p (n d) -> p n d", d=32), 9, 32, b, 128, t1, t2)
                rope(H[:, b, 3048:3080].rearrange("p (n d) -> p n d", d=32), 1, 32, b, 128, t1, t2)
            lt = Region(BIG, c.at, c.at + 2560)
            LTH = Region(BIGR, c.at, BIGN)(5, 256)
            LTL = Region(BIGR, c.at + 1280, BIGN)(5, 256)
            c.at += 2560
            ln = c(2, 640)
            rstd([H[:, b, 2408:2792] for b in range(2)], 384, SM[:, 0:2], t1, V.now())
            rstd([H[:, b, 2792:3048] for b in range(2)], 256, SM[:, 2:4], t1, V.now())
            for b in range(2):
                V((lambda b: lambda e: e.tensor_scalar(ln[:, b, 0:384], H[:, b, 2408:2792], SM[:, b:b + 1], None,
                                                      ALU.mult))(b), S.now())
                V((lambda b: lambda e: e.tensor_scalar(ln[:, b, 384:640], H[:, b, 2792:3048], SM[:, 2 + b:3 + b],
                                                      None, ALU.mult))(b))
            tl = V.now()
            for k in range(5):
                g = col("c_q_norm", l * 3 + k) if k < 3 else col("c_kv_norm", l * 2 + k - 3)
                tp = P([(lambda k, b: lambda e: e.transpose(PB[k][:, b * 128:(b + 1) * 128],
                                                           ln[:, b, k * 128:(k + 1) * 128], IDENT))(k, b)
                        for b in range(2)], tl)
                V((lambda k, g: lambda e: e.tensor_scalar(LTH[:, k, :], PB[k][:, 0:256], g, None, ALU.mult))(k, g), tp)
                V((lambda k, g: lambda e: e.scalar_tensor_tensor(LTL[:, k, :], PB[k][:, 0:256], g,
                                                                LTH[:, k, :].bitcast(F32), ALU.mult,
                                                                ALU.subtract))(k, g))
            QC = c(2, 480)
            KV = c(2, 640)
            wq = need()
            wk = need()
            barrier()
            tq = []
            for b in range(2):
                s = slice(b * 128, (b + 1) * 128)
                tk = P(mm3(PB[b][:, 0:480], [(LTH[:, k, s], LTL[:, k, s]) for k in range(3)],
                           [(wq.h[:, k, :], wq.l[:, k, :]) for k in range(3)]), wq.ready)
                V((lambda b: lambda e: e.tensor_copy(QC[:, b, :], PB[b][:, 0:480]))(b), tk)
                for h in range(2):
                    q = slice(h * 320, (h + 1) * 320)
                    tk2 = P(mm3(PB[2 + 2 * b + h][:, 0:320], [(LTH[:, 3 + k, s], LTL[:, 3 + k, s]) for k in range(2)],
                                [(wk.h[:, k, q], wk.l[:, k, q]) for k in range(2)]), wk.ready)
                    S((lambda b, h: lambda e: e.activation(KV[:, b, h * 320:(h + 1) * 320],
                                                          PB[2 + 2 * b + h][:, 0:320], ACT.Copy))(b, h), tk2)
            wq.free(tk)
            wk.free(tk2)
            QV = QC.rearrange("p b (h d) -> p b h d", d=96)
            KVV = KV.rearrange("p b (h d) -> p b h d", d=128)
            KC = c(2, 480)
            KCV = KC.rearrange("p b (h d) -> p b h d", d=96)
            for b in range(2):
                rope(QV[:, b, :, 64:96], 5, 32, b, 128, t1, t2)
                G((lambda b: lambda e: e.tensor_copy(KCV[:, b, :, 0:64], KVV[:, b, :, 0:64]))(b), S.now())
                G((lambda b: lambda e: e.tensor_copy(
                    KCV[:, b, :, 64:96], H[:, b, 3048:3080].unsqueeze(1).broadcast_to([128, 5, 32])))(b), tl)
            IK = t1[:, 0:256].rearrange("p (b r d) -> p b r d", b=2, r=4)
            for b in range(2):
                t = V((lambda b: lambda e: e.tensor_copy(
                    IK[:, b, :, :], H[:, b, 2368:2400].unsqueeze(1).broadcast_to([128, 4, 32])))(b))
            barrier()
            AQ, AK, BQ, BK = ht(3, 256), ht(3, 256), ht(3, 256), ht(3, 256)
            CQ, CK = ht(5, 256), ht(5, 256)
            IQT, IKT = c(2, 256), c(256)
            jobs = []
            for b in range(2):
                s = slice(b * 128, (b + 1) * 128)
                for k in range(2):
                    jobs.append((IQT[:, k, s], H[:, b, 2112 + k * 128:2112 + (k + 1) * 128]))
                jobs.append((IKT[:, s], IK[:, b, :, :].rearrange("p r d -> p (r d)")))
            for dst, base, w in ((AQ, 0, 384), (AK, 384, 384), (BQ, 1152, 320), (BK, 1472, 320)):
                for k in range(3):
                    for b in range(2):
                        m = min(128, w - k * 128)
                        jobs.append((dst[0:m, k, b * 128:(b + 1) * 128],
                                     H[:, b, base + k * 128:base + k * 128 + m]))
            for h in range(5):
                for b in range(2):
                    jobs.append((CQ[0:96, h, b * 128:(b + 1) * 128], QC[:, b, h * 96:(h + 1) * 96]))
                    jobs.append((CK[0:96, h, b * 128:(b + 1) * 128], KC[:, b, h * 96:(h + 1) * 96]))
            transposes(jobs, list(range(8)), (V.now(),))
            barrier()
            SCR = lt(2, 256)
            WRK = lt(2, 256)
            TMP = lt(256)
            SEL = lt(2, 256)
            WI = SM[:, 16:32].rearrange("p (b h) -> p b h", b=2)
            t = V(lambda e: e.tensor_scalar(WI, H[:, :, 2400:2408], float(8 ** -0.5 * 32 ** -0.5), None, ALU.mult))
            for b in range(2):
                nk = 128 * (b + 1)
                toks = []
                for h in range(8):
                    r0 = 32 * (h % 4)
                    toks.append(P([mm(PB[h][:, 0:nk], IQT[r0:r0 + 32, h // 4, b * 128:(b + 1) * 128],
                                      IKT[r0:r0 + 32, 0:nk])], V.now()))
                for h in range(8):
                    dst = SCR[:, b, 0:nk]
                    if h == 0:
                        V((lambda dst, nk, b: lambda e: e.tensor_scalar(
                            dst, PB[0][:, 0:nk], 0.0, WI[:, b, 0:1], ALU.max, ALU.mult))(dst, nk, b), toks[0])
                    else:
                        V((lambda h, nk, b: lambda e: e.tensor_scalar(
                            TMP[:, 0:nk], PB[h][:, 0:nk], 0.0, WI[:, b, h:h + 1], ALU.max, ALU.mult))(h, nk, b),
                          toks[h])
                        V((lambda dst, nk: lambda e: e.tensor_tensor(dst, dst, TMP[:, 0:nk], ALU.add))(dst, nk))
                V((lambda b, nk: lambda e: e.memset(SCR[0:64, b, nk - 64:nk], NEG))(b, nk))
                m8 = SM[:, 32:40]
                for r_ in range(8):
                    src = (SCR if r_ == 0 else WRK)[:, b, 0:nk]
                    V((lambda src: lambda e: e.max(m8, src))(src))
                    V((lambda src, b, nk: lambda e: e.match_replace(WRK[:, b, 0:nk], m8, src, LOW))(src, b, nk))
                V((lambda b, nk: lambda e: e.tensor_scalar(SEL[:, b, 0:nk], WRK[:, b, 0:nk], -2e38, NEG,
                                                          ALU.is_gt, ALU.mult))(b, nk))
            barrier()
            pb = ln.rearrange("p b n -> p (b n)")[:, 0:1024].rearrange("p (a n) -> p a n", a=4)
            pt = KC.rearrange("p b n -> p (b n)")[:, 0:512].rearrange("p (a n) -> p a n", a=2)
            rs = SM[:, 48:64]
            units = []
            for h in range(6):
                for b in range(2):
                    nk = 128 * (b + 1)
                    r0 = 64 * (h % 2)
                    vs = [H[:, kb, 768 + h * 64:768 + (h + 1) * 64] for kb in range(b + 1)]
                    units.append((AQ[r0:r0 + 64, h // 2, b * 128:(b + 1) * 128], AK[r0:r0 + 64, h // 2, 0:nk],
                                  [(0, nk, J8, WB[:, h, 128 * (1 - b):256]), (nk - 64, nk, HALF[:, :], NROW[:, :])],
                                  vs, O[:, b, h * 64:(h + 1) * 64], 0.125))
            for h in range(5):
                for b in range(2):
                    nk = 128 * (b + 1)
                    r0 = 64 * (h % 2)
                    vs = [H[:, kb, 1792 + h * 64:1792 + (h + 1) * 64] for kb in range(b + 1)]
                    units.append((BQ[r0:r0 + 64, h // 2, b * 128:(b + 1) * 128], BK[r0:r0 + 64, h // 2, 0:nk],
                                  [(0, nk, IDENT, SEL[:, b, 0:nk])],
                                  vs, O[:, b, 384 + h * 64:384 + (h + 1) * 64], 0.125))
            for h in range(5):
                for b in range(2):
                    nk = 128 * (b + 1)
                    vs = [KVV[:, kb, h, 64:128] for kb in range(b + 1)]
                    units.append((CQ[0:96, h, b * 128:(b + 1) * 128], CK[0:96, h, 0:nk],
                                  [(nk - 64, nk, HALF[:, :], NROW[:, :])],
                                  vs, O[:, b, 704 + h * 64:704 + (h + 1) * 64], float(96 ** -0.5)))
            attend(units, None, pb, pt, rs, [lb])
            barrier()
            dump(f"O{l}", O, V.now())
            project_out(O, None)
            dump(f"X{l}", X[:, :, :], V.now())

        def plan_out(w):
            wv = w.rearrange("(k p) n -> p k n", p=128)
            for j in range(4):
                plan(wv[:, :, j * 256:(j + 1) * 256], 8, 256)

        def project_out(O, gate, gains=None):
            ready = transposed(O, gains, banks=(0, 1, 2, 3))
            n = 0
            prev = {}
            for j in range(4):
                w = need()
                for b in range(2):
                    bank = PB[4 + n % 4]
                    s = slice(b * 128, (b + 1) * 128)
                    tk = P(mm3(bank[:, 0:256], [(HTH[:, k, s], HTL[:, k, s]) for k in range(8)],
                               [(w.h[:, k, :], w.l[:, k, :]) for k in range(8)]),
                           ready, w.ready, *([prev[n - 4]] if n >= 4 else []))
                    xv = X[:, b, j * 256:(j + 1) * 256]
                    if gate is not None:
                        gv = gate[:, j * 256:(j + 1) * 256]
                        V((lambda bank, gv: lambda e: e.tensor_tensor(bank[:, 0:256], bank[:, 0:256], gv,
                                                                     ALU.mult))(bank, gv), tk)
                    prev[n] = V((lambda bank, xv: lambda e: e.tensor_tensor(xv, xv, bank[:, 0:256],
                                                                          ALU.add))(bank, xv), tk)
                    n += 1
                w.free(tk)

        def second():
            barrier()
            reg = Region(BIG, 0, BIGN)
            G1, G2 = reg(1024), reg(1024)
            at_a = reg.at
            hn = reg(2, 1024)
            reg.at = at_a + 3072
            CX = Region(BIG, reg.at, BIGN)(2, 1024)
            FG = Region(BIG, reg.at + 2048, BIGN)(1024)
            now = V.now(), S.now(), PE.now(), G.now()
            c2 = load_once("c2", FG, A["final_norm"].partition_broadcast(128), *now)
            c2 = load_once("c2", CX, A["ctx_2"].rearrange("o (b p) n -> p (o b) n", p=128), *now)
            GA = SM[:, 160:208].rearrange("p (s k) -> p s k", s=6)
            for s, (sc, sh, name) in enumerate(((8, 0, "norm1_g_2"), (56, 48, "norm1_g_2"), (32, 24, "norm2_g_2"))):
                gn = COLS[:, COL[name]:COL[name] + 8]
                V((lambda s, sc, gn: lambda e: e.scalar_tensor_tensor(
                    GA[:, 2 * s, :], MODC[:, sc:sc + 8], 1.0, gn, ALU.add, ALU.mult))(s, sc, gn))
                V((lambda s, sh: lambda e: e.tensor_copy(GA[:, 2 * s + 1, :], MODC[:, sh:sh + 8]))(s, sh))
            V.wait(c2)
            S.wait(c2)
            t = normed(CX, CX, V.now())
            transposed(CX, lambda kc: GA[:, 2, kc:kc + 1], toff=256, shift=lambda kc: GA[:, 3, kc:kc + 1], after=(t,))
            tr = rstd([X[:, b, :] for b in range(2)], 1024, SM[:, 0:2], hn.rearrange("p b n -> p (b n)"), V.now())
            for b in range(2):
                V((lambda b: lambda e: e.scalar_tensor_tensor(X[:, b, :], X[:, b, :], SM[:, b:b + 1], FG,
                                                             ALU.mult, ALU.mult))(b), tr)
            dump("XN", X[:, :, :], V.now())
            t = normed(hn, X, V.now())
            ready = transposed(hn, lambda kc: GA[:, 0, kc:kc + 1], shift=lambda kc: GA[:, 1, kc:kc + 1],
                               banks=(0, 1, 2, 3), after=(t,))
            for g_, c0 in ((G1, 16), (G2, 40)):
                dg = hn.rearrange("p b n -> p (b n)")[:, 0:1024]
                td_ = V((lambda c0, dg: lambda e: e.tensor_tensor(
                    dg.rearrange("p (k t) -> p k t", t=128), IDENT.unsqueeze(1).broadcast_to([128, 8, 128]),
                    MODC[:, c0:c0 + 8].unsqueeze(2).broadcast_to([128, 8, 128]), ALU.mult))(c0, dg), PE.now())
                for h in range(2):
                    tk = P([mm(PB[h][:, :], ONES[:, :], dg[:, h * 512:(h + 1) * 512])], td_)
                    V((lambda g_, h: lambda e: e.tensor_copy(g_[:, h * 512:(h + 1) * 512], PB[h][:, :]))(g_, h), tk)
            QR, KR = Region(BIG, at_a, at_a + 3072)(4, 256), Region(BIG, at_a + 1024, at_a + 3072)(4, 512)
            QT, KT, KTOK = reg(4, 256), reg(4, 512), reg(4, 512)
            VA = reg(4, 4, 129)
            MO, GV, GR, GQ, GK = reg(2, 512), reg(4, 512), reg(2, 512), reg(2, 256), reg(2, 512)
            GLR = reg(512, parts=32)
            GT = SM[:, 0:64].rearrange("p (b g) -> p b g", b=4)
            barrier()
            V(lambda e: e.memset(VA[:, :, :, 128:129], 1.0))
            n = [0]
            prev = {}

            def project(prods, width, evac, arr, parts=128):
                m = n[0]
                bank = PB[m % 8]
                tk = P(mm3(bank[0:parts, 0:width], [p_[0] for p_ in prods], [p_[1] for p_ in prods]),
                       ready, arr, *([prev[m - 8]] if m >= 8 else []))
                q = (V, S)[m % 2]
                prev[m] = q(evac(q, bank[0:parts, 0:width]), tk, free=True)
                n[0] += 1
                return tk

            def copy_to(dst, scale=1.0):
                def evac(q, src):
                    if q is V:
                        return lambda e: e.tensor_scalar(dst, src, scale, None, ALU.mult)
                    return lambda e: e.activation(dst, src, ACT.Copy, scale=scale)
                return evac

            def features(w, c0, m, nt, dst, scale=1.0):
                return project([((w.h[:, k, c0:c0 + m], w.l[:, k, c0:c0 + m]), (HTH[:, k, 0:nt], HTL[:, k, 0:nt]))
                                for k in range(8)], nt, copy_to(dst, scale),
                               w.ready, parts=m)

            def tokens(w, c0, m, b, dst):
                s = slice(b * 128, (b + 1) * 128)
                return project([((HTH[:, k, s], HTL[:, k, s]), (w.h[:, k, c0:c0 + m], w.l[:, k, c0:c0 + m]))
                                for k in range(8)], m,
                               copy_to(dst) if len(dst.shape) == 2 else
                               (lambda q, src: copy_to(dst)(q, src.rearrange("p (h d) -> p h d", d=128))), w.ready)

            for j in range(2):
                w = need()
                for k in range(2):
                    tk = features(w, k * 128, 128, 256, QR[:, 2 * j + k, :])
                w.free(tk)
            for j in range(2):
                w = need()
                for k in range(2):
                    tk = features(w, k * 128, 128, 512, KR[:, 2 * j + k, :])
                w.free(tk)
            for j in range(2):
                w = need()
                for b in range(4):
                    tk = tokens(w, 0, 256, b, VA[:, b, 2 * j:2 * j + 2, 0:128])
                w.free(tk)
            for j in range(2):
                w = need()
                for b in range(2):
                    tk = tokens(w, 0, 256, b, MO[:, b, j * 256:(j + 1) * 256])
                w.free(tk)
            w = need()
            for b in range(4):
                tokens(w, 0, 16, b, GT[:, b, :])
            for k in range(2):
                tk = features(w, 16 + k * 128, 128, 256, GQ[:, k, :], 0.125)
            w.free(tk)
            w = need()
            for k in range(2):
                tk = features(w, k * 128, 128, 512, GK[:, k, :])
            w.free(tk)
            for j in range(2):
                w = need()
                for b in range(4):
                    tk = tokens(w, 0, 256, b, GV[:, b, j * 256:(j + 1) * 256])
                w.free(tk)
            w = need()
            for b in range(2):
                tk = tokens(w, 0, 280, b, GR[:, b, 0:280])
            w.free(tk)
            w = need()
            for b in range(2):
                tokens(w, 0, 232, b, GR[:, b, 280:512])
            tk = features(w, 232, 32, 512, GLR)
            w.free(tk)
            t = barrier()
            C2 = HTF[:, 6128:8192]
            c2 = load_once("c2", C2, A["c_cst2"], *t)
            MASK = C2[:, 0:256].rearrange("p (d t) -> p d t", d=2)
            GM = C2[:, 256:512].rearrange("p (d t) -> p d t", d=2)
            D0, D1, D64 = C2[0:8, 512:1024], C2[0:8, 1024:1536], C2[:, 1536:2048]
            V.wait(c2)
            PE.wait(c2)
            cw = COL["ml_conv_w_2"]
            for src, dst, h0, nt in ((QR, QT, 0, 256), (KR, KT, 4, 512)):
                for h in range(4):
                    w0, w1, w2 = (COLS[:, cw + 8 * j + h0 + h:cw + 8 * j + h0 + h + 1] for j in range(3))
                    u, y = src[:, h, :], dst[:, h, :]
                    V((lambda u, y, w1: lambda e: e.tensor_scalar(y, u, w1, None, ALU.mult))(u, y, w1))
                    parts = [(u[:, 0:256].rearrange("p (r t) -> p r t", t=64),
                              y[:, 0:256].rearrange("p (r t) -> p r t", t=64), 64)]
                    if nt == 512:
                        parts.append((u[:, 256:512].rearrange("p (r t) -> p r t", t=256),
                                      y[:, 256:512].rearrange("p (r t) -> p r t", t=256), 256))
                    for uu, yy, m in parts:
                        for wc, a_, b_ in ((w0, slice(1, m), slice(0, m - 1)), (w2, slice(0, m - 1), slice(1, m))):
                            V((lambda uu, yy, wc, a_, b_: lambda e: e.scalar_tensor_tensor(
                                yy[:, :, a_], uu[:, :, b_], wc, yy[:, :, a_], ALU.mult, ALU.add))(uu, yy, wc, a_, b_))
            ts = S(lambda e: e.activation(QT, QT, ACT.Silu), V.now())
            ts = S(lambda e: e.activation(KT, KT, ACT.Silu))
            V(lambda e: e.tensor_scalar(KT, KT, float(128 ** -0.5), None, ALU.mult), ts)
            ts = S(lambda e: e.activation(MO, MO, ACT.Sigmoid))
            ts = S(lambda e: e.activation(GR, GR, ACT.Silu))
            barrier()
            transposes([(KTOK[:, b, h * 128:(h + 1) * 128], KT[:, h, b * 128:(b + 1) * 128])
                        for b in range(4) for h in range(4)], list(range(8)), (V.now(),))
            tmp = Region(HTF, 0, 6128)
            GB = tmp(16)
            tb_ = load_once("gb", GB, A["ml_gate_b_2"][0].partition_broadcast(128), *t)
            GP = tmp(4, 4, 8)
            V(lambda e: e.tensor_tensor(GT, GT, GB.unsqueeze(1).broadcast_to([128, 4, 16]), ALU.add), tb_)
            V(lambda e: e.memset(GP, 0.0))
            for d in range(2):
                for q in range(2):
                    V((lambda d, q: lambda e: e.tensor_copy(GP[:, 2 * q + d, :, d * 4:d * 4 + 4],
                                                           GT[:, :, d * 8 + q * 4:d * 8 + q * 4 + 4]))(d, q))
            barrier()
            ORD = [[2, 3, 0, 1], [3, 2, 1, 0]]
            ops = []
            for q in range(2):
                for c in range(4):
                    o_ = PB[q][0:8, c * 128:(c + 1) * 128]
                    ops.append(mm(o_, GP[:, 2 * q, ORD[0][c], :], IDENT, True, False))
                    ops.append(mm(o_, GP[:, 2 * q + 1, ORD[1][c], :], J, False, True))
            tk = P(ops)
            rr = Region(BIG, at_a, at_a + 3072)
            RQ = rr(5, 4, 128, parts=8)
            Bc = rr(4, 128, parts=8)
            late = Region(HTF, 5000, 6128)
            CM, LF = late(4, 128, parts=8), late(4, 128, parts=8)
            fl = "p c t -> p (c t)"
            igp = PB[0][0:8, :]
            fp = PB[1][0:8, :]
            lf, bb, cm = LF.rearrange(fl), Bc.rearrange(fl), CM.rearrange(fl)
            S(lambda e: e.activation(lf, fp, ACT.Abs), tk, V.now())
            ts = S(lambda e: e.activation(lf, lf, ACT.Exp, scale=-1.0))
            V(lambda e: e.tensor_scalar(lf, lf, 1.0, None, ALU.add), ts)
            ts = S(lambda e: e.activation(lf, lf, ACT.Ln), V.now())
            V(lambda e: e.scalar_tensor_tensor(lf, fp, 0.0, lf, ALU.min, ALU.subtract), ts)
            V(lambda e: e.tensor_tensor_scan(bb, D0, lf, 0.0, ALU.mult, ALU.add))
            a_row = RQ[:, 0, :, :].rearrange(fl)
            V(lambda e: e.tensor_tensor(a_row, igp, bb, ALU.subtract))
            V(lambda e: e.tensor_tensor_scan(cm, D1, a_row, LOW, ALU.add, ALU.max))
            MM = SM[0:8, 208:216]
            V(lambda e: e.memset(MM[:, 0:1], 0.0))
            for c in range(4):
                V((lambda c: lambda e: e.tensor_scalar(MM[:, c + 1:c + 2], CM[:, c, 127:128], MM[:, c:c + 1],
                                                      Bc[:, c, 127:128], ALU.max, ALU.add))(c))
                V((lambda c: lambda e: e.tensor_scalar(CM[:, c, :], CM[:, c, :], MM[:, c:c + 1], None,
                                                      ALU.max))(c))
            V(lambda e: e.tensor_scalar(RQ[:, 1, :, :], CM, -1.0, None, ALU.mult))
            V(lambda e: e.tensor_tensor(LF, Bc, CM, ALU.add))
            S(lambda e: e.activation(RQ[:, 3, :, :], LF, ACT.Exp, scale=-1.0), V.now())
            for c in range(4):
                S((lambda c: lambda e: e.activation(RQ[:, 2, c, :], CM[:, c, :], ACT.Exp, scale=-1.0,
                                                   bias=MM[:, c:c + 1]))(c))
                S((lambda c: lambda e: e.activation(RQ[:, 4, c, :], RQ[:, 0, c, :], ACT.Exp,
                                                   bias=RQ[:, 1, c, 127:128]))(c))
            DG8 = tmp(4, 8, parts=8)
            for c in range(4):
                V((lambda c: lambda e: e.tensor_scalar(DG8[:, c, :], IDENT[0:8, 0:8], RQ[:, 2, c, 127:128], None,
                                                      ALU.mult))(c), S.now())
            DEC = tmp(32)
            ops = [(lambda c, q: lambda e: e.transpose(PB[2][:, (c * 5 + q) * 8:(c * 5 + q) * 8 + 8],
                                                      RQ[:, q, c, :], IDENT[0:8, 0:8]))(c, q)
                   for c in range(4) for q in range(5)]
            ops.append(mm(PB[3][:, 0:32], ONES[0:8, :], DG8.rearrange("p c r -> p (c r)")))
            tk = P(ops, V.now(), S.now())
            CP, NAT = tmp(4, 5, 8), tmp(4, 5, 8)
            V(lambda e: e.tensor_copy(CP.rearrange("p c q r -> p (c q r)"), PB[2][:, 0:160]), tk)
            V(lambda e: e.tensor_copy(DEC, PB[3][:, 0:32]))
            tk = P([mm(PB[4][:, 0:160], J, CP.rearrange("p c q r -> p (c q r)"))], V.now())
            nv = PB[4][:, 0:160].rearrange("p (c q r) -> p c q r", c=4, q=5)
            for c in range(4):
                V((lambda c: lambda e: e.tensor_copy(NAT[:, ORD[0][c], :, 0:4], CP[:, c, :, 0:4]))(c), tk)
                V((lambda c: lambda e: e.tensor_copy(NAT[:, ORD[1][c], :, 4:8], nv[:, c, :, 4:8]))(c))
            barrier()
            EE, ST, DGm = tmp(4, 128), tmp(4, 128), tmp(4, 128)
            CS = [tmp(4, 129), tmp(4, 129)]
            WVA = tmp(4, 129)
            PS1 = tmp(2, 129)
            RR = tmp(2, 129)
            HM = tmp(2, 4, 128)
            DN = SM[:, 216:224]

            def state(d, c):
                b = ORD[d][c]
                wc = NAT[:, b, 4, 4 * d:4 * d + 4].unsqueeze(2).broadcast_to([128, 4, 129])
                tw = V(lambda e: e.tensor_tensor(WVA, VA[:, b, :, :], wc, ALU.mult), PE.now())
                for p in range(2):
                    tk = P([mm(PB[p][:, h * 129:(h + 1) * 129], KTOK[:, b, (2 * p + h) * 128:(2 * p + h + 1) * 128],
                               WVA[:, 2 * p + h, :]) for h in range(2)], tw)
                    for h in range(2):
                        hh = 2 * p + h
                        src = PB[p][:, h * 129:(h + 1) * 129]
                        dst = CS[d][:, hh, :]
                        if c == 0:
                            V((lambda dst, src: lambda e: e.tensor_copy(dst, src))(dst, src), tk)
                        else:
                            x = c * 8 + d * 4 + hh
                            V((lambda dst, src, x: lambda e: e.scalar_tensor_tensor(
                                dst, dst, DEC[:, x:x + 1], src, ALU.mult, ALU.add))(dst, src, x), tk)

            def outputs(d, c):
                b = ORD[d][c]
                s = slice(b * 128, (b + 1) * 128)
                gc = NAT[:, b, 1, 4 * d:4 * d + 4].unsqueeze(2).broadcast_to([128, 4, 128])
                tg = V(lambda e: e.tensor_tensor(DGm, IDENT.unsqueeze(1).broadcast_to([128, 4, 128]), gc,
                                                 ALU.mult), PE.now())
                te = P([mm(PB[2][:, :], ONES[:, :], DGm.rearrange("p h t -> p (h t)"), True, False)] +
                       [mm(PB[2][:, h * 128:(h + 1) * 128], IDENT, MASK[:, d, :], False, h == 3)
                        for h in range(4)], tg, S.now())
                for h in range(4):
                    S((lambda h: lambda e: e.activation(EE[:, h, :], PB[2][:, h * 128:(h + 1) * 128], ACT.Exp,
                                                       bias=NAT[:, b, 0, 4 * d + h:4 * d + h + 1]))(h), te, tg)
                tq = P([mm(PB[3][:, h * 128:(h + 1) * 128], KT[:, h, s], QT[:, h, s]) for h in range(4)], tg)
                tst = V(lambda e: e.tensor_tensor(ST.rearrange("p h t -> p (h t)"), PB[3][:, :],
                                                  EE.rearrange("p h t -> p (h t)"), ALU.mult), tq, S.now())
                for p in range(2):
                    tk1 = P([mm(PB[4 + p][:, h * 129:(h + 1) * 129], ST[:, 2 * p + h, :], VA[:, b, 2 * p + h, :])
                             for h in range(2)], tst)
                    tk2 = P([mm(PB[6 + p][:, h * 129:(h + 1) * 129], QT[:, 2 * p + h, s], CS[d][:, 2 * p + h, :])
                             for h in range(2)], tst)
                    ts = S((lambda p: lambda e: e.activation(PS1.rearrange("p h t -> p (h t)"),
                                                            PB[4 + p][:, 0:258], ACT.Copy))(p), tk1, V.now())
                    for h in range(2):
                        hh = 2 * p + h
                        r = 4 * d + hh
                        V((lambda p, h, r: lambda e: e.scalar_tensor_tensor(
                            RR[:, h, :], PB[6 + p][:, h * 129:(h + 1) * 129], NAT[:, b, 2, r:r + 1], PS1[:, h, :],
                            ALU.mult, ALU.add))(p, h, r), tk2, ts)
                    r = 4 * d + 2 * p
                    V(lambda e: e.scalar_tensor_tensor(DN[:, 0:2], RR[:, :, 128], -1.0, RR[:, :, 128],
                                                       ALU.mult, ALU.max))
                    V((lambda r: lambda e: e.tensor_tensor(DN[:, 0:2], DN[:, 0:2], NAT[:, b, 3, r:r + 2],
                                                          ALU.max))(r))
                    V(lambda e: e.reciprocal(DN[:, 2:4], DN[:, 0:2]))
                    for h in range(2):
                        dst = HM[:, b, 2 * p + h, :]
                        if d == 0:
                            V((lambda dst, h: lambda e: e.tensor_scalar(dst, RR[:, h, 0:128], DN[:, 2 + h:3 + h], None,
                                                                       ALU.mult))(dst, h))
                        else:
                            V((lambda dst, h: lambda e: e.scalar_tensor_tensor(
                                dst, RR[:, h, 0:128], DN[:, 2 + h:3 + h], dst, ALU.mult, ALU.add))(dst, h))

            for d in range(2):
                state(d, 0)
                state(d, 1)
                outputs(d, 2)
                state(d, 2)
                outputs(d, 3)
            dump("HM", HM.rearrange("p b h t -> p b (h t)"), V.now())
            t = barrier()
            ht2 = Region(HTF, 0, 6128)
            keep = Region(BIG, at_a, at_a + 3072 + 7184)
            LA, BB = keep(2, 2, 512), keep(2, 2, 512)
            W2 = keep(512, parts=32)
            QB = keep(2, 2, 256)
            QQ, KK, KST = keep(2, 256), keep(2, 256), keep(4, 256)
            SS = [keep(2, 256), keep(2, 256)]
            AT = keep(4, 128)
            HMc = keep(2, 512)
            HG, TE, TF = ht2(2, 512), ht2(2, 512), ht2(2, 256)
            KS, EBE = ht2(2, 512), ht2(2, 2, 8)
            V(lambda e: e.tensor_copy(HMc, HM.rearrange("p b h t -> p b (h t)")))
            V.wait(*barrier())
            tz = V(lambda e: e.memset(W2, 0.0))
            for d in range(2):
                tw = load_once("lrw", W2[d * 16:(d + 1) * 16, d * 256:(d + 1) * 256], A["gla_lr_w2_2"][0, d], tz, *t)
            V(lambda e: e.memset(SS[0], 0.0))
            V(lambda e: e.memset(SS[1], 0.0))
            V(lambda e: e.memset(QB, 0.0))
            ops = [mm(PB[2 * d + f][:, :], W2[:, d * 256 + f * 128:d * 256 + (f + 1) * 128], GLR)
                   for d in range(2) for f in range(2)]
            tk = P(ops, tw, V.now())
            for d in range(2):
                for f in range(2):
                    V((lambda d, f: lambda e: e.tensor_scalar(LA[:, d, f, :], PB[2 * d + f][:, :],
                                                             col("gla_alpha_b_2", 2 * d + f), None, ALU.add))(d, f), tk)
            S(lambda e: e.activation(BB, LA, ACT.Abs), V.now())
            ts = S(lambda e: e.activation(BB, BB, ACT.Exp, scale=-1.0))
            V(lambda e: e.tensor_scalar(BB, BB, 1.0, None, ALU.add), ts)
            ts = S(lambda e: e.activation(BB, BB, ACT.Ln), V.now())
            V(lambda e: e.tensor_scalar(LA, LA, 0.0, None, ALU.min))
            V(lambda e: e.tensor_tensor(LA, LA, BB, ALU.subtract), ts)
            V(lambda e: e.tensor_scalar(LA, LA, 1.0 / 16, None, ALU.mult))
            for d in range(2):
                for f in range(2):
                    V((lambda d, f: lambda e: e.tensor_tensor_scan(BB[:, d, f, :], D64, LA[:, d, f, :], 0.0,
                                                                  ALU.mult, ALU.add))(d, f))
            for f in range(2):
                bv = BB[:, 1, f, :].rearrange("p (c t) -> p c t", t=64)
                lv = LA[:, 1, f, :].rearrange("p (c t) -> p c t", t=64)
                V((lambda bv, lv: lambda e: e.tensor_tensor(lv, lv, bv, ALU.subtract))(bv, lv))
                V((lambda bv, lv: lambda e: e.tensor_tensor(
                    lv, lv, bv[:, :, 63:64].broadcast_to([128, 8, 64]), ALU.add))(bv, lv))
                V((lambda f: lambda e: e.tensor_copy(BB[:, 1, f, :], LA[:, 1, f, :]))(f))
            ZR = AT[0:1, :, :].rearrange("p h t -> p (h t)")
            V(lambda e: e.memset(ZR, 0.0))
            P([mm(PB[6 + b][:, :], ONES[0:1, :], ZR, True, False) for b in range(2)], V.now())
            pair = [0]
            for d in range(2):
                end, mid = (63, 32) if d == 0 else (0, 31)
                for f in range(2):
                    bv = BB[:, d, f, :].rearrange("p (c t) -> p c t", t=64)
                    be = bv[:, :, end:end + 1]
                    te = TE[:, f, :].rearrange("p (c t) -> p c t", t=64)
                    tf = TF[:, f, :].rearrange("p (c t) -> p c t", t=64)
                    V((lambda te, be, bv: lambda e: e.tensor_tensor(te, be.broadcast_to([128, 8, 64]), bv,
                                                                   ALU.subtract))(te, be, bv), PE.now())
                    V((lambda tf, bv, mid: lambda e: e.tensor_tensor(
                        tf, bv[:, 0:4, :], bv[:, 0:4, mid:mid + 1].broadcast_to([128, 4, 64]),
                        ALU.subtract))(tf, bv, mid))
                    S((lambda d, f, be: lambda e: e.activation(EBE[:, d, f, :].unsqueeze(2), be, ACT.Exp))(d, f, be),
                      V.now())
                S(lambda e: e.activation(TE, TE, ACT.Exp), V.now())
                S(lambda e: e.activation(QQ, TF, ACT.Exp), PE.now())
                S(lambda e: e.activation(KK, TF, ACT.Exp, scale=-1.0))
                S((lambda d: lambda e: e.activation(TF, BB[:, d, :, 0:256], ACT.Exp))(d))
                V(lambda e: e.tensor_tensor(KS, TE, GK, ALU.mult), S.now(), PE.now())
                V(lambda e: e.tensor_tensor(QQ, QQ, GQ, ALU.mult))
                V(lambda e: e.tensor_tensor(KK, KK, GK[:, :, 0:256], ALU.mult))
                for f in range(2):
                    tv = TF[:, f, :].rearrange("p (c h t) -> p c h t", c=2, h=2)
                    gv = GQ[:, f, :].rearrange("p (c h t) -> p c h t", c=2, h=2)
                    for x in range(2):
                        qv = QB[:, x, f, :].rearrange("p (c h t) -> p c h t", c=2, h=2)
                        V((lambda qv, tv, gv, x: lambda e: e.tensor_tensor(qv[:, :, x, :], tv[:, :, x, :],
                                                                         gv[:, :, x, :], ALU.mult))(qv, tv, gv, x))
                barrier()
                transposes([(KST[:, b, f * 128:(f + 1) * 128], KS[:, f, b * 128:(b + 1) * 128])
                            for b in range(4) for f in range(2)], [0, 1], (V.now(),))
                barrier()
                for b in range(2):
                    s = slice(b * 128, (b + 1) * 128)
                    gm = GM[:, d, :].unsqueeze(1).broadcast_to([128, 2, 128])
                    for x in range(2):
                        r = slice(64 * x, 64 * x + 64)
                        bank = PB[(2, 5)[x]]
                        tk = P([mm(bank[:, f * 128:(f + 1) * 128], KK[r, f, s], QQ[r, f, s]) for f in range(2)],
                               V.now())
                        av = AT.rearrange("p (f x) t -> p f x t", x=2)[:, :, x, :]
                        pv2 = bank[:, 0:256].rearrange("p (h t) -> p h t", h=2)
                        V((lambda av, pv2, gm: lambda e: e.tensor_tensor(av, pv2, gm, ALU.min))(av, pv2, gm), tk)
                        V((lambda av, gm: lambda e: e.scalar_tensor_tensor(av, gm, -1.0, av, ALU.mult,
                                                                         ALU.max))(av, gm))
                    P([mm(PB[6 + b][:, h * 128:(h + 1) * 128], AT[:, h, :], GV[:, b, h * 128:(h + 1) * 128],
                          False, False) for h in range(4)], V.now())
                    V.wait(PE.now())
                chunks = [4, 5, 6, 7, 0, 1, 2, 3] if d == 0 else [7, 6, 5, 4, 3, 2, 1, 0]
                if d == 1:
                    V(lambda e: e.memset(SS[0], 0.0), PE.now())
                for n_, ch in enumerate(chunks):
                    b, x = ch // 2, ch % 2
                    cur, nxt = SS[n_ % 2], SS[(n_ + 1) % 2]
                    if n_ >= 4:
                        last = d == 1 and n_ == 7
                        P([mm(PB[6 + b][:, f * 256:(f + 1) * 256], QB[:, x, f, b * 128:(b + 1) * 128], cur[:, f, :],
                              False, (d == 1 and x == 0 and f == 1)) for f in range(2)], V.now())
                    if n_ < 7:
                        bank = PB[3 + n_ % 2]
                        tk = P([mm(bank[:, f * 256:(f + 1) * 256], KST[64 * x:64 * x + 64, b, f * 128:(f + 1) * 128],
                                   GV[64 * x:64 * x + 64, b, f * 256:(f + 1) * 256]) for f in range(2)], V.now())
                        for f in range(2):
                            for h in range(2):
                                r = slice(64 * h, 64 * h + 64)
                                q = slice(128 * h, 128 * h + 128)
                                V((lambda cur, nxt, f, r, q, bank, h, ch, d: lambda e: e.scalar_tensor_tensor(
                                    nxt[r, f, q], cur[r, f, q], EBE[r, d, f, ch:ch + 1],
                                    bank[r, f * 256 + 128 * h:f * 256 + 128 * h + 128], ALU.mult, ALU.add))(
                                        cur, nxt, f, r, q, bank, h, ch, d), tk)
                barrier()
            for b in range(2):
                S((lambda b: lambda e: e.activation(HG[:, b, :], PB[6 + b][:, :], ACT.Copy))(b))
            dump("HG", HG, S.now())
            barrier()
            OO = keep.base[:, at_a:at_a + 2048].rearrange("p (b n) -> p b n", b=2)
            R8 = SM[:, 224:240]
            TT = BIG[:, at_a + 2048:at_a + 3072].rearrange("p (b n) -> p b n", b=2)
            HMf = HMc
            for s_, (src, gate, o0) in enumerate(((HMf, MO, 0), (HG, GR, 512))):
                V((lambda src: lambda e: e.tensor_tensor(TT, src, src, ALU.mult))(src))
                V((lambda s_: lambda e: e.tensor_reduce(R8[:, s_ * 8:s_ * 8 + 8],
                                                       TT.rearrange("p b (h t) -> p (b h) t", h=4), AX.X,
                                                       ALU.add))(s_))
                V((lambda src, gate, o0: lambda e: e.tensor_tensor(OO[:, :, o0:o0 + 512], src, gate,
                                                                  ALU.mult))(src, gate, o0))
            V(lambda e: e.tensor_scalar(R8, R8, 1.0 / 128, EPS, ALU.mult, ALU.add))
            V(lambda e: e.reciprocal(R8, R8))
            ts = S(lambda e: e.activation(R8, R8, ACT.Sqrt), V.now())
            for s_ in range(2):
                for b in range(2):
                    ov = OO[:, b, s_ * 512:(s_ + 1) * 512].rearrange("p (h t) -> p h t", h=4)
                    rv = R8[:, s_ * 8 + b * 4:s_ * 8 + b * 4 + 4].unsqueeze(2).broadcast_to([128, 4, 128])
                    V((lambda ov, rv: lambda e: e.tensor_tensor(ov, ov, rv, ALU.mult))(ov, rv), ts)
            barrier()
            project_out(OO, G1,
                        lambda kc: col("ml_norm_g_2", kc) if kc < 4 else col("gla_norm_g_2", kc - 4))
            dump("Y", X[:, :, :], V.now())
            barrier()
            if stop == "mix":
                return
            peer(GA, G2, at_a)

        def peer(GA, G2, at_a):
            reg = Region(BIG, at_a, BIGN)
            hn = reg(2, 1024)
            H2 = reg(2, 1024)
            QP = reg(16, 256)
            KEYT = reg(16, 128)
            big = Region(BIG, reg.at, BIGN)
            KEYS = big(16, 128)
            tkeys = load_once("keys", KEYS, A["peer_keys_2"][0].rearrange("h s k q -> k (h s) q"),
                              V.now(), S.now(), PE.now(), G.now())
            t = normed(hn, X, V.now())
            transposed(hn, lambda kc: GA[:, 4, kc:kc + 1], shift=lambda kc: GA[:, 5, kc:kc + 1], after=(t,))
            for b in range(2):
                for k in range(8):
                    V((lambda b, k: lambda e: e.tensor_tensor(
                        hn[:, b, k * 128:(k + 1) * 128], HTH[:, k, b * 128:(b + 1) * 128].bitcast(F32),
                        HTL[:, k, b * 128:(b + 1) * 128].bitcast(F32), ALU.add))(b, k),
                      PE.now(), free=k > 0)
            barrier()
            transposes([(H2[:, b, k * 128:(k + 1) * 128], hn[:, b, k * 128:(k + 1) * 128])
                        for b in range(2) for k in range(8)], [0, 1, 2, 3], (V.now(),))
            V.wait(tkeys)
            S.wait(tkeys)
            PE.wait(tkeys)
            transposes([(KEYT[:, k, :], KEYS[:, k, :]) for k in range(16)], [4, 5, 6, 7], (V.now(),))
            barrier()
            prev = {}
            for j in range(8):
                w = need()
                for c in range(2):
                    q = slice(c * 128, (c + 1) * 128)
                    tk = P(mm3(PB[j % 4][:, c * 256:(c + 1) * 256], [(w.h[:, k, q], w.l[:, k, q]) for k in range(8)],
                               [(HTH[:, k, 0:256], HTL[:, k, 0:256]) for k in range(8)]),
                           w.ready, *([prev[j - 4]] if j >= 4 else []))
                w.free(tk)
                prev[j] = S((lambda j: lambda e: e.activation(
                    QP[:, 2 * j:2 * j + 2, :], PB[j % 4][:, :].rearrange("p (a b) -> p a b", a=2), ACT.Copy))(j), tk,
                    free=True)
            barrier()
            big = Region(BIG, reg.at, BIGN)
            SC, WK, WK2 = big(16, 128), big(256), big(256)
            htp = Region(HTF, 0, 8192)
            CD, OH, IO16 = htp(8, 16, 16), htp(8, 16, 16), htp(16)
            tio = load_once("io", IO16, A["c_cst2"][:, 2048:2064], V.now(), S.now(), PE.now())
            V.wait(tio)
            TS = big(16, 16)
            TI, TIF = big(16, 16), big(16, 16)
            TI = TI.bitcast(U32)
            BS, I1F, I2F, ID1, ID2 = big(8, 16), big(8, 16), big(8, 16), big(8, 16), big(8, 16)
            BI, I1 = big(8, 16).bitcast(U32), big(8, 16).bitcast(U32)
            IDX = big(2, 128).bitcast(U32)
            GW = big(2, 8, 16)
            AV = big(2, 128)
            for b in range(2):
                for g in range(4):
                    tk = P([mm(PB[4 + g][:, x * 128:(x + 1) * 128], QP[:, 4 * g + x, b * 128:(b + 1) * 128],
                               KEYT[:, 4 * g + x, :]) for x in range(4)], V.now(), S.now())
                    S((lambda g: lambda e: e.activation(SC[:, 4 * g:4 * g + 4, :],
                                                       PB[4 + g][:, :].rearrange("p (a b) -> p a b", a=4),
                                                       ACT.Copy))(g), tk, V.now())

                def top16(vals, idx, src, work):
                    V(lambda e: e.max(vals[:, 0:8], src))
                    V(lambda e: e.max_index(idx[:, 0:8], vals[:, 0:8], src))
                    V(lambda e: e.match_replace(work, vals[:, 0:8], src, LOW))
                    V(lambda e: e.max(vals[:, 8:16], work))
                    V(lambda e: e.max_index(idx[:, 8:16], vals[:, 8:16], work))

                V.wait(S.now())
                for x in range(16):
                    top16(TS[:, x, :], TI[:, x, :], SC[:, x, :], WK[:, 0:128])
                tsv = TS.rearrange("p (h s) k -> p h s k", s=2)
                V(lambda e: e.tensor_copy(TIF, TI))
                V(lambda e: e.tensor_tensor(CD, tsv[:, :, 0, :].unsqueeze(3).broadcast_to([128, 8, 16, 16]),
                                            tsv[:, :, 1, :].unsqueeze(2).broadcast_to([128, 8, 16, 16]), ALU.add))
                for h in range(8):
                    top16(BS[:, h, :], BI[:, h, :], CD[:, h, :, :].rearrange("p a b -> p (a b)"), WK)
                tif = TIF.rearrange("p (h s) k -> p h s k", s=2)
                for s_, (idf, dst) in enumerate(((I1F, ID1), (I2F, ID2))):
                    op, val = ((ALU.logical_shift_right, 4), (ALU.bitwise_and, 15))[s_]
                    V((lambda op, val: lambda e: e.tensor_scalar(I1, BI, val, None, op))(op, val))
                    V((lambda idf: lambda e: e.tensor_copy(idf, I1))(idf))
                    V((lambda idf: lambda e: e.tensor_tensor(
                        OH.rearrange("p h k j -> p (h k) j"),
                        idf.rearrange("p h k -> p (h k)").unsqueeze(2).broadcast_to([128, 128, 16]),
                        IO16.unsqueeze(1).broadcast_to([128, 128, 16]), ALU.is_equal))(idf))
                    V((lambda s_: lambda e: e.tensor_tensor(
                        OH, OH, tif[:, :, s_, :].unsqueeze(2).broadcast_to([128, 8, 16, 16]), ALU.mult))(s_))
                    V((lambda dst: lambda e: e.tensor_reduce(dst.rearrange("p h k -> p (h k)"),
                                                            OH.rearrange("p h k j -> p (h k) j"), AX.X,
                                                            ALU.add))(dst))
                V(lambda e: e.scalar_tensor_tensor(ID1, ID1, 128.0, ID2, ALU.mult, ALU.add))
                V((lambda b: lambda e: e.tensor_copy(IDX[:, b, :], ID1.rearrange("p h k -> p (h k)")))(b))
                V((lambda b: lambda e: e.tensor_tensor(GW[:, b, :, :], BS,
                                                      BS[:, :, 0:1].broadcast_to([128, 8, 16]),
                                                      ALU.subtract))(b))
                ts = S((lambda b: lambda e: e.activation(GW[:, b, :, :], GW[:, b, :, :], ACT.Exp))(b), V.now())
                V((lambda b: lambda e: e.tensor_reduce(SM[:, 0:8], GW[:, b, :, :], AX.X, ALU.add))(b), ts)
                V(lambda e: e.reciprocal(SM[:, 8:16], SM[:, 0:8]))
                V((lambda b: lambda e: e.tensor_tensor(GW[:, b, :, :], GW[:, b, :, :],
                                                      SM[:, 8:16].unsqueeze(2).broadcast_to([128, 8, 16]),
                                                      ALU.mult))(b))
            barrier()
            NG = 20
            ROWS_ = [RAW[:, i * 1024:(i + 1) * 1024] for i in range(10)] + \
                [HIF[:, i * 1024:(i + 1) * 1024] for i in range(10)]
            gs = [sem(f"s_row{i}") for i in range(NG)]
            gn = [0] * NG
            used = [None] * NG
            ACC = QP.rearrange("p a b -> p (a b)")[:, 0:2048].rearrange("p (b n) -> p b n", b=2)
            JK = hn[:, 0, :]
            V(lambda e: e.memset(ACC, 0.0))
            tx = V.now()
            g = 0
            ups, us = A["peer_u_2"][0], A["peer_v_2"][0]

            def gather(table, b, j):
                nonlocal g
                i = g % NG
                g += 1
                G.dma((lambda i, b, j: lambda e: e.indirect_dma_start(
                    out=ROWS_[i], out_offset=None, in_=table,
                    in_offset=bass.IndirectOffsetOnAxis(ap=IDX[:, b, j:j + 1], axis=0)))(i, b, j),
                    gs[i], *([used[i]] if used[i] else [tx]))
                gn[i] += 16
                return i, (gs[i], gn[i])

            for b in range(2):
                for j in range(128):
                    i, arr = gather(ups, b, j)
                    used[i] = V((lambda i, b, j: lambda e: e.tensor_tensor_reduce(
                        out=JK, in0=ROWS_[i], in1=H2[:, b, :], scale=1.0, scalar=0.0, op0=ALU.mult,
                        op1=ALU.add, accum_out=AV[:, b, j:j + 1]))(i, b, j), arr)
                ts = S((lambda b: lambda e: e.activation(AV[:, b, :], AV[:, b, :], ACT.Gelu))(b), V.now())
                V((lambda b: lambda e: e.tensor_tensor(AV[:, b, :], AV[:, b, :],
                                                      GW[:, b, :, :].rearrange("p h k -> p (h k)"),
                                                      ALU.mult))(b), ts)
                for j in range(128):
                    i, arr = gather(us, b, j)
                    used[i] = V((lambda i, b, j: lambda e: e.scalar_tensor_tensor(
                        ACC[:, b, :], ROWS_[i], AV[:, b, j:j + 1], ACC[:, b, :], ALU.mult, ALU.add))(i, b, j), arr)
            FG = HTF[:, 0:1024]
            tf = load_once("nf", FG, A["norm_f_g_2"].partition_broadcast(128), tx)
            V(lambda e: e.tensor_tensor(ACC, ACC, G2.unsqueeze(1).broadcast_to([128, 2, 1024]), ALU.mult))
            V(lambda e: e.tensor_tensor(X[:, :, :], X[:, :, :], ACC, ALU.add))
            tr = rstd([X[:, b, :] for b in range(2)], 1024, SM[:, 0:2], hn.rearrange("p b n -> p (b n)"), V.now())
            for b in range(2):
                V((lambda b: lambda e: e.scalar_tensor_tensor(X[:, b, :], X[:, b, :], SM[:, b:b + 1], FG,
                                                             ALU.mult, ALU.mult))(b), tr, tf)

        def finish():
            t = barrier()
            SP.dma(lambda e: e.dma_start(out.rearrange("o (b p) n -> p (o b) n", p=128), X[:, :, :]), outsem, *t)
            SP.wait((outsem, dumped[0] + 16))

        def plan_second():
            wv = A["w_in_2"][0].rearrange("(k p) n -> p k n", p=128)
            cuts = [256 * i for i in range(9)] + [2320, 2576, 2832, 3088, 3368, 3632]
            for a_, b_ in zip(cuts, cuts[1:]):
                plan(wv[:, :, a_:b_], 8, b_ - a_)
            plan_out(A["w_out_2"][0])
            wq = A["peer_wq_2"][0].rearrange("(k p) n -> p k n", p=128)
            for j in range(8):
                plan(wq[:, :, j * 256:(j + 1) * 256], 8, 256)

        def program():
            for l in range(2):
                plan_ffn(l, 1)
                plan_hybrid(l)
                plan_ffn(l, 2)
            plan_second()
            loads()
            for l in range(2):
                ffn(l, 1)
                dump(f"F{l}", X[:, :, :], V.now())
                if stop == f"ffn{l}":
                    return
                hybrid(l)
                if stop == f"hyb{l}":
                    return
                ffn(l, 2)
            if stop == "first":
                return
            second()

        program()
        finish()

        block = ctx.enter_context(nc.Block())

        @block.sync
        def _(e):
            SP.emit(e)

        @block.tensor
        def _(e):
            PE.emit(e)

        @block.vector
        def _(e):
            V.emit(e)

        @block.scalar
        def _(e):
            S.emit(e)

        @block.gpsimd
        def _(e):
            G.emit(e)


_INS = ["x", "ffn1_norm", "ffn1_w_gate", "ffn1_w_up", "ffn1_w_down", "mix_norm", "w_in", "c_q_norm",
        "c_kv_norm", "c_w_uq", "c_w_ukv", "w_out", "ffn2_norm", "ffn2_w_gate", "ffn2_w_up", "ffn2_w_down",
        "final_norm", "c_2", "ctx_2", "c_ctx_2", "w_mod_2", "b_mod_2", "norm1_g_2", "w_in_2", "ml_conv_w_2",
        "ml_gate_b_2", "ml_norm_g_2", "gla_lr_w2_2", "gla_alpha_b_2", "gla_norm_g_2", "w_out_2", "norm2_g_2",
        "peer_wq_2", "peer_keys_2", "peer_u_2", "peer_v_2", "norm_f_g_2"]


def constants():
    c = np.zeros((128, 768), np.float32)
    c[:, 0:128] = np.eye(128)
    c[:, 128:256] = np.eye(128)[::-1]
    c[:, 256:384] = 8 * np.eye(128)[::-1]
    pos = np.arange(256, dtype=np.float32)
    t = np.zeros((256, 192), np.float32)
    for d, off in ((64, 0), (32, 128)):
        inv = (np.float32(10000.0) ** (-np.arange(0, d, 2, dtype=np.float32) / np.float32(d))).astype(np.float32)
        ang = (pos[:, None] * inv[None, :]).astype(np.float32).astype(np.float64)
        co, si = np.cos(ang), np.sin(ang)
        t[:, off:off + 2 * d] = np.concatenate([co, co, -si, si], axis=1)
    c[:, 384:768] = t.reshape(2, 128, 192).transpose(1, 0, 2).reshape(128, 384)
    return c


def constants2():
    c = np.zeros((128, 2064), np.float32)
    s, t = np.arange(128)[:, None], np.arange(128)[None, :]
    c[:, 0:128] = np.where(s <= t, 0, NEG)
    c[:, 128:256] = np.where(s >= t, 0, NEG)
    same = s // 64 == t // 64
    c[:, 256:384] = np.where(same & (s <= t), 3e38, 0)
    c[:, 384:512] = np.where(same & (s >= t), 3e38, 0)
    n = np.arange(512)
    c[:, 512:1024] = np.where(n % 128 == 0, 0, 1)
    c[:, 1024:1536] = np.where(n % 128 == 0, -3e37, 0)
    c[:, 1536:2048] = np.where(n % 64 == 0, 0, 1)
    c[:, 2048:2064] = np.arange(16)
    return c


def tensors(nc, inputs):
    arrays, A = {}, {}
    for name in _INS:
        arrays["in_" + name] = np.ascontiguousarray(inputs[name])
    order = np.clip(255 - np.arange(383), -63, 128) + 63
    arrays["in_c_rel"] = np.ascontiguousarray(np.asarray(inputs["a_rel_bias"])[:, :, order])
    arrays["in_c_cst"] = constants()
    arrays["in_c_cst2"] = constants2()
    for name, a in arrays.items():
        A[name[3:]] = nc.dram_tensor(name, a.shape, mybir.dt.from_np(a.dtype), kind="ExternalInput").ap()
    rel = A["c_rel"]
    A["c_relw"] = [bass.AP(tensor=rel.tensor, offset=l * 6 * 383, ap=[[1, 128], [383, 6], [1, 256]])
                   for l in range(2)]
    return arrays, A


def kernel(**inputs):
    import concourse.bacc as _bacc
    from concourse.bass_utils import run_bass_kernel_spmd as _run

    nc = _bacc.Bacc("TRN2", target_bir_lowering=False, num_devices=1)
    arrays, A = tensors(nc, inputs)
    o = nc.dram_tensor("out_0", (1, 256, 1024), F32, kind="ExternalOutput").ap()
    build(nc, A, o, {})
    r = _run(nc, [arrays], core_ids=[0])
    return r.results[0]["out_0"]
```

```python
import numpy as np
import concourse.bass as bass
from concourse import mybir
from contextlib import ExitStack

F32 = mybir.dt.float32
U32 = mybir.dt.uint32
F32R = mybir.dt.float32r
ALU = mybir.AluOpType
ACT = mybir.ActivationFunctionType
AX = mybir.AxisListType
NEG = -1e30
LOW = -3e38
EPS = 1e-6


class Queue:

    def __init__(self, sem, chained):
        self.sem, self.chained, self.n, self.items = sem, chained, 0, []

    def __call__(self, fn, *after, free=False):
        if self.chained and not free and self.n:
            after = after + ((self.sem, self.n),)
        self.n += 1
        self.items.append((after, fn, self.sem, 1))
        return (self.sem, self.n)

    def wait(self, *after):
        self.items.append((after, None, None, 0))

    def dma(self, fn, sem, *after):
        self.items.append((after, fn, sem, 16))

    def now(self):
        return (self.sem, self.n)

    def emit(self, engine):
        seen = {}
        for after, fn, sem, by in self.items:
            for s, v in after:
                if v > seen.get(id(s), 0):
                    engine.wait_ge(s, v)
                    seen[id(s)] = v
            if fn is not None:
                fn(engine).then_inc(sem, by)


def build(nc, A, out, dbg, stop=None):
    ctx = ExitStack()
    with ctx:
        def sb(name, *shape, dt=F32):
            return ctx.enter_context(nc.sbuf_tensor(name, list(shape), dt))

        def sem(name):
            return ctx.enter_context(nc.semaphore(name))

        PE = Queue(sem("s_pe"), False)
        V = Queue(sem("s_v"), True)
        S = Queue(sem("s_s"), True)
        G = Queue(sem("s_g"), True)
        SP = Queue(sem("s_sp"), False)
        outsem = sem("s_out")

        PB = [ctx.enter_context(nc.psum_tensor(f"PB{i}", [128, 512], F32)) for i in range(8)]

        def mm(o, l, r, st=True, sp=True):
            return lambda e: e.matmul(o, l, r, start=st, stop=sp)

        def P(ops, *after):
            def run(e):
                for f in ops:
                    x = f(e)
                return x
            return PE(run, *after)

        def barrier():
            now = [q.now() for q in (PE, V, S, G)]
            for q in (PE, V, S, G):
                q.wait(*[t for t in now if t[0] is not q.sem or q is not PE])
            return now

        NS, SLOT, BIGN = 5, 2240, 18460
        with (nc.sbuf_tensor("RAW", [128, NS * SLOT], F32) as RAW, nc.sbuf_tensor("HTF", [128, 8192], F32) as HTF,
              nc.sbuf_tensor("BIG", [128, BIGN], F32) as BIG, nc.sbuf_tensor("HIF", [128, NS * SLOT], F32) as HIF):
            pass
        LOWS = sb("LOWS", 128, NS * SLOT, dt=F32R)
        HTR = sb("HTR", 128, 8192, dt=F32R)
        BIGR = sb("BIGR", 128, BIGN, dt=F32R)
        HIGH = sb("HIGH", 128, NS * SLOT, dt=F32R)
        HTH = HTR[:, 0:4096].rearrange("p (k t) -> p k t", k=8)
        HTL = HTR[:, 4096:8192].rearrange("p (k t) -> p k t", k=8)
        X = sb("X", 128, 2, 1024)
        CST = sb("CST", 128, 768)
        IDENT, J, J8 = CST[:, 0:128], CST[:, 128:256], CST[:, 256:384]
        ROPE = CST[:, 384:768].rearrange("p (b n) -> p b n", b=2)
        COLS = sb("COLS", 128, 256)
        MODC = sb("MODC", 128, 64)
        CT = sb("CT", 128, 16)
        SM = sb("SM", 128, 256)
        ONES = sb("ONES", 128, 128)
        HALF = sb("HALF", 1, 128)
        NROW = sb("NROW", 1, 64)

        class Region:

            def __init__(self, base, at, end):
                self.base, self.at, self.end = base, at, end

            def __call__(self, *shape, parts=128):
                n = int(np.prod(shape))
                assert self.at + n <= self.end, (self.at, n, self.end)
                self.at += n
                return shaped(self.base[0:parts, self.at - n:self.at], shape)

        def shaped(v, shape):
            names = "abcd"[:len(shape)]
            if len(shape) > 1:
                v = v.rearrange("p (" + " ".join(names) + ") -> p " + " ".join(names),
                                **{k: s for k, s in zip(names[:-1], shape)})
            return v

        NX = NS + 2
        XAT = BIGN - 2 * SLOT * 2
        MEM = [(RAW, HIGH, LOWS, i * SLOT, i * SLOT) for i in range(NS)] + \
            [(BIG, BIGR, BIGR, XAT + i * SLOT, XAT + (2 + i) * SLOT) for i in range(2)]
        slot_sem = [sem(f"s_w{i}") for i in range(NX)]
        slot_n, last = [0] * NX, [None] * NX
        tiles, extra = [], {}
        at = {"load": 0, "high": 0, "low": 0, "use": 0}

        class Tile:
            def __init__(self, n, src, shape, split, wide, slots):
                some = range(NX if wide else slots)
                i = min(some, key=lambda i: -1 if last[i] is None else last[i].n)
                self.n, self.i, self.src, self.split, self.released = n, i, src, split, None
                self.before, last[i] = last[i], self
                self.sem, self.wide = slot_sem[i], wide
                self.size = int(np.prod(shape))
                assert self.size <= SLOT
                raw, high, low, a, c = MEM[i]
                self.raw, self.h, self.l = (shaped(m[:, x:x + self.size], shape)
                                            for m, x in ((raw, a), (high, c), (low, a)))

            def free(self, *tokens):
                self.released = tokens
                loads()

        def plan(src, *shape, split=True, wide=False, slots=NS):
            tiles.append(Tile(len(tiles), src, shape, split, wide, slots))

        def loads():
            while at["load"] < len(tiles):
                t = tiles[at["load"]]
                after = ()
                if t.before is not None:
                    if t.before.released is None:
                        return
                    after = t.before.released
                if t.i >= NS:
                    if t.wide not in extra:
                        return
                    after = after + extra[t.wide]
                SP.dma((lambda t: lambda e: e.dma_start(t.raw, t.src))(t), t.sem, *after)
                slot_n[t.i] += 16
                t.arrived = (t.sem, slot_n[t.i])
                at["load"] += 1

        def need(ahead=1):
            n = at["use"]
            at["use"] += 1
            while at["high"] < min(n + 2 + ahead, len(tiles)) and at["high"] < at["load"]:
                t = tiles[at["high"]]
                if t.split:
                    t.high = S((lambda t: lambda e: e.activation(t.h, t.raw, ACT.Copy))(t), t.arrived, free=True)
                at["high"] += 1
            while at["low"] < min(n + 1 + ahead, len(tiles)) and at["low"] < at["high"]:
                t = tiles[at["low"]]
                t.ready = t.arrived
                if t.split:
                    t.ready = V((lambda t: lambda e: e.tensor_tensor(t.l, t.raw, t.h.bitcast(F32), ALU.subtract))(t),
                                t.high, free=True)
                at["low"] += 1
            assert at["low"] > n, n
            return tiles[n]

        def mm3(o, ls, rs, st=True, sp=True):
            ops = []
            for k, ((lh, ll), (rh, rl)) in enumerate(zip(ls, rs)):
                f, z = st and k == 0, sp and k == len(ls) - 1
                ops += [mm(o, lh, rh, f, False), mm(o, lh, rl, False, False), mm(o, ll, rh, False, z)]
            return ops

        once = {}

        def load_once(name, dst, src, *after):
            if name not in once:
                once[name] = [sem("s_" + name), 0]
            s = once[name]
            s[1] += 16
            SP.dma(lambda e: e.dma_start(dst, src), s[0], *after)
            return (s[0], s[1])

        def dump(name, view, *after):
            if name in dbg:
                SP.dma(lambda e: e.dma_start(dbg[name], view), outsem, *after)
                dumped[0] += 16
                for q in (PE, V, S, G):
                    q.wait((outsem, dumped[0]))

        dumped = [0]

        ROWS, ROWS2 = BIG[:, 0:128], BIG[:, 128:256]
        load_once("cst", CST[:, 0:768], A["c_cst"])
        rows = [("ffn1_norm", 16), ("mix_norm", 16), ("ffn2_norm", 16), ("norm1_g_2", 8), ("norm2_g_2", 8),
                ("ml_norm_g_2", 4), ("gla_norm_g_2", 4), ("c_q_norm", 6), ("c_kv_norm", 4),
                ("ml_conv_w_2", 24), ("gla_alpha_b_2", 4)]
        COL = {}
        r = 0
        for name, n in rows:
            src = A[name]
            nd = len(src.shape)
            if nd == 1:
                v = src.rearrange("(a p) -> a p", p=128)
            elif nd == 2:
                v = src.rearrange("l (a p) -> (l a) p", p=128)
            else:
                v = src.rearrange("l k (a p) -> (l k a) p", p=128)
            load_once("cst", ROWS[r:r + n, :], v)
            COL[name] = r
            r += n
        nrow = r
        load_once("cst", ROWS2[0:48, :], A["b_mod_2"].rearrange("l (a p) -> (l a) p", p=128))
        load_once("cst", ROWS2[48:56, :], A["c_2"].rearrange("l (a p) -> (l a) p", p=128))
        cst = load_once("cst", ROWS2[56:64, :], A["c_ctx_2"].rearrange("(a p) -> a p", p=128))
        xin = load_once("x", X[:, :, :], A["x"].rearrange("o (b p) n -> p (o b) n", p=128))
        V(lambda e: e.memset(ONES[:, :], 1.0), free=True)
        V(lambda e: e.memset(HALF[:, :], 0.0), free=True)
        V(lambda e: e.memset(HALF[:, 0:64], 1.0))
        kv = V(lambda e: e.memset(NROW[:, :], NEG), free=True)
        P([lambda e: e.transpose(PB[0][:, 0:nrow], ROWS[0:nrow, :], IDENT[0:nrow, 0:nrow])], cst)
        t = P([lambda e: e.transpose(PB[1][:, 0:64], ROWS2[0:64, :], IDENT[0:64, 0:64])])
        V(lambda e: e.tensor_copy(COLS[:, 0:nrow], PB[0][:, 0:nrow]), t, cst, kv)
        t = V(lambda e: e.tensor_copy(COLS[:, 128:192], PB[1][:, 0:64]), xin)
        S.wait(cst, xin)
        ts = S(lambda e: e.activation(COLS[:, 192:208], COLS[:, 176:192], ACT.Silu), t)
        V(lambda e: e.tensor_copy(CT[:, :], COLS[:, 192:208]), ts)
        COND = CT[:, :].rearrange("p (w k) -> p w k", w=2)

        def col(name, i):
            c = COL[name] + i
            return COLS[:, c:c + 1]

        def rstd(views, n, dst, junk, *after):
            k = len(views)
            for i, v in enumerate(views):
                if i == 1 and junk.shape[-1] >= 2 * n:
                    V((lambda v, i: lambda e: e.tensor_tensor_reduce(
                        out=junk[:, n:2 * n], in0=v, in1=v, scale=1.0, scalar=0.0, op0=ALU.mult, op1=ALU.add,
                        accum_out=dst[:, i:i + 1]))(v, i), *after)
                else:
                    t = S((lambda v, i: lambda e: e.activation(junk[:, 0:n], v, ACT.Square,
                                                              accum_out=dst[:, i:i + 1]))(v, i), *after)
            V(lambda e: e.tensor_scalar(dst[:, 0:k], dst[:, 0:k], 1.0 / n, EPS, ALU.mult, ALU.add), t)
            t = V(lambda e: e.reciprocal(dst[:, 0:k], dst[:, 0:k]))
            t = S(lambda e: e.activation(dst[:, 0:k], dst[:, 0:k], ACT.Sqrt), t)
            return t

        def transposed(src, gain, toff=0, shift=None, banks=(4, 5, 6, 7), after=()):
            tok, lows = None, []
            for j in range(4):
                bk = PB[banks[j]]
                tp = P([(lambda j, k, b, bk: lambda e: e.transpose(
                    bk[:, k * 256 + b * 128:k * 256 + b * 128 + 128],
                    src[:, b, (2 * j + k) * 128:(2 * j + k + 1) * 128], IDENT))(j, k, b, bk)
                    for k in range(2) for b in range(2)], *after)
                for k in range(2):
                    kc = 2 * j + k
                    hd, ld = HTH[:, kc, toff:toff + 256], HTL[:, kc, toff:toff + 256]
                    ps = bk[:, k * 256:k * 256 + 256]
                    g = 1.0 if gain is None else gain(kc)
                    if shift is None:
                        th = S((lambda hd, ps, g: lambda e: e.activation(hd, ps, ACT.Copy, scale=g))(hd, ps, g),
                               tp, *after, free=True)
                    else:
                        y = HTF[:, 4096 + kc * 512 + toff:4096 + kc * 512 + toff + 256]
                        ty = V((lambda y, ps, kc, g: lambda e: e.tensor_scalar(y, ps, g, shift(kc), ALU.mult,
                                                                              ALU.add))(y, ps, kc, g), tp,
                               free=True)
                        th = S((lambda y, hd: lambda e: e.activation(hd, y, ACT.Copy))(y, hd), ty, *after,
                               free=True)
                        lows.append((y, hd, ld, th))
                while len(lows) > (0 if j == 3 else 2):
                    y, hd, ld, th = lows.pop(0)
                    tok = V((lambda y, hd, ld: lambda e: e.tensor_tensor(ld, y, hd.bitcast(F32),
                                                                        ALU.subtract))(y, hd, ld), th, free=True)
                if shift is None:
                    for k in range(2):
                        kc = 2 * j + k
                        hd, ld = HTH[:, kc, toff:toff + 256], HTL[:, kc, toff:toff + 256]
                        ps = bk[:, k * 256:k * 256 + 256]
                        g = 1.0 if gain is None else gain(kc)
                        tok = V((lambda hd, ld, ps, g: lambda e: e.scalar_tensor_tensor(
                            ld, ps, g, hd.bitcast(F32), ALU.mult, ALU.subtract))(hd, ld, ps, g), th, free=True)
            return tok

        def normed(hn, src, *after):
            t = rstd([src[:, b, :] for b in range(2)], 1024, SM[:, 0:2],
                     HTF[:, 0:1024] if hn is src else hn.rearrange("p b n -> p (b n)"), *after)
            return (V(lambda e: e.tensor_scalar(hn[:, 0, :], src[:, 0, :], SM[:, 0:1], None, ALU.mult), t),
                    S(lambda e: e.activation(hn[:, 1, :], src[:, 1, :], ACT.Copy, scale=SM[:, 1:2]), V.now()))

        def halves(src, dst_h, dst_l, *after):
            V(lambda e: e.tensor_copy(dst_h, src), *after)
            return V(lambda e: e.tensor_tensor(dst_l, src, dst_h.bitcast(F32), ALU.subtract))

        GA = SM[:, 160:208].rearrange("p (s k) -> p s k", s=6)
        MODS = {(0, 1): 0, (0, 2): 6, (1, 1): 12, (1, 2): 18}

        def plan_ffn(l, which):
            wg, wu, wd = (A[f"ffn{which}_w_{x}"][l] for x in ("gate", "up", "down"))
            wg = wg.rearrange("(k p) n -> p k n", p=128)
            wu = wu.rearrange("(k p) n -> p k n", p=128)
            wd = wd.rearrange("(f p) n -> p f n", p=128)
            wm = A["w_mod_2"][0].rearrange("(k p) n -> p k n", p=128)
            for j in range(11):
                phase = (l, which) if j > 1 else False
                plan(wg[:, :, j * 256:(j + 1) * 256], 8, 256, wide=phase)
                plan(wu[:, :, j * 256:(j + 1) * 256], 8, 256, wide=phase)
                if 3 <= j < 9:
                    m = MODS[l, which] + j - 3
                    plan(wm[:, :, m * 256:(m + 1) * 256], 8, 256, split=False, wide=phase)
                plan(wd[:, 2 * j:2 * j + 2, :], 2, 1024, wide=phase)

        def modulation(t, m, w, acc):
            a = acc[:, w, :]
            V(lambda e: e.tensor_scalar(a, t.raw[:, 0, :], COND[:, w, 0:1], None, ALU.mult), t.ready, PE.now())
            for k in range(1, 8):
                V((lambda k: lambda e: e.scalar_tensor_tensor(a, t.raw[:, k, :], COND[:, w, k:k + 1], a,
                                                             ALU.mult, ALU.add))(k))
            if w == (m < 8):
                t.free(V.now())
            return [mm(PB[7][:, 2 * w + h:2 * w + h + 1], a[:, h * 128:(h + 1) * 128], ONES[:, 0:1])
                    for h in range(2)], V.now(), m, w

        def modulation_out(ops, tv, m, w, *after):
            tk = P(ops, tv, *after)
            V(lambda e: e.tensor_tensor(MODC[:, 48 * w + 2 * m:48 * w + 2 * m + 2], PB[7][:, 2 * w:2 * w + 2],
                                        COLS[:, 128 + 2 * m:130 + 2 * m], ALU.add), tk)

        def ffn(l, which):
            reg = Region(BIG, 0, BIGN)
            hn, sg, pr, acc = reg(2, 1024), reg(3, 256), reg(3, 256), reg(2, 256)
            ah = Region(BIGR, reg.at, BIGN)(3, 256)
            al = Region(BIGR, reg.at + 768, BIGN)(3, 256)
            name = f"ffn{which}_norm"
            assert reg.at + 1536 <= XAT
            now = barrier()
            extra[l, which] = tuple(now)
            loads()
            context = (l, which) == (1, 2)
            if context:
                cx = Region(BIG, reg.at + 1536, XAT)
                CX, junk = cx(2, 1024), cx(1024)
                c2 = load_once("c2", CX, A["ctx_2"].rearrange("o (b p) n -> p (o b) n", p=128), *now)
                gn = COLS[:, COL["norm1_g_2"]:COL["norm1_g_2"] + 8]
            t = normed(hn, X, V.now())
            ready = transposed(hn, lambda kc: col(name, l * 8 + kc), after=t)
            ta, tdown, td = {}, {}, {}
            AH = 2
            pend = None

            def down(f):
                w = td[f // 2]
                c = f % 3
                ops = []
                for b in range(2):
                    s = slice(b * 128, (b + 1) * 128)
                    for h in range(2):
                        q = slice(h * 512, (h + 1) * 512)
                        ops += mm3(PB[2 * b + h][:, :], [(ah[:, c, s], al[:, c, s])],
                                   [(w.h[:, f % 2, q], w.l[:, f % 2, q])], f == 0, f == 21)
                tdown[f] = P(ops, ta[f], w.ready)
                if f % 2:
                    w.free(tdown[f])

            tg = {}
            for f in range(22):
                c = f % 3
                if f % 2 == 0:
                    ws = [need(AH), need(AH)]
                bank = PB[4 + c]
                for s_ in range(2):
                    w = ws[s_]
                    q = slice((f % 2) * 128, (f % 2 + 1) * 128)
                    tk = P(mm3(bank[:, s_ * 256:(s_ + 1) * 256], [(w.h[:, k, q], w.l[:, k, q]) for k in range(8)],
                               [(HTH[:, k, 0:256], HTL[:, k, 0:256]) for k in range(8)]),
                           ready, w.ready, *([tg[f - 3]] if f >= 3 else []))
                    if f % 2:
                        w.free(tk)
                kc = f - 5
                if context and 0 <= kc < 8:
                    tc = P([(lambda kc, b: lambda e: e.transpose(
                        PB[7][:, 256 + b * 128:384 + b * 128], CX[:, b, kc * 128:(kc + 1) * 128], IDENT))(kc, b)
                        for b in range(2)], tcx, V.now())
                ts = S((lambda c, bank: lambda e: e.activation(sg[:, c, :], bank[:, 0:256], ACT.Silu))(c, bank),
                       tk, *([ta[f - 3]] if f >= 3 else []), free=True)
                tg[f] = V((lambda c, bank: lambda e: e.tensor_tensor(pr[:, c, :], bank[:, 256:512], sg[:, c, :],
                                                                    ALU.mult))(c, bank), ts)
                ta[f] = halves(pr[:, c, :], ah[:, c, :], al[:, c, :], *([tdown[f - 3]] if f >= 3 else []))
                if context and 0 <= kc < 8:
                    hd, y = (m[:, kc * 512 + 256:kc * 512 + 512] for m in (HTR, HTF[:, 4096:8192]))
                    ld = HTR[:, 4096 + kc * 512 + 256:4096 + kc * 512 + 512]
                    tcx = V((lambda y, kc: lambda e: e.tensor_scalar(
                        y, PB[7][:, 256:512], GA[:, 2, kc:kc + 1], GA[:, 3, kc:kc + 1], ALU.mult,
                        ALU.add))(y, kc), tc)
                    V((lambda hd, y: lambda e: e.tensor_copy(hd, y))(hd, y))
                    V((lambda ld, hd, y: lambda e: e.tensor_tensor(ld, y, hd.bitcast(F32), ALU.subtract))(ld, hd, y))
                if context and f == 3:
                    V(lambda e: e.scalar_tensor_tensor(GA[:, 2, :], MODC[:, 56:64], 1.0, gn, ALU.add, ALU.mult))
                    V(lambda e: e.tensor_copy(GA[:, 3, :], MODC[:, 48:56]))
                    tcx = rstd([CX[:, b, :] for b in range(2)], 1024, SM[:, 2:4], junk, c2)
                    V.wait(c2)
                if context and f == 4:
                    for b in range(2):
                        tcx = V((lambda b: lambda e: e.tensor_scalar(CX[:, b, :], CX[:, b, :], SM[:, 2 + b:3 + b],
                                                                    None, ALU.mult))(b), tcx)
                if f >= 1:
                    down(f - 1)
                if pend is not None:
                    modulation_out(*pend, *([tcx] if context and kc >= 0 else []))
                    pend = None
                if f % 2 == 0:
                    j = f // 2
                    if 3 <= j < 9:
                        tm, m = need(AH), MODS[l, which] + j - 3
                        pend = modulation(tm, m, 0, acc)
                    td[j] = need(AH)
                elif 3 <= f // 2 < 9 and m < 8:
                    pend = modulation(tm, m, 1, acc)
            down(21)
            for b in range(2):
                for h in range(2):
                    xv = X[:, b, h * 512:(h + 1) * 512]
                    V((lambda b, h, xv: lambda e: e.scalar_tensor_tensor(xv, PB[2 * b + h][:, :], 0.5, xv,
                                                                         ALU.mult, ALU.add))(b, h, xv),
                      tdown[21])

        def rope(x, nh, d, b, off, t1, t2):
            h = d // 2
            C = ROPE[:, b, off:off + d].unsqueeze(1).broadcast_to([128, nh, d])
            S1 = ROPE[:, b, off + d:off + d + h].unsqueeze(1).broadcast_to([128, nh, h])
            S2 = ROPE[:, b, off + d + h:off + 2 * d].unsqueeze(1).broadcast_to([128, nh, h])
            t1 = t1[:, 0:nh * d].rearrange("p (n d) -> p n d", d=d)
            t2 = t2[:, 0:nh * d].rearrange("p (n d) -> p n d", d=d)
            V(lambda e: e.tensor_tensor(t1, x, C, ALU.mult))
            V(lambda e: e.tensor_tensor(t2[:, :, 0:h], x[:, :, h:d], S1, ALU.mult), free=True)
            V(lambda e: e.tensor_tensor(t2[:, :, h:d], x[:, :, 0:h], S2, ALU.mult), free=True)
            return V(lambda e: e.tensor_tensor(x, t1, t2, ALU.add))

        def transposes(jobs, banks, after):
            toks = []
            bank_free = {}
            for g in range(0, len(jobs), 4):
                bk = banks[(g // 4) % len(banks)]
                part = jobs[g:g + 4]
                ops = []
                for i, (dst, src) in enumerate(part):
                    m, n = dst.shape[0], src.shape[0]
                    ops.append((lambda i, src, m, n, bk: lambda e: e.transpose(
                        PB[bk][0:m, i * 128:i * 128 + n], src, IDENT[0:n, 0:n]))(i, src, m, n, bk))
                tp = P(ops, *after, *bank_free.get(bk, ()))
                got = []
                for i, (dst, src) in enumerate(part):
                    m, n = dst.shape[0], src.shape[0]
                    q = (S, V)[(g // 4) % 2]
                    if q is S:
                        fn = (lambda i, dst, m, n, bk: lambda e: e.activation(
                            dst, PB[bk][0:m, i * 128:i * 128 + n], ACT.Copy))(i, dst, m, n, bk)
                    else:
                        fn = (lambda i, dst, m, n, bk: lambda e: e.tensor_copy(
                            dst, PB[bk][0:m, i * 128:i * 128 + n]))(i, dst, m, n, bk)
                    got.append(q(fn, tp, *after, free=True))
                bank_free[bk] = tuple(got)
                toks += got
            return (S.now(), V.now())

        def turned(groups, banks, after):
            free = {}
            for g, (dst, srcs) in enumerate(groups):
                bk = banks[g % len(banks)]
                ops, w = [], 0
                for src in srcs:
                    n, m = src.shape
                    ops.append((lambda w, src, m, n, bk: lambda e: e.transpose(
                        PB[bk][0:m, w:w + n], src, IDENT[0:n, 0:n]))(w, src, m, n, bk))
                    w += n
                tp = P(ops, *after, *free.get(bk, ()))
                ps = PB[bk][0:m, 0:w]
                if g % 2:
                    t = V((lambda dst, ps: lambda e: e.tensor_copy(dst, ps))(dst, ps), tp, free=True)
                else:
                    t = S((lambda dst, ps: lambda e: e.activation(dst, ps, ACT.Copy))(dst, ps), tp, free=True)
                free[bk] = (t,)
            return (S.now(), V.now())

        def attend(units, pb, pt, rs, ready, pieces):
            n = len(units)
            t1, tmx, tex, ttr, tev, to, tdst = {}, {}, {}, {}, {}, {}, {}
            for i in range(n + 3):
                if i < n:
                    q, k, extra, vs, dst, scale, late = units[i]
                    nk = k.shape[-1]
                    ps = PB[i % 4]
                    ops = [mm(ps[:, 0:nk], q, k, True, not extra)]
                    for x, (a, b_, l_, r_) in enumerate(extra):
                        ops.append(mm(ps[:, a:b_], l_, r_, False, x == len(extra) - 1))
                    t1[i] = P(ops, *ready, *late(), *([tex[i - 4]] if i >= 4 else []))
                    m = rs[:, (i % 4) * 4:(i % 4) * 4 + 4]
                    tr = V((lambda ps, m, nk: lambda e: e.tensor_reduce(m[:, 0:1], ps[:, 0:nk], AX.X, ALU.max,
                                                                       negate=True))(ps, m, nk), t1[i],
                           *([tex[i - 4]] if i >= 4 else []), free=True)
                u = i - 3
                if 0 <= u < n:
                    vs, dst = units[u][3], units[u][4]
                    po = PB[6 + u % 2][:, 0:64]
                    ops = [mm(po, pt[:, u % 2, kb * 128:(kb + 1) * 128], v, kb == 0, kb == len(vs) - 1)
                           for kb, v in enumerate(vs)]
                    to[u] = P(ops, tev[u], *([tdst[u - 2]] if u >= 2 else []))
                    mu = rs[:, (u % 4) * 4:(u % 4) * 4 + 4]
                    trc = V((lambda m: lambda e: e.reciprocal(m[:, 3:4], m[:, 2:3]))(mu), tex[u],
                            *([tdst[u - 4]] if u >= 4 else []), free=True)
                if i < n:
                    tmx[i] = V((lambda m, scale: lambda e: e.tensor_scalar(m[:, 1:2], m[:, 0:1], scale, None,
                                                                          ALU.mult))(m, scale), tr, free=True)
                    tex[i] = S((lambda ps, m, nk, i, scale: lambda e: e.activation(
                        pb[:, i % 4, 0:nk], ps[:, 0:nk], ACT.Exp, bias=m[:, 1:2], scale=scale,
                        accum_out=m[:, 2:3]))(ps, m, nk, i, scale), tmx[i],
                        *([ttr[i - 4], tdst[i - 4]] if i >= 4 else []), free=True)
                if 0 <= u < n:
                    tdst[u] = V((lambda m, dst, po: lambda e: e.tensor_scalar(dst, po, m[:, 3:4], None,
                                                                            ALU.mult))(mu, dst, po), to[u], trc,
                                free=True)
                u = i - 2
                if 0 <= u < n:
                    nb = units[u][1].shape[-1] // 128
                    bk = PB[4 + u % 2]
                    ops = [(lambda kb, bk, u: lambda e: e.transpose(bk[:, kb * 128:(kb + 1) * 128],
                                                                  pb[:, u % 4, kb * 128:(kb + 1) * 128],
                                                                  IDENT))(kb, bk, u) for kb in range(nb)]
                    ttr[u] = P(ops, tex[u], *([tev[u - 2]] if u >= 2 else []))
                    q_ = (S, V)[u % 2]
                    if q_ is S:
                        fn = (lambda bk, u, nb: lambda e: e.activation(pt[:, u % 2, 0:nb * 128], bk[:, 0:nb * 128],
                                                                      ACT.Copy))(bk, u, nb)
                    else:
                        fn = (lambda bk, u, nb: lambda e: e.tensor_copy(pt[:, u % 2, 0:nb * 128],
                                                                       bk[:, 0:nb * 128]))(bk, u, nb)
                    tev[u] = q_(fn, ttr[u], *([to[u - 2]] if u >= 2 else []), free=True)
                if pieces:
                    pieces.pop(0)()
            return V.now()

        def plan_hybrid(l):
            wv = A["w_in"][l].rearrange("(k p) n -> p k n", p=128)
            for j in range(10, -1, -1):
                plan(wv[:, :, j * 280:(j + 1) * 280], 8, 280)
                if j == 5:
                    plan(A["c_w_uq"][l].rearrange("(k p) n -> p k n", p=128), 3, 480)
                    plan(A["c_w_ukv"][l].rearrange("(k p) n -> p k n", p=128), 2, 640)
            plan_out(A["w_out"][l])

        def hybrid(l):
            c = Region(BIG, 0, BIGN)
            H = c(2, 3080)
            hn = c(2, 1024)
            WB = c(6, 256)
            lt = Region(BIG, c.at, c.at + 2560)
            LTH = Region(BIGR, c.at, BIGN)(5, 256)
            LTL = Region(BIGR, c.at + 1280, BIGN)(5, 256)
            c.at += 2560
            ln = c(2, 640)
            QC, KV, KC = c(2, 480), c(2, 640), c(2, 480)
            IQT, IKT = c(2, 256), c(256)
            QV = QC.rearrange("p b (h d) -> p b h d", d=96)
            KVV = KV.rearrange("p b (h d) -> p b h d", d=128)
            KCV = KC.rearrange("p b (h d) -> p b h d", d=96)
            tmp = Region(BIG, 6160, 6160 + 2048)
            t1, t2, IK = tmp(640), tmp(640), tmp(2, 4, 32)
            now = barrier()
            lb = load_once("bias", WB, A["c_relw"][l], *now)
            t = normed(hn, X, V.now())
            ready = transposed(hn, lambda kc: col("mix_norm", l * 8 + kc), after=t)
            W = 280
            prev = {}
            tok = {}

            def latent_norms():
                V.wait(S.now())
                junk = ln.rearrange("p b n -> p (b n)")
                rstd([H[:, b, 2408:2792] for b in range(2)], 384, SM[:, 0:2], junk, V.now())
                t = rstd([H[:, b, 2792:3048] for b in range(2)], 256, SM[:, 2:4], junk, V.now())
                for b in range(2):
                    V((lambda b: lambda e: e.tensor_scalar(ln[:, b, 0:384], H[:, b, 2408:2792], SM[:, b:b + 1], None,
                                                          ALU.mult))(b), t)
                    V((lambda b: lambda e: e.tensor_scalar(ln[:, b, 384:640], H[:, b, 2792:3048], SM[:, 2 + b:3 + b],
                                                          None, ALU.mult))(b), free=True)
                tok["ln"] = V.now()

            def index_positions():
                V.wait(S.now(), PE.now())
                for b in range(2):
                    rope(H[:, b, 2112:2400].rearrange("p (n d) -> p n d", d=32), 9, 32, b, 128, t1, t2)
                    rope(H[:, b, 3048:3080].rearrange("p (n d) -> p n d", d=32), 1, 32, b, 128, t1, t2)
                for b in range(2):
                    V((lambda b: lambda e: e.tensor_copy(
                        IK[:, b, :, :], H[:, b, 2368:2400].unsqueeze(1).broadcast_to([128, 4, 32])))(b))
                tok["index"] = V.now()

            def latent_halves():
                tp = []
                for k in range(5):
                    tp.append(P([(lambda k, b: lambda e: e.transpose(
                        PB[4 + k // 2][:, (k % 2) * 256 + b * 128:(k % 2) * 256 + (b + 1) * 128],
                        ln[:, b, k * 128:(k + 1) * 128], IDENT))(k, b) for b in range(2)], tok["ln"], ready))
                for k in range(5):
                    g = col("c_q_norm", l * 3 + k) if k < 3 else col("c_kv_norm", l * 2 + k - 3)
                    ps = PB[4 + k // 2][:, (k % 2) * 256:(k % 2) * 256 + 256]
                    th = V((lambda k, g, ps: lambda e: e.tensor_scalar(LTH[:, k, :], ps, g, None, ALU.mult))(k, g, ps),
                           tp[-1], free=True)
                for k in range(5):
                    g = col("c_q_norm", l * 3 + k) if k < 3 else col("c_kv_norm", l * 2 + k - 3)
                    ps = PB[4 + k // 2][:, (k % 2) * 256:(k % 2) * 256 + 256]
                    tok["lt"] = V((lambda k, g, ps: lambda e: e.scalar_tensor_tensor(
                        LTL[:, k, :], ps, g, LTH[:, k, :].bitcast(F32), ALU.mult, ALU.subtract))(k, g, ps), th,
                        free=True)

            def index_columns():
                tok["iqt"] = turned(
                    [(IQT.rearrange("p k n -> p (k n)"),
                      [H[:, b, 2112 + k * 128:2112 + (k + 1) * 128] for k in range(2) for b in range(2)]),
                     (IKT, [IK[:, b, :, :].rearrange("p r d -> p (r d)") for b in range(2)])],
                    [7, 4], (tok["index"], tok["lt"]))

            def latent_heads():
                wq, wk = need(), need()
                for b in range(2):
                    s = slice(b * 128, (b + 1) * 128)
                    tk = P(mm3(PB[5 + b][:, 0:480], [(LTH[:, k, s], LTL[:, k, s]) for k in range(3)],
                               [(wq.h[:, k, :], wq.l[:, k, :]) for k in range(3)]), wq.ready, tok["lt"], *tok["iqt"])
                    V((lambda b: lambda e: e.tensor_copy(QC[:, b, :], PB[5 + b][:, 0:480]))(b), tk)
                te = {}
                for b in range(2):
                    s = slice(b * 128, (b + 1) * 128)
                    for h in range(2):
                        q = slice(h * 320, (h + 1) * 320)
                        bank = PB[(7, 4)[h]]
                        tk2 = P(mm3(bank[:, 0:320], [(LTH[:, 3 + k, s], LTL[:, 3 + k, s]) for k in range(2)],
                                    [(wk.h[:, k, q], wk.l[:, k, q]) for k in range(2)]), wk.ready,
                                *([te[h]] if b else []))
                        te[h] = S((lambda b, h, bank: lambda e: e.activation(
                            KV[:, b, h * 320:(h + 1) * 320], bank[:, 0:320], ACT.Copy))(b, h, bank), tk2, free=True)
                wq.free(tk)
                wk.free(tk2)
                tok["kv"] = S.now(), V.now(), tk2

            def latent_positions():
                for b in range(2):
                    G((lambda b: lambda e: e.tensor_copy(KCV[:, b, :, 0:64], KVV[:, b, :, 0:64]))(b), *tok["kv"])
                    G((lambda b: lambda e: e.tensor_copy(
                        KCV[:, b, :, 64:96], H[:, b, 3048:3080].unsqueeze(1).broadcast_to([128, 5, 32])))(b))
                    rope(QV[:, b, :, 64:96], 5, 32, b, 128, t1, t2)

            WI = SM[:, 16:32].rearrange("p (b h) -> p b h", b=2)
            SCR, WRK, SEL, TMP = lt(2, 256), lt(2, 256), lt(2, 256), lt(2, 256)
            M8 = SM[:, 32:48].rearrange("p (b m) -> p b m", b=2)

            def index_scores(b):
                nk = 128 * (b + 1)
                where = [PB[4 + h % 4][:, (h // 4) * 256:(h // 4) * 256 + nk] for h in range(8)]
                tp = P([mm(where[h], IQT[32 * (h % 4):32 * (h % 4) + 32, h // 4, b * 128:(b + 1) * 128],
                           IKT[32 * (h % 4):32 * (h % 4) + 32, 0:nk]) for h in range(8)],
                       *tok["iqt"], *tok["kv"], V.now())
                if b == 1:
                    V(lambda e: e.tensor_scalar(WI, H[:, :, 2400:2408], float(8 ** -0.5 * 32 ** -0.5), None,
                                                ALU.mult), *tok["kv"])
                dst = SCR[:, b, 0:nk]
                V(lambda e: e.tensor_scalar(dst, where[0], 0.0, WI[:, b, 0:1], ALU.max, ALU.mult), tp)
                ta = tw = V.now()
                ts = {}
                for h in range(1, 9):
                    if h < 8:
                        x = TMP[:, h % 2, 0:nk]
                        ts[h] = V((lambda h, x: lambda e: e.tensor_scalar(
                            x, where[h], 0.0, WI[:, b, h:h + 1], ALU.max, ALU.mult))(h, x),
                            ts.get(("a", h - 2), tw), free=True)
                    if h > 1:
                        x = TMP[:, (h - 1) % 2, 0:nk]
                        ta = ts["a", h - 1] = V((lambda x: lambda e: e.tensor_tensor(dst, dst, x, ALU.add))(x),
                                                ts[h - 1], ta, free=True)
                V(lambda e: e.memset(SCR[0:64, b, nk - 64:nk], NEG))

            lane = {}

            def selection(first, count):
                for b in range(2):
                    if first == 0:
                        lane[b] = V.now()
                for r_ in range(first, first + count):
                    for step in range(2):
                        for b in range(2):
                            nk = 128 * (b + 1)
                            src, m8, wrk = (SCR if r_ == 0 else WRK)[:, b, 0:nk], M8[:, b, :], WRK[:, b, 0:nk]
                            if step == 0:
                                fn = (lambda m8, src: lambda e: e.max(m8, src))(m8, src)
                            else:
                                fn = (lambda m8, src, wrk: lambda e: e.match_replace(wrk, m8, src, LOW))(m8, src, wrk)
                            lane[b] = V(fn, lane[b], free=True)
                if first + count == 8:
                    for b in range(2):
                        nk = 128 * (b + 1)
                        V((lambda b, nk: lambda e: e.tensor_scalar(SEL[:, b, 0:nk], WRK[:, b, 0:nk], -2e38, NEG,
                                                                  ALU.is_gt, ALU.mult))(b, nk))
                    tok["sel"] = V.now()

            def head_positions():
                for b in range(2):
                    rope(H[:, b, 1152:1792].rearrange("p (n d) -> p n d", d=64), 10, 64, b, 0, t1, t2)

            rounds = [lambda r_=r_: selection(r_, 1) for r_ in range(8)]
            beside = {3: [latent_norms], 4: [index_positions], 5: [latent_halves, index_columns],
                      7: [lambda: index_scores(1)],
                      8: [lambda: index_scores(0)],
                      9: [lambda: V.wait(S.now()), head_positions], 10: [rounds.pop(0) for _ in range(2)]}
            n = 0
            for p, j in enumerate(range(10, -1, -1)):
                w = need()
                for f in beside.get(p, ()):
                    f()
                for b in range(2):
                    bank = PB[n % 4]
                    s = slice(b * 128, (b + 1) * 128)
                    tk = P(mm3(bank[:, 0:W], [(HTH[:, k, s], HTL[:, k, s]) for k in range(8)],
                               [(w.h[:, k, :], w.l[:, k, :]) for k in range(8)]),
                           ready, w.ready, *([prev[n - 4]] if n >= 4 else []))
                    dst = H[:, b, j * W:(j + 1) * W]
                    prev[n] = S((lambda dst, bank: lambda e: e.activation(dst, bank[:, 0:W], ACT.Copy))(dst, bank),
                                tk, free=True)
                    n += 1
                w.free(tk)
                if p == 5:
                    latent_heads()
                if p == 6:
                    latent_positions()
            dump(f"H{l}", H, V.now(), S.now())
            O = hn
            ht = Region(HTF, 0, 8192)
            AQ, AK, BQ, BK = ht(3, 256), ht(3, 256), ht(3, 256), ht(3, 256)
            CQ, CK = ht(5, 256), ht(5, 256)
            groups = []
            for dst, base, w in ((AQ, 0, 384), (AK, 384, 384), (BQ, 1152, 320), (BK, 1472, 320)):
                for k0, k1 in ((0, 2), (2, 3)):
                    m = min(128, w - k0 * 128)
                    groups.append((dst[0:m, k0:k1, :].rearrange("p k n -> p (k n)"),
                                   [H[:, b, base + k * 128:base + k * 128 + m]
                                    for k in range(k0, k1) for b in range(2)]))
            for dst, src in ((CQ, QC), (CK, KC)):
                for h0, h1 in ((0, 2), (2, 4), (4, 5)):
                    groups.append((dst[0:96, h0:h1, :].rearrange("p k n -> p (k n)"),
                                   [src[:, b, h * 96:(h + 1) * 96] for h in range(h0, h1) for b in range(2)]))
            S.wait(PE.now(), V.now())
            V.wait(PE.now())
            tt = turned(groups, list(range(8)), (V.now(), S.now(), G.now()))
            pb = ln.rearrange("p b n -> p (b n)")[:, 0:1024].rearrange("p (a n) -> p a n", a=4)
            pt = KC.rearrange("p b n -> p (b n)")[:, 0:512].rearrange("p (a n) -> p a n", a=2)
            rs = SM[:, 48:64]
            units = []
            for h in range(6):
                for b in range(2):
                    nk = 128 * (b + 1)
                    r0 = 64 * (h % 2)
                    vs = [H[:, kb, 768 + h * 64:768 + (h + 1) * 64] for kb in range(b + 1)]
                    units.append((AQ[r0:r0 + 64, h // 2, b * 128:(b + 1) * 128], AK[r0:r0 + 64, h // 2, 0:nk],
                                  [(0, nk, J8, WB[:, h, 128 * (1 - b):256]), (nk - 64, nk, HALF[:, :], NROW[:, :])],
                                  vs, O[:, b, h * 64:(h + 1) * 64], 0.125, lambda: ()))
            for h in range(5):
                for b in range(2):
                    nk = 128 * (b + 1)
                    vs = [KVV[:, kb, h, 64:128] for kb in range(b + 1)]
                    units.append((CQ[0:96, h, b * 128:(b + 1) * 128], CK[0:96, h, 0:nk],
                                  [(nk - 64, nk, HALF[:, :], NROW[:, :])],
                                  vs, O[:, b, 704 + h * 64:704 + (h + 1) * 64], float(96 ** -0.5), lambda: ()))
            for h in range(5):
                for b in range(2):
                    nk = 128 * (b + 1)
                    r0 = 64 * (h % 2)
                    vs = [H[:, kb, 1792 + h * 64:1792 + (h + 1) * 64] for kb in range(b + 1)]
                    units.append((BQ[r0:r0 + 64, h // 2, b * 128:(b + 1) * 128], BK[r0:r0 + 64, h // 2, 0:nk],
                                  [(0, nk, IDENT, SEL[:, b, 0:nk])],
                                  vs, O[:, b, 384 + h * 64:384 + (h + 1) * 64], 0.125, lambda: (tok["sel"],)))
            V.wait(*tt)
            S.wait(*tt)
            attend(units, pb, pt, rs, [lb, *tt], rounds)
            barrier()
            dump(f"O{l}", O, V.now())
            project_out(O, None)
            dump(f"X{l}", X[:, :, :], V.now())

        def plan_out(w, slots=NS):
            wv = w.rearrange("(k p) n -> p k n", p=128)
            for j in range(4):
                plan(wv[:, :, j * 256:(j + 1) * 256], 8, 256, slots=slots)

        def project_out(O, gate, gains=None):
            ready = transposed(O, gains, banks=(0, 1, 2, 3))
            n = 0
            prev = {}
            for j in range(4):
                w = need()
                for b in range(2):
                    bank = PB[4 + n % 4]
                    s = slice(b * 128, (b + 1) * 128)
                    tk = P(mm3(bank[:, 0:256], [(HTH[:, k, s], HTL[:, k, s]) for k in range(8)],
                               [(w.h[:, k, :], w.l[:, k, :]) for k in range(8)]),
                           ready, w.ready, *([prev[n - 4]] if n >= 4 else []))
                    xv = X[:, b, j * 256:(j + 1) * 256]
                    if gate is not None:
                        gv = gate[:, j * 256:(j + 1) * 256]
                        V((lambda bank, gv: lambda e: e.tensor_tensor(bank[:, 0:256], bank[:, 0:256], gv,
                                                                     ALU.mult))(bank, gv), tk)
                    prev[n] = V((lambda bank, xv: lambda e: e.tensor_tensor(xv, xv, bank[:, 0:256],
                                                                          ALU.add))(bank, xv), tk)
                    n += 1
                w.free(tk)

        def second():
            barrier()
            reg = Region(BIG, 0, BIGN)
            G1, G2 = reg(1024), reg(1024)
            at_a = reg.at
            hn = reg(2, 1024)
            reg.at = at_a + 3072
            FG = Region(BIG, reg.at, BIGN)(1024)
            now = V.now(), S.now(), PE.now(), G.now()
            fg = load_once("fg", FG, A["final_norm"].partition_broadcast(128), *now)
            for s, (sc, sh, name) in ((0, (8, 0, "norm1_g_2")), (2, (32, 24, "norm2_g_2"))):
                gn = COLS[:, COL[name]:COL[name] + 8]
                V((lambda s, sc, gn: lambda e: e.scalar_tensor_tensor(
                    GA[:, 2 * s, :], MODC[:, sc:sc + 8], 1.0, gn, ALU.add, ALU.mult))(s, sc, gn))
                V((lambda s, sh: lambda e: e.tensor_copy(GA[:, 2 * s + 1, :], MODC[:, sh:sh + 8]))(s, sh))
            tr = rstd([X[:, b, :] for b in range(2)], 1024, SM[:, 0:2], hn.rearrange("p b n -> p (b n)"), V.now())
            for b in range(2):
                V((lambda b: lambda e: e.scalar_tensor_tensor(X[:, b, :], X[:, b, :], SM[:, b:b + 1], FG,
                                                             ALU.mult, ALU.mult))(b), tr, fg)
            dump("XN", X[:, :, :], V.now())
            t = normed(hn, X, V.now())
            ready = transposed(hn, lambda kc: GA[:, 0, kc:kc + 1], shift=lambda kc: GA[:, 1, kc:kc + 1],
                               banks=(0, 1, 2, 3), after=t)
            QR, KR = Region(BIG, at_a, at_a + 3072)(4, 256), Region(BIG, at_a + 1024, at_a + 3072)(4, 512)
            QT, KT, KTOK = reg(4, 256), reg(4, 512), reg(4, 512)
            VA = reg(4, 4, 129)
            MO, GV, GR, GQ, GK = reg(2, 512), reg(4, 512), reg(2, 512), reg(2, 256), reg(2, 512)
            GLR = reg(512, parts=32)
            GT = SM[:, 0:64].rearrange("p (b g) -> p b g", b=4)
            barrier()
            V(lambda e: e.memset(VA[:, :, :, 128:129], 1.0))
            n = [0]
            prev = {}

            def project(prods, width, evac, arr, parts=128):
                m = n[0]
                bank = PB[m % 8]
                tk = P(mm3(bank[0:parts, 0:width], [p_[0] for p_ in prods], [p_[1] for p_ in prods]),
                       ready, arr, *([prev[m - 8]] if m >= 8 else []))
                q = (V, S)[m % 2]
                prev[m] = q(evac(q, bank[0:parts, 0:width]), tk, free=True)
                n[0] += 1
                return tk

            def copy_to(dst, scale=1.0):
                def evac(q, src):
                    if q is V:
                        return lambda e: e.tensor_scalar(dst, src, scale, None, ALU.mult)
                    return lambda e: e.activation(dst, src, ACT.Copy, scale=scale)
                return evac

            def features(w, c0, m, nt, dst, scale=1.0):
                return project([((w.h[:, k, c0:c0 + m], w.l[:, k, c0:c0 + m]), (HTH[:, k, 0:nt], HTL[:, k, 0:nt]))
                                for k in range(8)], nt, copy_to(dst, scale),
                               w.ready, parts=m)

            def tokens(w, c0, m, b, dst):
                s = slice(b * 128, (b + 1) * 128)
                return project([((HTH[:, k, s], HTL[:, k, s]), (w.h[:, k, c0:c0 + m], w.l[:, k, c0:c0 + m]))
                                for k in range(8)], m,
                               copy_to(dst) if len(dst.shape) == 2 else
                               (lambda q, src: copy_to(dst)(q, src.rearrange("p (h d) -> p h d", d=128))), w.ready)

            def spare(ops, evac, q, *after):
                m = n[0]
                n[0] += 1
                bank = PB[m % 8]
                tk = P(ops(bank), *after, *([prev[m - 8]] if m >= 8 else []))
                prev[m] = q(evac(bank), tk, free=True)

            dg = RAW[:, 4 * SLOT:4 * SLOT + 1024]

            def residual_gate(g_, c0):
                t = PE.now()
                for k in range(8):
                    t = S((lambda k: lambda e: e.activation(dg[:, k * 128:(k + 1) * 128], IDENT, ACT.Copy,
                                                           scale=MODC[:, c0 + k:c0 + k + 1]))(k), t, free=True)
                for h in range(2):
                    spare(lambda bank: [mm(bank[:, :], ONES[:, :], dg[:, h * 512:(h + 1) * 512])],
                          lambda bank: (lambda bank, h: lambda e: e.activation(
                              g_[:, h * 512:(h + 1) * 512], bank[:, :], ACT.Copy))(bank, h), S, S.now())

            cw = COL["ml_conv_w_2"]

            def convolved(x, h):
                src, dst, h0, nt = ((QR, QT, 0, 256), (KR, KT, 4, 512))[x]
                w0, w1, w2 = (COLS[:, cw + 8 * j + h0 + h:cw + 8 * j + h0 + h + 1] for j in range(3))
                u, y = src[:, h, :], dst[:, h, :]
                V.wait(S.now())
                V((lambda u, y, w1: lambda e: e.tensor_scalar(y, u, w1, None, ALU.mult))(u, y, w1))
                parts = [(u[:, 0:256].rearrange("p (r t) -> p r t", t=64),
                          y[:, 0:256].rearrange("p (r t) -> p r t", t=64), 64)]
                if nt == 512:
                    parts.append((u[:, 256:512].rearrange("p (r t) -> p r t", t=256),
                                  y[:, 256:512].rearrange("p (r t) -> p r t", t=256), 256))
                for uu, yy, m in parts:
                    for wc, a_, b_ in ((w0, slice(1, m), slice(0, m - 1)), (w2, slice(0, m - 1), slice(1, m))):
                        V((lambda uu, yy, wc, a_, b_: lambda e: e.scalar_tensor_tensor(
                            yy[:, :, a_], uu[:, :, b_], wc, yy[:, :, a_], ALU.mult, ALU.add))(uu, yy, wc, a_, b_))
                ts = S((lambda y: lambda e: e.activation(y, y, ACT.Silu))(y), V.now())
                return ts, y

            scaled = []

            def scale_keys():
                while scaled:
                    ts, y = scaled.pop(0)
                    V((lambda y: lambda e: e.tensor_scalar(y, y, float(128 ** -0.5), None, ALU.mult))(y), ts)

            def keys_by_token():
                for b in range(4):
                    spare(lambda bank: [(lambda h, b: lambda e: e.transpose(
                        bank[:, h * 128:(h + 1) * 128], KT[:, h, b * 128:(b + 1) * 128], IDENT))(h, b)
                        for h in range(4)],
                        lambda bank: (lambda bank, b: (lambda e: e.activation(KTOK[:, b, :], bank[:, :], ACT.Copy))
                                      if b % 2 else (lambda e: e.tensor_copy(KTOK[:, b, :], bank[:, :])))(bank, b),
                        (V, S)[b % 2], V.now())

            D64, W2 = Region(BIG, at_a, at_a + 512)(512), Region(BIG, at_a + 512, at_a + 1024)(512, parts=32)
            LA = shaped(HIF[:, 4 * SLOT:4 * SLOT + 2048], (2, 2, 512))
            BB = shaped(RAW[:, 4 * SLOT:4 * SLOT + 2048], (2, 2, 512))
            tw = []

            def gate_weights_in():
                tz = V(lambda e: e.memset(W2, 0.0))
                tw.append(load_once("d64", D64, A["c_cst2"][:, 1536:2048], tz))
                for d in range(2):
                    tl = load_once("lrw", W2[d * 16:(d + 1) * 16, d * 256:(d + 1) * 256],
                                   A["gla_lr_w2_2"][0, d], tz)
                tw.append(tl)

            def gate_inputs():
                V.wait(S.now(), PE.now())
                for d in range(2):
                    for f in range(2):
                        spare(lambda bank: [mm(bank[:, :], W2[:, d * 256 + f * 128:d * 256 + (f + 1) * 128], GLR)],
                              lambda bank: (lambda bank, d, f: lambda e: e.tensor_scalar(
                                  LA[:, d, f, :], bank[:, :], col("gla_alpha_b_2", 2 * d + f), None,
                                  ALU.add))(bank, d, f), V, V.now(), S.now(), *tw)
                S.wait(PE.now())
                S(lambda e: e.activation(BB, LA, ACT.Abs), V.now())
                gate_inputs.t = S(lambda e: e.activation(BB, BB, ACT.Exp, scale=-1.0))

            def gate_logs():
                V(lambda e: e.tensor_scalar(BB, BB, 1.0, None, ALU.add), gate_inputs.t)
                gate_logs.t = S(lambda e: e.activation(BB, BB, ACT.Ln), V.now())
                V(lambda e: e.tensor_scalar(LA, LA, 0.0, None, ALU.min))

            def gate_values():
                V(lambda e: e.tensor_tensor(LA, LA, BB, ALU.subtract), gate_logs.t)
                V(lambda e: e.tensor_scalar(LA, LA, 1.0 / 16, None, ALU.mult))

            def gate_sums():
                t = V.now()
                V.wait(*tw)
                for d in range(2):
                    for f in range(2):
                        V((lambda d, f: lambda e: e.tensor_tensor_scan(BB[:, d, f, :], D64, LA[:, d, f, :], 0.0,
                                                                      ALU.mult, ALU.add))(d, f), t, free=True)

            def gate_reversed():
                for f in range(2):
                    bv = BB[:, 1, f, :].rearrange("p (c t) -> p c t", t=64)
                    lv = LA[:, 1, f, :].rearrange("p (c t) -> p c t", t=64)
                    V((lambda bv, lv: lambda e: e.tensor_tensor(lv, lv, bv, ALU.subtract))(bv, lv))
                    V((lambda bv, lv: lambda e: e.tensor_tensor(
                        lv, lv, bv[:, :, 63:64].broadcast_to([128, 8, 64]), ALU.add))(bv, lv))
                    V((lambda f: lambda e: e.tensor_copy(BB[:, 1, f, :], LA[:, 1, f, :]))(f))

            for j in range(2):
                w = need()
                for k in range(2):
                    tk = features(w, k * 128, 128, 256, QR[:, 2 * j + k, :])
                w.free(tk)
            residual_gate(G1, 16)
            for j in range(2):
                w = need()
                for k in range(2):
                    tk = features(w, k * 128, 128, 512, KR[:, 2 * j + k, :])
                w.free(tk)
                convolved(0, 2 * j)
                convolved(0, 2 * j + 1)
            gate_weights_in()
            residual_gate(G2, 40)
            w = need()
            for b in range(2):
                tokens(w, 0, 232, b, GR[:, b, 280:512])
            tk = features(w, 232, 32, 512, GLR)
            w.free(tk)
            scaled.append(convolved(1, 0))
            w = need()
            for b in range(4):
                tokens(w, 0, 16, b, GT[:, b, :])
            gate_inputs()
            for k in range(2):
                tk = features(w, 16 + k * 128, 128, 256, GQ[:, k, :], 0.125)
            w.free(tk)
            scaled.append(convolved(1, 1))
            w = need()
            for k in range(2):
                tk = features(w, k * 128, 128, 512, GK[:, k, :])
            w.free(tk)
            gate_logs()
            scaled.append(convolved(1, 2))
            for j in range(2):
                w = need()
                for b in range(4):
                    tk = tokens(w, 0, 256, b, VA[:, b, 2 * j:2 * j + 2, 0:128])
                w.free(tk)
                if j == 0:
                    gate_values()
                    scaled.append(convolved(1, 3))
                else:
                    gate_sums()
            for j in range(2):
                w = need()
                for b in range(2):
                    tk = tokens(w, 0, 256, b, MO[:, b, j * 256:(j + 1) * 256])
                w.free(tk)
                (gate_reversed, scale_keys)[j]()
            for j in range(2):
                w = need()
                for b in range(4):
                    tk = tokens(w, 0, 256, b, GV[:, b, j * 256:(j + 1) * 256])
                w.free(tk)
                if j == 0:
                    keys_by_token()
            w = need()
            for b in range(2):
                tk = tokens(w, 0, 280, b, GR[:, b, 0:280])
            w.free(tk)
            t = barrier()
            C2 = HTF[:, 6128:8192]
            c2 = load_once("c2", C2, A["c_cst2"], *t)
            MASK = C2[:, 0:256].rearrange("p (d t) -> p d t", d=2)
            GM = C2[:, 256:512].rearrange("p (d t) -> p d t", d=2)
            D0, D1 = C2[0:8, 512:1024], C2[0:8, 1024:1536]
            V.wait(c2)
            PE.wait(c2)
            ts = S(lambda e: e.activation(GR, GR, ACT.Silu))
            ts = S(lambda e: e.activation(MO, MO, ACT.Sigmoid))
            tmp = Region(HTF, 0, 6128)
            GB = tmp(16)
            tb_ = load_once("gb", GB, A["ml_gate_b_2"][0].partition_broadcast(128), *t)
            GP = tmp(4, 4, 8)
            V(lambda e: e.tensor_tensor(GT, GT, GB.unsqueeze(1).broadcast_to([128, 4, 16]), ALU.add), tb_)
            V(lambda e: e.memset(GP, 0.0))
            for d in range(2):
                for q in range(2):
                    V((lambda d, q: lambda e: e.tensor_copy(GP[:, 2 * q + d, :, d * 4:d * 4 + 4],
                                                           GT[:, :, d * 8 + q * 4:d * 8 + q * 4 + 4]))(d, q))
            barrier()
            ORD = [[2, 3, 0, 1], [3, 2, 1, 0]]
            ops = []
            for q in range(2):
                for c in range(4):
                    o_ = PB[q][0:8, c * 128:(c + 1) * 128]
                    ops.append(mm(o_, GP[:, 2 * q, ORD[0][c], :], IDENT, True, False))
                    ops.append(mm(o_, GP[:, 2 * q + 1, ORD[1][c], :], J, False, True))
            tk = P(ops)
            rr = Region(BIG, at_a, at_a + 3072)
            RQ = rr(5, 4, 128, parts=8)
            Bc = rr(4, 128, parts=8)
            late = Region(HTF, 5000, 6128)
            CM, LF = late(4, 128, parts=8), late(4, 128, parts=8)
            fl = "p c t -> p (c t)"
            igp = PB[0][0:8, :]
            fp = PB[1][0:8, :]
            lf, bb, cm = LF.rearrange(fl), Bc.rearrange(fl), CM.rearrange(fl)
            S(lambda e: e.activation(lf, fp, ACT.Abs), tk, V.now())
            ts = S(lambda e: e.activation(lf, lf, ACT.Exp, scale=-1.0))
            V(lambda e: e.tensor_scalar(lf, lf, 1.0, None, ALU.add), ts)
            ts = S(lambda e: e.activation(lf, lf, ACT.Ln), V.now())
            V(lambda e: e.scalar_tensor_tensor(lf, fp, 0.0, lf, ALU.min, ALU.subtract), ts)
            V(lambda e: e.tensor_tensor_scan(bb, D0, lf, 0.0, ALU.mult, ALU.add))
            a_row = RQ[:, 0, :, :].rearrange(fl)
            V(lambda e: e.tensor_tensor(a_row, igp, bb, ALU.subtract))
            V(lambda e: e.tensor_tensor_scan(cm, D1, a_row, LOW, ALU.add, ALU.max))
            MM = SM[0:8, 208:216]
            V(lambda e: e.memset(MM[:, 0:1], 0.0))
            for c in range(4):
                V((lambda c: lambda e: e.tensor_scalar(MM[:, c + 1:c + 2], CM[:, c, 127:128], MM[:, c:c + 1],
                                                      Bc[:, c, 127:128], ALU.max, ALU.add))(c))
                V((lambda c: lambda e: e.tensor_scalar(CM[:, c, :], CM[:, c, :], MM[:, c:c + 1], None,
                                                      ALU.max))(c))
            V(lambda e: e.tensor_scalar(RQ[:, 1, :, :], CM, -1.0, None, ALU.mult))
            V(lambda e: e.tensor_tensor(LF, Bc, CM, ALU.add))
            S(lambda e: e.activation(RQ[:, 3, :, :], LF, ACT.Exp, scale=-1.0), V.now())
            for c in range(4):
                S((lambda c: lambda e: e.activation(RQ[:, 2, c, :], CM[:, c, :], ACT.Exp, scale=-1.0,
                                                   bias=MM[:, c:c + 1]))(c))
                S((lambda c: lambda e: e.activation(RQ[:, 4, c, :], RQ[:, 0, c, :], ACT.Exp,
                                                   bias=RQ[:, 1, c, 127:128]))(c))
            DG8 = tmp(4, 8, parts=8)
            for c in range(4):
                V((lambda c: lambda e: e.tensor_scalar(DG8[:, c, :], IDENT[0:8, 0:8], RQ[:, 2, c, 127:128], None,
                                                      ALU.mult))(c), S.now())
            DEC = tmp(32)
            ops = [(lambda c, q: lambda e: e.transpose(PB[2][:, (c * 5 + q) * 8:(c * 5 + q) * 8 + 8],
                                                      RQ[:, q, c, :], IDENT[0:8, 0:8]))(c, q)
                   for c in range(4) for q in range(5)]
            ops.append(mm(PB[3][:, 0:32], ONES[0:8, :], DG8.rearrange("p c r -> p (c r)")))
            tk = P(ops, V.now(), S.now())
            CP, NAT = tmp(4, 5, 8), tmp(4, 5, 8)
            V(lambda e: e.tensor_copy(CP.rearrange("p c q r -> p (c q r)"), PB[2][:, 0:160]), tk)
            V(lambda e: e.tensor_copy(DEC, PB[3][:, 0:32]))
            tk = P([mm(PB[4][:, 0:160], J, CP.rearrange("p c q r -> p (c q r)"))], V.now())
            nv = PB[4][:, 0:160].rearrange("p (c q r) -> p c q r", c=4, q=5)
            for c in range(4):
                V((lambda c: lambda e: e.tensor_copy(NAT[:, ORD[0][c], :, 0:4], CP[:, c, :, 0:4]))(c), tk)
                V((lambda c: lambda e: e.tensor_copy(NAT[:, ORD[1][c], :, 4:8], nv[:, c, :, 4:8]))(c))
            barrier()
            EE, ST, DGm = tmp(4, 128), tmp(4, 128), tmp(4, 128)
            CS = [tmp(4, 129), tmp(4, 129)]
            WVA = tmp(4, 129)
            PS1 = tmp(4, 129)
            RR = tmp(4, 129)
            HM = tmp(2, 4, 128)
            DN = SM[:, 216:224]

            def state(d, c):
                b = ORD[d][c]
                wc = NAT[:, b, 4, 4 * d:4 * d + 4].unsqueeze(2).broadcast_to([128, 4, 129])
                tw = V(lambda e: e.tensor_tensor(WVA, VA[:, b, :, :], wc, ALU.mult), PE.now())
                for p in range(2):
                    tk = P([mm(PB[p][:, h * 129:(h + 1) * 129], KTOK[:, b, (2 * p + h) * 128:(2 * p + h + 1) * 128],
                               WVA[:, 2 * p + h, :]) for h in range(2)], tw)
                    for h in range(2):
                        hh = 2 * p + h
                        src = PB[p][:, h * 129:(h + 1) * 129]
                        dst = CS[d][:, hh, :]
                        if c == 0:
                            V((lambda dst, src: lambda e: e.tensor_copy(dst, src))(dst, src), tk, tw, free=True)
                        else:
                            x = c * 8 + d * 4 + hh
                            V((lambda dst, src, x: lambda e: e.scalar_tensor_tensor(
                                dst, dst, DEC[:, x:x + 1], src, ALU.mult, ALU.add))(dst, src, x), tk, tw,
                              free=True)

            def outputs(d, c):
                b = ORD[d][c]
                s = slice(b * 128, (b + 1) * 128)
                gc = NAT[:, b, 1, 4 * d:4 * d + 4].unsqueeze(2).broadcast_to([128, 4, 128])
                tg = V(lambda e: e.tensor_tensor(DGm, IDENT.unsqueeze(1).broadcast_to([128, 4, 128]), gc,
                                                 ALU.mult), PE.now())
                te = P([mm(PB[2][:, :], ONES[:, :], DGm.rearrange("p h t -> p (h t)"), True, False)] +
                       [mm(PB[2][:, h * 128:(h + 1) * 128], IDENT, MASK[:, d, :], False, h == 3)
                        for h in range(4)], tg, S.now())
                for h in range(4):
                    S((lambda h: lambda e: e.activation(EE[:, h, :], PB[2][:, h * 128:(h + 1) * 128], ACT.Exp,
                                                       bias=NAT[:, b, 0, 4 * d + h:4 * d + h + 1]))(h), te, tg)
                tq = P([mm(PB[3][:, h * 128:(h + 1) * 128], KT[:, h, s], QT[:, h, s]) for h in range(4)], tg)
                tst = V(lambda e: e.tensor_tensor(ST.rearrange("p h t -> p (h t)"), PB[3][:, :],
                                                  EE.rearrange("p h t -> p (h t)"), ALU.mult), tq, S.now())
                t0 = V.now()
                tk, ts = {}, {}
                for p in range(2):
                    tk1 = P([mm(PB[4 + p][:, h * 129:(h + 1) * 129], ST[:, 2 * p + h, :], VA[:, b, 2 * p + h, :])
                             for h in range(2)], t0)
                    tk[p] = P([mm(PB[6 + p][:, h * 129:(h + 1) * 129], QT[:, 2 * p + h, s], CS[d][:, 2 * p + h, :])
                               for h in range(2)], t0)
                    ts[p] = S((lambda p: lambda e: e.activation(
                        PS1[:, 2 * p:2 * p + 2, :].rearrange("p h t -> p (h t)"), PB[4 + p][:, 0:258],
                        ACT.Copy))(p), tk1, t0, free=True)
                for hh in range(4):
                    p, h = hh // 2, hh % 2
                    V((lambda p, h, hh: lambda e: e.scalar_tensor_tensor(
                        RR[:, hh, :], PB[6 + p][:, h * 129:(h + 1) * 129], NAT[:, b, 2, 4 * d + hh:4 * d + hh + 1],
                        PS1[:, hh, :], ALU.mult, ALU.add))(p, h, hh), tk[p], ts[p], t0, free=True)
                V(lambda e: e.scalar_tensor_tensor(DN[:, 0:4], RR[:, :, 128], -1.0, RR[:, :, 128],
                                                   ALU.mult, ALU.max))
                V(lambda e: e.tensor_tensor(DN[:, 0:4], DN[:, 0:4], NAT[:, b, 3, 4 * d:4 * d + 4], ALU.max))
                tr = V(lambda e: e.reciprocal(DN[:, 4:8], DN[:, 0:4]))
                for hh in range(4):
                    dst = HM[:, b, hh, :]
                    if d == 0:
                        V((lambda dst, hh: lambda e: e.tensor_scalar(dst, RR[:, hh, 0:128], DN[:, 4 + hh:5 + hh], None,
                                                                    ALU.mult))(dst, hh), tr, free=True)
                    else:
                        V((lambda dst, hh: lambda e: e.scalar_tensor_tensor(
                            dst, RR[:, hh, 0:128], DN[:, 4 + hh:5 + hh], dst, ALU.mult, ALU.add))(dst, hh), tr,
                          free=True)

            for d in range(2):
                state(d, 0)
                state(d, 1)
                outputs(d, 2)
                state(d, 2)
                outputs(d, 3)
            dump("HM", HM.rearrange("p b h t -> p b (h t)"), V.now())
            t = barrier()
            ht2 = Region(HTF, 0, 6128)
            keep = Region(BIG, at_a, at_a + 3072 + 7184)
            QB = keep(2, 2, 256)
            QQ, KK, KST = keep(2, 256), keep(2, 256), keep(4, 256)
            SS = [keep(2, 256), keep(2, 256)]
            AT = [keep(4, 128), keep(4, 128)]
            HMc = keep(2, 512)
            HG, TE, TF = ht2(2, 512), ht2(2, 512), ht2(2, 256)
            KS, EBE = ht2(2, 512), ht2(2, 2, 8)
            V(lambda e: e.tensor_copy(HMc, HM.rearrange("p b h t -> p b (h t)")))
            V.wait(*barrier())
            V(lambda e: e.memset(SS[0], 0.0))
            V(lambda e: e.memset(SS[1], 0.0))
            V(lambda e: e.memset(QB, 0.0))
            ZR = AT[0][0:1, :, :].rearrange("p h t -> p (h t)")
            V(lambda e: e.memset(ZR, 0.0))
            P([mm(PB[6 + b][:, :], ONES[0:1, :], ZR, True, False) for b in range(2)], V.now())
            pair = [0]
            for d in range(2):
                end, mid = (63, 32) if d == 0 else (0, 31)
                for f in range(2):
                    bv = BB[:, d, f, :].rearrange("p (c t) -> p c t", t=64)
                    be = bv[:, :, end:end + 1]
                    te = TE[:, f, :].rearrange("p (c t) -> p c t", t=64)
                    tf = TF[:, f, :].rearrange("p (c t) -> p c t", t=64)
                    V((lambda te, be, bv: lambda e: e.tensor_tensor(te, be.broadcast_to([128, 8, 64]), bv,
                                                                   ALU.subtract))(te, be, bv), PE.now())
                    V((lambda tf, bv, mid: lambda e: e.tensor_tensor(
                        tf, bv[:, 0:4, :], bv[:, 0:4, mid:mid + 1].broadcast_to([128, 4, 64]),
                        ALU.subtract))(tf, bv, mid))
                    S((lambda d, f, be: lambda e: e.activation(EBE[:, d, f, :].unsqueeze(2), be, ACT.Exp))(d, f, be),
                      V.now())
                S(lambda e: e.activation(TE, TE, ACT.Exp), V.now())
                S(lambda e: e.activation(QQ, TF, ACT.Exp), PE.now())
                S(lambda e: e.activation(KK, TF, ACT.Exp, scale=-1.0))
                S((lambda d: lambda e: e.activation(TF, BB[:, d, :, 0:256], ACT.Exp))(d))
                V(lambda e: e.tensor_tensor(KS, TE, GK, ALU.mult), S.now(), PE.now())
                V(lambda e: e.tensor_tensor(QQ, QQ, GQ, ALU.mult))
                V(lambda e: e.tensor_tensor(KK, KK, GK[:, :, 0:256], ALU.mult))
                for f in range(2):
                    tv = TF[:, f, :].rearrange("p (c h t) -> p c h t", c=2, h=2)
                    gv = GQ[:, f, :].rearrange("p (c h t) -> p c h t", c=2, h=2)
                    for x in range(2):
                        qv = QB[:, x, f, :].rearrange("p (c h t) -> p c h t", c=2, h=2)
                        V((lambda qv, tv, gv, x: lambda e: e.tensor_tensor(qv[:, :, x, :], tv[:, :, x, :],
                                                                         gv[:, :, x, :], ALU.mult))(qv, tv, gv, x))
                barrier()
                transposes([(KST[:, b, f * 128:(f + 1) * 128], KS[:, f, b * 128:(b + 1) * 128])
                            for b in range(4) for f in range(2)], [0, 1], (V.now(),))
                barrier()
                t0 = V.now()
                gm = GM[:, d, :].unsqueeze(1).broadcast_to([128, 2, 128])
                tk, ta = {}, {}
                for b in range(2):
                    s = slice(b * 128, (b + 1) * 128)
                    for x in range(2):
                        r = slice(64 * x, 64 * x + 64)
                        bank = PB[(2, 5, 0, 1)[2 * b + x]]
                        tk[b, x] = P([mm(bank[:, f * 128:(f + 1) * 128], KK[r, f, s], QQ[r, f, s])
                                      for f in range(2)], t0)
                for b in range(2):
                    for step in range(2):
                        for x in range(2):
                            av = AT[b].rearrange("p (f x) t -> p f x t", x=2)[:, :, x, :]
                            pv2 = PB[(2, 5, 0, 1)[2 * b + x]][:, 0:256].rearrange("p (h t) -> p h t", h=2)
                            if step == 0:
                                ta[x] = V((lambda av, pv2, gm: lambda e: e.tensor_tensor(av, pv2, gm, ALU.min))(
                                    av, pv2, gm), tk[b, x], free=True)
                            else:
                                V((lambda av, gm: lambda e: e.scalar_tensor_tensor(
                                    av, gm, -1.0, av, ALU.mult, ALU.max))(av, gm), ta[x], free=True)
                    P([mm(PB[6 + b][:, h * 128:(h + 1) * 128], AT[b][:, h, :], GV[:, b, h * 128:(h + 1) * 128],
                          False, False) for h in range(4)], V.now())
                chunks = [4, 5, 6, 7, 0, 1, 2, 3] if d == 0 else [7, 6, 5, 4, 3, 2, 1, 0]
                if d == 1:
                    V(lambda e: e.memset(SS[0], 0.0), PE.now())
                tadd, tss, tread = {}, {-1: V.now()}, {}

                def add(n_):
                    b, x = chunks[n_] // 2, chunks[n_] % 2
                    tadd[n_] = P([mm(PB[3 + n_ % 2][:, f * 256:(f + 1) * 256],
                                     KST[64 * x:64 * x + 64, b, f * 128:(f + 1) * 128],
                                     GV[64 * x:64 * x + 64, b, f * 256:(f + 1) * 256]) for f in range(2)],
                                 t0, *([tss[n_ - 2]] if n_ > 1 else []))

                add(0)
                add(1)
                for n_, ch in enumerate(chunks):
                    b, x = ch // 2, ch % 2
                    cur, nxt = SS[n_ % 2], SS[(n_ + 1) % 2]
                    bank = PB[3 + n_ % 2]
                    if n_ < 7:
                        for f in range(2):
                            for h in range(2):
                                r = slice(64 * h, 64 * h + 64)
                                q = slice(128 * h, 128 * h + 128)
                                tss[n_] = V((lambda cur, nxt, f, r, q, bank, h, ch, d: lambda e:
                                             e.scalar_tensor_tensor(
                                                 nxt[r, f, q], cur[r, f, q], EBE[r, d, f, ch:ch + 1],
                                                 bank[r, f * 256 + 128 * h:f * 256 + 128 * h + 128], ALU.mult,
                                                 ALU.add))(cur, nxt, f, r, q, bank, h, ch, d),
                                            tadd[n_], tss[n_ - 1], *([tread[n_ - 1]] if n_ - 1 in tread else []),
                                            free=True)
                    if n_ >= 4:
                        tread[n_] = P([mm(PB[6 + b][:, f * 256:(f + 1) * 256], QB[:, x, f, b * 128:(b + 1) * 128],
                                          cur[:, f, :], False, (d == 1 and x == 0 and f == 1)) for f in range(2)],
                                      tss[n_ - 1])
                    if n_ + 2 < 7:
                        add(n_ + 2)
                barrier()
            for b in range(2):
                S((lambda b: lambda e: e.activation(HG[:, b, :], PB[6 + b][:, :], ACT.Copy))(b))
            dump("HG", HG, S.now())
            barrier()
            OO = keep.base[:, at_a:at_a + 2048].rearrange("p (b n) -> p b n", b=2)
            R8 = SM[:, 224:240]
            TT = [BIG[:, a_:a_ + 1024].rearrange("p (b n) -> p b n", b=2) for a_ in (at_a + 2048, at_a + 3072)]
            HMf = HMc
            tsq = [S((lambda src, tt: lambda e: e.activation(tt, src, ACT.Square))(src, tt), V.now())
                   for src, tt in zip((HMf, HG), TT)]
            for s_, (src, gate, o0) in enumerate(((HMf, MO, 0), (HG, GR, 512))):
                V((lambda src, gate, o0: lambda e: e.tensor_tensor(OO[:, :, o0:o0 + 512], src, gate,
                                                                  ALU.mult))(src, gate, o0), free=True)
                V((lambda s_: lambda e: e.tensor_reduce(R8[:, s_ * 8:s_ * 8 + 8],
                                                       TT[s_].rearrange("p b (h t) -> p (b h) t", h=4), AX.X,
                                                       ALU.add))(s_), tsq[s_])
            V(lambda e: e.tensor_scalar(R8, R8, 1.0 / 128, EPS, ALU.mult, ALU.add))
            V(lambda e: e.reciprocal(R8, R8))
            ts = S(lambda e: e.activation(R8, R8, ACT.Sqrt), V.now())
            for s_ in range(2):
                for b in range(2):
                    ov = OO[:, b, s_ * 512:(s_ + 1) * 512].rearrange("p (h t) -> p h t", h=4)
                    rv = R8[:, s_ * 8 + b * 4:s_ * 8 + b * 4 + 4].unsqueeze(2).broadcast_to([128, 4, 128])
                    V((lambda ov, rv: lambda e: e.tensor_tensor(ov, ov, rv, ALU.mult))(ov, rv), ts, free=True)
            barrier()
            project_out(OO, G1,
                        lambda kc: col("ml_norm_g_2", kc) if kc < 4 else col("gla_norm_g_2", kc - 4))
            dump("Y", X[:, :, :], V.now())
            barrier()
            if stop == "mix":
                return
            peer(GA, G2, at_a)

        def peer(GA, G2, at_a):
            reg = Region(BIG, at_a, BIGN)
            hn = reg(2, 1024)
            H2 = reg(2, 1024)
            QP = reg(2, 2, 256)
            KEYT = reg(16, 128)
            SC = reg(8, 2, 2, 128)
            KEYS = Region(BIG, reg.at, BIGN)(16, 128)
            free_now = V.now(), S.now(), PE.now(), G.now()
            tkeys = load_once("keys", KEYS, A["peer_keys_2"][0].rearrange("h s k q -> k (h s) q"), *free_now)
            t = normed(hn, X, V.now())
            ready = transposed(hn, lambda kc: GA[:, 4, kc:kc + 1], shift=lambda kc: GA[:, 5, kc:kc + 1],
                               after=t)
            V.wait(tkeys)
            S.wait(tkeys)
            PE.wait(tkeys)
            tt = transposes([(KEYT[:, k, :], KEYS[:, k, :]) for k in range(16)], [0, 1, 2, 3], (V.now(),))
            for b in range(2):
                q = slice(b * 128, (b + 1) * 128)
                V((lambda b, q: lambda e: e.tensor_tensor(
                    hn[:, b, :].rearrange("p (k t) -> p k t", t=128), HTH[:, :, q].bitcast(F32),
                    HTL[:, :, q].bitcast(F32), ALU.add))(b, q), PE.now())
            th = V.now()
            reg = Region(BIG, reg.at, BIGN)
            WK, CD, OH = ([reg(16, 16) for _ in range(2)] for _ in range(3))
            IO16 = reg(16)
            tio = load_once("io", IO16, A["c_cst2"][:, 2048:2064], *tt, PE.now())
            TS, TIF, TI = ([reg(2, 16) for _ in range(2)] for _ in range(3))
            BS = reg(2, 8, 16)
            ID1, ID2, BI, I1, I1F = ([reg(16) for _ in range(2)] for _ in range(5))
            IDX = reg(2, 128).bitcast(U32)
            GW, AV = reg(2, 8, 16), reg(2, 128)
            V.wait(tio, *tt)

            def top16(vals, idx, src, work, *after):
                idx = idx.bitcast(U32)
                return [(lambda e: e.max(vals[:, 0:8], src), after),
                        (lambda e: e.max_index(idx[:, 0:8], vals[:, 0:8], src), ()),
                        (lambda e: e.match_replace(work, vals[:, 0:8], src, LOW), ()),
                        (lambda e: e.max(vals[:, 8:16], work), ()),
                        (lambda e: e.max_index(idx[:, 8:16], vals[:, 8:16], work), ())]

            tsc, tidx, tgw = {}, {}, {}

            def selection(b, h):
                i = h % 2
                wk = WK[i].rearrange("p a b -> p (a b)")
                steps = []
                for x in range(2):
                    steps += top16(TS[i][:, x, :], TI[i][:, x, :], SC[:, h, b, x, :], wk[:, 0:128], tsc[h])
                steps.append((lambda e: e.tensor_copy(TIF[i], TI[i].bitcast(U32)), ()))
                steps.append((lambda e: e.tensor_tensor(CD[i], TS[i][:, 0, :].unsqueeze(2).broadcast_to([128, 16, 16]),
                                                        TS[i][:, 1, :].unsqueeze(1).broadcast_to([128, 16, 16]),
                                                        ALU.add), ()))
                steps += top16(BS[:, b, h, :], BI[i], CD[i].rearrange("p a b -> p (a b)"), wk)
                for x, dst in enumerate((ID1[i], ID2[i])):
                    op, val = ((ALU.logical_shift_right, 4), (ALU.bitwise_and, 15))[x]
                    steps += [
                        ((lambda op, val: lambda e: e.tensor_scalar(I1[i].bitcast(U32), BI[i].bitcast(U32), val, None,
                                                                    op))(op, val), ()),
                        (lambda e: e.tensor_copy(I1F[i], I1[i].bitcast(U32)), ()),
                        (lambda e: e.tensor_tensor(OH[i], I1F[i].unsqueeze(2).broadcast_to([128, 16, 16]),
                                                   IO16.unsqueeze(1).broadcast_to([128, 16, 16]), ALU.is_equal), ()),
                        ((lambda x: lambda e: e.tensor_tensor(
                            OH[i], OH[i], TIF[i][:, x, :].unsqueeze(1).broadcast_to([128, 16, 16]),
                            ALU.mult))(x), ()),
                        ((lambda dst: lambda e: e.tensor_reduce(dst, OH[i], AX.X, ALU.add))(dst), ())]
                steps.append((lambda e: e.scalar_tensor_tensor(IDX[:, b, h * 16:(h + 1) * 16], ID1[i], 128.0, ID2[i],
                                                               ALU.mult, ALU.add), ()))
                return steps

            pair = {}

            def steps_of(b, h, first, count):
                if first == 0:
                    for i in range(2):
                        pair[i] = selection(b, h + i), V.now()
                for n in range(first, first + count):
                    for i in range(2):
                        steps, t = pair[i]
                        if n < len(steps):
                            fn, after = steps[n]
                            t = V(fn, t, *after, free=True)
                            pair[i] = steps, t
                            if n == len(steps) - 1:
                                tidx[b, h + i] = t

            def gate_weights(b):
                V(lambda e: e.tensor_tensor(GW[:, b, :, :], BS[:, b, :, :],
                                            BS[:, b, :, 0:1].broadcast_to([128, 8, 16]), ALU.subtract))
                ts = S(lambda e: e.activation(GW[:, b, :, :], GW[:, b, :, :], ACT.Exp), V.now())
                V(lambda e: e.tensor_reduce(SM[:, 0:8], GW[:, b, :, :], AX.X, ALU.add), ts)
                V(lambda e: e.reciprocal(SM[:, 8:16], SM[:, 0:8]))
                V(lambda e: e.tensor_tensor(GW[:, b, :, :], GW[:, b, :, :],
                                            SM[:, 8:16].unsqueeze(2).broadcast_to([128, 8, 16]), ALU.mult))
                tgw[b] = V.now()

            pieces = []
            for b in range(2):
                for h in range(0, 8, 2):
                    for n in range(0, 28, 4):
                        pieces.append(lambda b=b, h=h, n=n: steps_of(b, h, n, 4))
                pieces.append(lambda b=b: gate_weights(b))

            def piece():
                if pieces:
                    pieces.pop(0)()

            tq, ts_ = {}, {}

            def scores(j):
                tk = P([mm(PB[4 + j % 2][:, b * 256 + x * 128:b * 256 + (x + 1) * 128],
                           QP[:, j % 2, x, b * 128:(b + 1) * 128], KEYT[:, 2 * j + x, :])
                        for b in range(2) for x in range(2)], tq[j], *([tsc[j - 2]] if j > 1 else []))
                ts_[j] = tk
                tsc[j] = S(lambda e: e.activation(SC[:, j, :, :, :], shaped(PB[4 + j % 2][:, :], (2, 2, 128)),
                                                  ACT.Copy), tk, free=True)

            for j in range(8):
                w = need()
                for c in range(2):
                    q = slice(c * 128, (c + 1) * 128)
                    tk = P(mm3(PB[j % 2][:, c * 256:(c + 1) * 256], [(w.h[:, k, q], w.l[:, k, q]) for k in range(8)],
                               [(HTH[:, k, 0:256], HTL[:, k, 0:256]) for k in range(8)]),
                           ready, *tt, w.ready, *([tq[j - 2]] if j > 1 else []))
                w.free(tk)
                tq[j] = S((lambda j: lambda e: e.activation(QP[:, j % 2, :, :], shaped(PB[j % 2][:, :], (2, 256)),
                                                           ACT.Copy))(j), tk, *([ts_[j - 2]] if j > 1 else []),
                          free=True)
                if j:
                    scores(j - 1)
                if j > 1:
                    piece()
            tw = PE.now()
            scores(7)
            for b in range(2):
                th2 = transposes([(H2[:, b, k * 128:(k + 1) * 128], hn[:, b, k * 128:(k + 1) * 128])
                                  for k in range(8)], [2 + 4 * b, 3 + 4 * b], (th,))
            NG = 20
            ROWS_ = [RAW[:, i * 1024:(i + 1) * 1024] for i in range(10)] + \
                [HIF[:, i * 1024:(i + 1) * 1024] for i in range(10)]
            gs = [sem(f"s_row{i}") for i in range(NG)]
            gn = [0] * NG
            used = [None] * NG
            ACC = HTF[:, 0:2048].rearrange("p (b n) -> p b n", b=2)
            FG = HTF[:, 2048:3072]
            JK = HTF[:, 3072:4096]
            JKS = [JK, HTF[:, 5120:6144]]
            tdot = {}
            DG = HTF[:, 4096:4608].rearrange("p (a n) -> p a n", a=4)
            tdg = {}
            diags = [0]
            V(lambda e: e.memset(ACC, 0.0), tw)
            V.wait(*th2)
            tf = load_once("nf", FG, A["norm_f_g_2"].partition_broadcast(128), tw, V.now())
            tables = A["peer_u_2"][0], A["peer_v_2"][0]
            order = [(b, s_, j) for b in range(2) for s_ in range(2) for j in range(128)]
            sent = [0]
            where = {}

            def gather():
                g = sent[0]
                b, s_, j = order[g]
                sent[0] += 1
                i = g % NG
                while (b, j // 16) not in tidx:
                    piece()
                G.dma(lambda e: e.indirect_dma_start(
                    out=ROWS_[i], out_offset=None, in_=tables[s_],
                    in_offset=bass.IndirectOffsetOnAxis(ap=IDX[:, b, j:j + 1], axis=0)),
                    gs[i], tidx[b, j // 16], *([used[i]] if used[i] else [tw]))
                gn[i] += 16
                where[g] = i, (gs[i], gn[i])

            def finished(b):
                for h in range(2):
                    av = ACC[:, b, h * 512:(h + 1) * 512]
                    V((lambda h, av: lambda e: e.tensor_tensor(av, av, PB[4 * b + h][:, :], ALU.add))(h, av), PE.now())
                V(lambda e: e.tensor_tensor(ACC[:, b, :], ACC[:, b, :], G2, ALU.mult))
                V(lambda e: e.tensor_tensor(X[:, b, :], X[:, b, :], ACC[:, b, :], ALU.add))
                d = SM[:, 16 + b:17 + b]
                ts = S(lambda e: e.activation(hn[:, b, :], X[:, b, :], ACT.Square, accum_out=d), V.now())
                V(lambda e: e.tensor_scalar(d, d, 1.0 / 1024, EPS, ALU.mult, ALU.add), ts)
                V(lambda e: e.reciprocal(d, d))
                ts = S(lambda e: e.activation(d, d, ACT.Sqrt), V.now())
                t = V(lambda e: e.scalar_tensor_tensor(X[:, b, :], X[:, b, :], d, FG, ALU.mult, ALU.mult), ts, tf)
                SP.dma(lambda e: e.dma_start(out[0, b * 128:(b + 1) * 128, :], X[:, b, :]), outsem, t)
                dumped[0] += 16

            while pieces and (0, 0) not in tidx:
                piece()
            for g, (b, s_, j) in enumerate(order):
                while sent[0] < len(order) and sent[0] < g + NG and \
                        (order[sent[0]][0], order[sent[0]][2] // 16) in tidx:
                    gather()
                if g not in where:
                    gather()
                i, arr = where[g]
                if s_ == 0:
                    used[i] = tdot[b, j] = V((lambda i, b, j: lambda e: e.tensor_tensor_reduce(
                        out=JKS[j % 2], in0=ROWS_[i], in1=H2[:, b, :], scale=1.0, scalar=0.0, op0=ALU.mult,
                        op1=ALU.add, accum_out=AV[:, b, j:j + 1]))(i, b, j), arr,
                        tdot[b, j - 2] if j > 1 else V.now(), free=True)
                    if j == 127:
                        while b not in tgw:
                            piece()
                        ts = S((lambda b: lambda e: e.activation(AV[:, b, :], AV[:, b, :], ACT.Gelu))(b), V.now())
                        V((lambda b: lambda e: e.tensor_tensor(AV[:, b, :], AV[:, b, :],
                                                              GW[:, b, :, :].rearrange("p h k -> p (h k)"),
                                                              ALU.mult))(b), ts)
                elif j % 2:
                    d = diags[0]
                    diags[0] += 1
                    td = S((lambda d, b, j: lambda e: e.activation(DG[:, d % 4, :], IDENT, ACT.Copy,
                                                                  scale=AV[:, b, j:j + 1]))(d, b, j),
                           tdg_first, *([tdg[d - 4]] if d > 3 else []), free=True)
                    used[i] = tdg[d] = P([mm(PB[4 * b + h][:, :], DG[:, d % 4, :], ROWS_[i][:, h * 512:(h + 1) * 512],
                                             j == 1, j == 127) for h in range(2)], td, arr, *th2)
                    if j == 127:
                        finished(b)
                else:
                    if j == 0:
                        tdg_first = V.now()
                    used[i] = V((lambda i, b, j: lambda e: e.scalar_tensor_tensor(
                        ACC[:, b, :], ROWS_[i], AV[:, b, j:j + 1], ACC[:, b, :], ALU.mult, ALU.add))(i, b, j), arr)
                first = (0, 7) not in tidx
                if g % (2 if first else 5) == 1:
                    piece()

        def finish():
            if stop:
                t = barrier()
                SP.dma(lambda e: e.dma_start(out.rearrange("o (b p) n -> p (o b) n", p=128), X[:, :, :]), outsem, *t)
                dumped[0] += 16
            SP.wait((outsem, dumped[0]))

        def plan_second():
            wv = A["w_in_2"][0].rearrange("(k p) n -> p k n", p=128)
            cuts = [256 * i for i in range(9)] + [2320, 2576, 2832, 3088, 3368, 3632]
            for i in (0, 1, 2, 3, 13, 8, 9, 4, 5, 6, 7, 10, 11, 12):
                plan(wv[:, :, cuts[i]:cuts[i + 1]], 8, cuts[i + 1] - cuts[i], slots=NS - 1)
            plan_out(A["w_out_2"][0], NS - 1)
            wq = A["peer_wq_2"][0].rearrange("(k p) n -> p k n", p=128)
            for j in range(8):
                plan(wq[:, :, j * 256:(j + 1) * 256], 8, 256, slots=NS - 1)

        def program():
            for l in range(2):
                plan_ffn(l, 1)
                plan_hybrid(l)
                plan_ffn(l, 2)
            plan_second()
            loads()
            for l in range(2):
                ffn(l, 1)
                dump(f"F{l}", X[:, :, :], V.now())
                if stop == f"ffn{l}":
                    return
                hybrid(l)
                if stop == f"hyb{l}":
                    return
                ffn(l, 2)
            if stop == "first":
                return
            second()

        program()
        finish()

        block = ctx.enter_context(nc.Block())

        @block.sync
        def _(e):
            SP.emit(e)

        @block.tensor
        def _(e):
            PE.emit(e)

        @block.vector
        def _(e):
            V.emit(e)

        @block.scalar
        def _(e):
            S.emit(e)

        @block.gpsimd
        def _(e):
            G.emit(e)


_INS = ["x", "ffn1_norm", "ffn1_w_gate", "ffn1_w_up", "ffn1_w_down", "mix_norm", "w_in", "c_q_norm",
        "c_kv_norm", "c_w_uq", "c_w_ukv", "w_out", "ffn2_norm", "ffn2_w_gate", "ffn2_w_up", "ffn2_w_down",
        "final_norm", "c_2", "ctx_2", "c_ctx_2", "w_mod_2", "b_mod_2", "norm1_g_2", "w_in_2", "ml_conv_w_2",
        "ml_gate_b_2", "ml_norm_g_2", "gla_lr_w2_2", "gla_alpha_b_2", "gla_norm_g_2", "w_out_2", "norm2_g_2",
        "peer_wq_2", "peer_keys_2", "peer_u_2", "peer_v_2", "norm_f_g_2"]


def constants():
    c = np.zeros((128, 768), np.float32)
    c[:, 0:128] = np.eye(128)
    c[:, 128:256] = np.eye(128)[::-1]
    c[:, 256:384] = 8 * np.eye(128)[::-1]
    pos = np.arange(256, dtype=np.float32)
    t = np.zeros((256, 192), np.float32)
    for d, off in ((64, 0), (32, 128)):
        inv = (np.float32(10000.0) ** (-np.arange(0, d, 2, dtype=np.float32) / np.float32(d))).astype(np.float32)
        ang = (pos[:, None] * inv[None, :]).astype(np.float32).astype(np.float64)
        co, si = np.cos(ang), np.sin(ang)
        t[:, off:off + 2 * d] = np.concatenate([co, co, -si, si], axis=1)
    c[:, 384:768] = t.reshape(2, 128, 192).transpose(1, 0, 2).reshape(128, 384)
    return c


def constants2():
    c = np.zeros((128, 2064), np.float32)
    s, t = np.arange(128)[:, None], np.arange(128)[None, :]
    c[:, 0:128] = np.where(s <= t, 0, NEG)
    c[:, 128:256] = np.where(s >= t, 0, NEG)
    same = s // 64 == t // 64
    c[:, 256:384] = np.where(same & (s <= t), 3e38, 0)
    c[:, 384:512] = np.where(same & (s >= t), 3e38, 0)
    n = np.arange(512)
    c[:, 512:1024] = np.where(n % 128 == 0, 0, 1)
    c[:, 1024:1536] = np.where(n % 128 == 0, -3e37, 0)
    c[:, 1536:2048] = np.where(n % 64 == 0, 0, 1)
    c[:, 2048:2064] = np.arange(16)
    return c


def tensors(nc, inputs):
    arrays, A = {}, {}
    for name in _INS:
        arrays["in_" + name] = np.ascontiguousarray(inputs[name])
    order = np.clip(255 - np.arange(383), -63, 128) + 63
    arrays["in_c_rel"] = np.ascontiguousarray(np.asarray(inputs["a_rel_bias"])[:, :, order])
    arrays["in_c_cst"] = constants()
    arrays["in_c_cst2"] = constants2()
    for name, a in arrays.items():
        A[name[3:]] = nc.dram_tensor(name, a.shape, mybir.dt.from_np(a.dtype), kind="ExternalInput").ap()
    rel = A["c_rel"]
    A["c_relw"] = [bass.AP(tensor=rel.tensor, offset=l * 6 * 383, ap=[[1, 128], [383, 6], [1, 256]])
                   for l in range(2)]
    return arrays, A


def kernel(**inputs):
    import concourse.bacc as _bacc
    from concourse.bass_utils import run_bass_kernel_spmd as _run

    nc = _bacc.Bacc("TRN2", target_bir_lowering=False, num_devices=1)
    arrays, A = tensors(nc, inputs)
    o = nc.dram_tensor("out_0", (1, 256, 1024), F32, kind="ExternalOutput").ap()
    build(nc, A, o, {})
    r = _run(nc, [arrays], core_ids=[0])
    return r.results[0]["out_0"]
```
